# Optimizing a Trainium2 kernel written in Bass

```python
import jax, jax.numpy as jnp
from jax import lax
import numpy as np
import math

D_MODEL = 1024
BATCH = 1
SEQ = 512
DEPTH = 2

HEAD_DIM = 64
D_FF = 2816
D_PLE = 256
ATTN_Q_HEADS = 8
ATTN_KV_HEADS = 2
ATTN_GROUP = ATTN_Q_HEADS // ATTN_KV_HEADS
WINDOW = 128
ROPE_THETA = 500000.0
ROPE_DIM = HEAD_DIM // 4
MLSTM_HEADS = 4
MLSTM_CHUNK = 64
MLSTM_CONV = 4
GATE_CAP = 15.0
RWKV_HEADS = 4
RWKV_W_RANK = 64
RWKV_A_RANK = 64
RWKV_G_RANK = 128
RWKV_GN_EPS = 64e-5
NORM_EPS = 1e-6
NEG_INF = -1e30

ATTN_W = ATTN_Q_HEADS * HEAD_DIM
KV_W = ATTN_KV_HEADS * HEAD_DIM
MLSTM_W = MLSTM_HEADS * HEAD_DIM
RWKV_W = RWKV_HEADS * HEAD_DIM
D_MIX = ATTN_W + MLSTM_W + RWKV_W
ATTN_COLS = ATTN_W + 2 * KV_W
MLSTM_COLS = 4 * MLSTM_W + 2 * MLSTM_HEADS
RWKV_COLS = 3 * RWKV_W + RWKV_W_RANK + RWKV_A_RANK + RWKV_G_RANK
D_IN = ATTN_COLS + MLSTM_COLS + RWKV_COLS


def rms_norm(x, gain):
    xf = x.astype(jnp.float32)
    y = xf * lax.rsqrt(jnp.mean(xf * xf, axis=-1, keepdims=True) + NORM_EPS)
    return (y * gain.astype(jnp.float32)).astype(x.dtype)

def swiglu(x, w_in, w_out):
    gate, up = jnp.split(x @ w_in, 2, axis=-1)
    return (jax.nn.silu(gate) * up) @ w_out

def rope_tables(positions):
    inv_freq = ROPE_THETA ** (-jnp.arange(0, ROPE_DIM, 2, dtype=jnp.float32) / ROPE_DIM)
    ang = positions.astype(jnp.float32)[..., None] * inv_freq
    return jnp.cos(ang)[:, :, None, :], jnp.sin(ang)[:, :, None, :]

def partial_rope(x, cos, sin):
    half = ROPE_DIM // 2
    x1 = x[..., :half].astype(jnp.float32)
    x2 = x[..., half:ROPE_DIM].astype(jnp.float32)
    rot = jnp.concatenate([x1 * cos - x2 * sin, x2 * cos + x1 * sin], axis=-1).astype(x.dtype)
    return jnp.concatenate([rot, x[..., ROPE_DIM:]], axis=-1)

def sliding_window_gqa(q, k, v, sinks):
    B, S = q.shape[:2]
    nb = S // WINDOW
    qb = q.reshape(B, nb, WINDOW, ATTN_KV_HEADS, ATTN_GROUP, HEAD_DIM)

    def band_keys(t):
        tb = t.reshape(B, nb, WINDOW, ATTN_KV_HEADS, HEAD_DIM)
        prev = jnp.pad(tb[:, :-1], ((0, 0), (1, 0), (0, 0), (0, 0), (0, 0)))
        return jnp.concatenate([prev, tb], axis=2)

    kb, vb = band_keys(k), band_keys(v)
    scores = jnp.einsum('bnqhgd,bnkhd->bnhgqk', qb, kb).astype(jnp.float32) * (HEAD_DIM ** -0.5)
    qi = jnp.arange(WINDOW)[:, None]
    kj = jnp.arange(2 * WINDOW)[None, :]
    lag = qi + WINDOW - kj
    in_band = (lag >= 0) & (lag < WINDOW)
    blk = jnp.arange(nb)[:, None, None]
    valid = in_band[None] & ((blk > 0) | (kj >= WINDOW)[None])
    scores = jnp.where(valid[None, :, None, None], scores, NEG_INF)
    sink = jnp.broadcast_to(
        sinks.astype(jnp.float32).reshape(1, 1, ATTN_KV_HEADS, ATTN_GROUP, 1, 1),
        scores.shape[:-1] + (1,))
    probs = jax.nn.softmax(jnp.concatenate([scores, sink], axis=-1), axis=-1)[..., :-1]
    out = jnp.einsum('bnhgqk,bnkhd->bnqhgd', probs.astype(v.dtype), vb)
    return out.reshape(B, S, ATTN_W)

def causal_depthwise_conv(x, w):
    return lax.conv_general_dilated(
        x, w[:, None, :].astype(x.dtype), window_strides=(1,),
        padding=((w.shape[0] - 1, 0),), dimension_numbers=('NWC', 'WIO', 'NWC'),
        feature_group_count=x.shape[-1])

def mlstm_chunkwise(q, k, v, i_pre, f_pre):
    B, S, H, D = q.shape
    L = MLSTM_CHUNK
    nc = S // L

    def chunks(t):
        return jnp.moveaxis(t.reshape((B, nc, L, H) + t.shape[3:]), 3, 1)

    q = chunks(q * (D ** -0.5))
    k = chunks(k)
    v = chunks(v)
    ig = chunks(i_pre)
    g = jnp.cumsum(chunks(jax.nn.log_sigmoid(f_pre)), axis=-1)
    g_tot = g[..., -1]

    a = g_tot[..., None] - g + ig
    m_loc = jnp.max(a, axis=-1)
    w_loc = jnp.exp(a - m_loc[..., None])
    c_loc = jnp.einsum('bhcl,bhclv,bhclk->bhcvk', w_loc, v, k)
    n_loc = jnp.einsum('bhcl,bhclk->bhck', w_loc, k)

    def carry_state(state, xs):
        c, n, m = state
        gt, ml, cl, nl = xs
        m_new = jnp.maximum(gt + m, ml)
        s_old = jnp.exp(gt + m - m_new)
        s_loc = jnp.exp(ml - m_new)
        c_new = s_old[..., None, None] * c + s_loc[..., None, None] * cl
        n_new = s_old[..., None] * n + s_loc[..., None] * nl
        return (c_new, n_new, m_new), (c, n, m)

    init = (jnp.zeros((B, H, D, D), jnp.float32), jnp.zeros((B, H, D), jnp.float32),
            jnp.full((B, H), NEG_INF, jnp.float32))
    xs = tuple(jnp.moveaxis(t, 2, 0) for t in (g_tot, m_loc, c_loc, n_loc))
    _, (c_prev, n_prev, m_prev) = lax.scan(carry_state, init, xs)
    c_prev = jnp.moveaxis(c_prev, 0, 2)
    n_prev = jnp.moveaxis(n_prev, 0, 2)
    m_prev = jnp.moveaxis(m_prev, 0, 2)

    causal = jnp.tril(jnp.ones((L, L), dtype=bool))
    d_intra = jnp.where(causal, g[..., :, None] - g[..., None, :] + ig[..., None, :], NEG_INF)
    inter = g + m_prev[..., None]
    m_row = jnp.maximum(inter, jnp.max(d_intra, axis=-1))
    w_intra = jnp.exp(d_intra - m_row[..., None])
    w_inter = jnp.exp(inter - m_row)
    s = jnp.einsum('bhcld,bhcsd->bhcls', q, k) * w_intra
    num = (jnp.einsum('bhcls,bhcsv->bhclv', s, v)
           + w_inter[..., None] * jnp.einsum('bhcvk,bhclk->bhclv', c_prev, q))
    den = jnp.sum(s, axis=-1) + w_inter * jnp.einsum('bhck,bhclk->bhcl', n_prev, q)
    h = num / jnp.maximum(jnp.abs(den), jnp.exp(-m_row))[..., None]
    return jnp.moveaxis(h, 1, 3).reshape(B, S, H, D)

def rwkv7_scan(r, decay, k, v, a_vec, b_vec):
    B, S, H, D = r.shape

    def step(state, xs):
        r_t, w_t, k_t, v_t, a_t, b_t = xs
        sa = jnp.einsum('bhvk,bhk->bhv', state, a_t)
        state = (state * w_t[:, :, None, :] + sa[..., None] * b_t[:, :, None, :]
                 + v_t[..., None] * k_t[:, :, None, :])
        return state, jnp.einsum('bhvk,bhk->bhv', state, r_t)

    xs = tuple(jnp.moveaxis(t, 1, 0) for t in (r, decay, k, v, a_vec, b_vec))
    _, y = lax.scan(step, jnp.zeros((B, H, D, D), jnp.float32), xs)
    return jnp.moveaxis(y, 0, 1)

def rwkv7_time_mix(u, mu, w0, w_up, a0, a_up, g_up, k_k, k_a, r_k, ln_w, ln_b):
    f32 = jnp.float32
    B, S, _ = u.shape
    u = u.astype(f32)
    prev = jnp.pad(u[:, :-1], ((0, 0), (1, 0), (0, 0)))
    u = u + (prev - u) * mu.astype(f32)
    r, k, v, xw, xa, xg = jnp.split(
        u, [RWKV_W, 2 * RWKV_W, 3 * RWKV_W, 3 * RWKV_W + RWKV_W_RANK,
            3 * RWKV_W + RWKV_W_RANK + RWKV_A_RANK], axis=-1)
    log_w = -jax.nn.softplus(-(w0.astype(f32) + jnp.tanh(xw) @ w_up.astype(f32))) - 0.5
    decay = jnp.exp(-jnp.exp(log_w))
    a = jax.nn.sigmoid(a0.astype(f32) + xa @ a_up.astype(f32))
    g = jax.nn.sigmoid(xg) @ g_up.astype(f32)

    def heads(t):
        return t.reshape(B, S, RWKV_HEADS, HEAD_DIM)

    kk = heads(k * k_k.astype(f32))
    kk = kk * lax.rsqrt(jnp.maximum(jnp.sum(kk * kk, axis=-1, keepdims=True), 1e-24))
    k = k * (1.0 + (a - 1.0) * k_a.astype(f32))
    r_h, k_h, v_h, a_h = heads(r), heads(k), heads(v), heads(a)
    y = rwkv7_scan(r_h, heads(decay), k_h, v_h, -kk, kk * a_h)
    mean = jnp.mean(y, axis=-1, keepdims=True)
    var = jnp.mean(jnp.square(y - mean), axis=-1, keepdims=True)
    y = ((y - mean) * lax.rsqrt(var + RWKV_GN_EPS) * ln_w.astype(f32).reshape(RWKV_HEADS, HEAD_DIM)
         + ln_b.astype(f32).reshape(RWKV_HEADS, HEAD_DIM))
    y = y + jnp.sum(r_h * k_h * r_k.astype(f32), axis=-1, keepdims=True) * v_h
    return y.reshape(B, S, RWKV_W) * g

def token_mixing(h, cos, sin, w_in, attn_sinks, mlstm_conv, mlstm_i_bias, mlstm_f_bias, mlstm_norm,
                 rwkv_mu, rwkv_w0, rwkv_w_up, rwkv_a0, rwkv_a_up, rwkv_g_up, rwkv_k_k, rwkv_k_a,
                 rwkv_r_k, rwkv_ln_w, rwkv_ln_b, w_out):
    f32 = jnp.float32
    B, S, _ = h.shape
    proj = h @ w_in
    attn_p, mlstm_p, rwkv_p = jnp.split(proj, [ATTN_COLS, ATTN_COLS + MLSTM_COLS], axis=-1)

    q_at, k_at, v_at = jnp.split(attn_p, [ATTN_W, ATTN_W + KV_W], axis=-1)
    q_at = partial_rope(q_at.reshape(B, S, ATTN_Q_HEADS, HEAD_DIM), cos, sin)
    k_at = partial_rope(k_at.reshape(B, S, ATTN_KV_HEADS, HEAD_DIM), cos, sin)
    v_at = v_at.reshape(B, S, ATTN_KV_HEADS, HEAD_DIM)
    y_attn = sliding_window_gqa(q_at, k_at, v_at, attn_sinks)

    qk_m, v_m, o_m, i_m, f_m = jnp.split(
        mlstm_p, [2 * MLSTM_W, 3 * MLSTM_W, 4 * MLSTM_W, 4 * MLSTM_W + MLSTM_HEADS], axis=-1)
    qk_m = jax.nn.silu(causal_depthwise_conv(qk_m, mlstm_conv))
    q_m, k_m = jnp.split(qk_m, 2, axis=-1)

    def m_heads(t):
        return t.astype(f32).reshape(B, S, MLSTM_HEADS, HEAD_DIM)

    i_pre = GATE_CAP * jnp.tanh((i_m.astype(f32) + mlstm_i_bias.astype(f32)) / GATE_CAP)
    f_pre = GATE_CAP * jnp.tanh((f_m.astype(f32) + mlstm_f_bias.astype(f32)) / GATE_CAP)
    h_m = mlstm_chunkwise(m_heads(q_m), m_heads(k_m), m_heads(v_m), i_pre, f_pre)
    h_m = (h_m * lax.rsqrt(jnp.mean(h_m * h_m, axis=-1, keepdims=True) + NORM_EPS)
           * mlstm_norm.astype(f32).reshape(MLSTM_HEADS, HEAD_DIM))
    y_mlstm = jax.nn.sigmoid(o_m.astype(f32)) * h_m.reshape(B, S, MLSTM_W)

    y_rwkv = rwkv7_time_mix(rwkv_p, rwkv_mu, rwkv_w0, rwkv_w_up, rwkv_a0, rwkv_a_up, rwkv_g_up,
                            rwkv_k_k, rwkv_k_a, rwkv_r_k, rwkv_ln_w, rwkv_ln_b)

    y = jnp.concatenate([y_attn, y_mlstm.astype(h.dtype), y_rwkv.astype(h.dtype)], axis=-1)
    return y @ w_out

def first_inputs(seed: int = 0) -> dict:
    key = jax.random.key(seed)
    ks = iter(jax.random.split(key, 48))
    f32 = jnp.float32

    def normal(shape, scale):
        return scale * jax.random.normal(next(ks), shape, f32)

    def uniform(shape, lo, hi):
        return jax.random.uniform(next(ks), shape, f32, lo, hi)

    def gain(width):
        return 1.0 + normal((DEPTH, width), 0.05)

    x = normal((BATCH, SEQ, D_MODEL), 1.0)
    p = normal((DEPTH, BATCH, SEQ, D_PLE), 1.0)
    start = jax.random.randint(next(ks), (BATCH, 1), 0, 4096, jnp.int32)
    positions = start + jnp.arange(SEQ, dtype=jnp.int32)[None, :]
    return {
        'x': x,
        'p': p,
        'positions': positions,
        'ln_ffn1_pre': gain(D_MODEL),
        'ln_ffn1_post': gain(D_MODEL),
        'w_ffn1_in': normal((DEPTH, D_MODEL, 2 * D_FF), D_MODEL ** -0.5),
        'w_ffn1_out': normal((DEPTH, D_FF, D_MODEL), D_FF ** -0.5),
        'ln_mix_pre': gain(D_MODEL),
        'w_in': normal((DEPTH, D_MODEL, D_IN), D_MODEL ** -0.5),
        'attn_sinks': normal((DEPTH, ATTN_Q_HEADS), 0.5),
        'mlstm_conv': normal((DEPTH, MLSTM_CONV, 2 * MLSTM_W), MLSTM_CONV ** -0.5),
        'mlstm_i_bias': normal((DEPTH, MLSTM_HEADS), 0.1),
        'mlstm_f_bias': uniform((DEPTH, MLSTM_HEADS), 3.0, 6.0),
        'mlstm_norm': gain(MLSTM_W),
        'rwkv_mu': uniform((DEPTH, RWKV_COLS), 0.0, 1.0),
        'rwkv_w0': uniform((DEPTH, RWKV_W), -1.5, 0.5),
        'rwkv_w_up': normal((DEPTH, RWKV_W_RANK, RWKV_W), 0.1),
        'rwkv_a0': normal((DEPTH, RWKV_W), 0.1),
        'rwkv_a_up': normal((DEPTH, RWKV_A_RANK, RWKV_W), 0.5 * RWKV_A_RANK ** -0.5),
        'rwkv_g_up': normal((DEPTH, RWKV_G_RANK, RWKV_W), RWKV_G_RANK ** -0.5),
        'rwkv_k_k': 0.85 + normal((DEPTH, RWKV_W), 0.05),
        'rwkv_k_a': 1.0 + normal((DEPTH, RWKV_W), 0.05),
        'rwkv_r_k': normal((DEPTH, RWKV_HEADS, HEAD_DIM), 0.1),
        'rwkv_ln_w': gain(RWKV_W),
        'rwkv_ln_b': normal((DEPTH, RWKV_W), 0.01),
        'w_out': normal((DEPTH, D_MIX, D_MODEL), D_MIX ** -0.5),
        'ln_mix_post': gain(D_MODEL),
        'ln_ffn2_pre': gain(D_MODEL),
        'ln_ffn2_post': gain(D_MODEL),
        'w_ffn2_in': normal((DEPTH, D_MODEL, 2 * D_FF), D_MODEL ** -0.5),
        'w_ffn2_out': normal((DEPTH, D_FF, D_MODEL), D_FF ** -0.5),
        'ln_ple_pre': gain(D_MODEL),
        'w_ple_gate': normal((DEPTH, D_MODEL, D_MODEL), D_MODEL ** -0.5),
        'w_ple_proj': normal((DEPTH, D_PLE, D_MODEL), D_PLE ** -0.5),
        'ln_ple_post': gain(D_MODEL),
    }

def first_block(x, p, positions, ln_ffn1_pre, ln_ffn1_post, w_ffn1_in, w_ffn1_out, ln_mix_pre, w_in,
              attn_sinks, mlstm_conv, mlstm_i_bias, mlstm_f_bias, mlstm_norm, rwkv_mu, rwkv_w0,
              rwkv_w_up, rwkv_a0, rwkv_a_up, rwkv_g_up, rwkv_k_k, rwkv_k_a, rwkv_r_k, rwkv_ln_w,
              rwkv_ln_b, w_out, ln_mix_post, ln_ffn2_pre, ln_ffn2_post, w_ffn2_in, w_ffn2_out,
              ln_ple_pre, w_ple_gate, w_ple_proj, ln_ple_post):
    cos, sin = rope_tables(positions)
    for l in range(DEPTH):
        x = x + 0.5 * rms_norm(swiglu(rms_norm(x, ln_ffn1_pre[l]), w_ffn1_in[l], w_ffn1_out[l]),
                               ln_ffn1_post[l])
        mix = token_mixing(rms_norm(x, ln_mix_pre[l]), cos, sin, w_in[l], attn_sinks[l],
                           mlstm_conv[l], mlstm_i_bias[l], mlstm_f_bias[l], mlstm_norm[l],
                           rwkv_mu[l], rwkv_w0[l], rwkv_w_up[l], rwkv_a0[l], rwkv_a_up[l],
                           rwkv_g_up[l], rwkv_k_k[l], rwkv_k_a[l], rwkv_r_k[l], rwkv_ln_w[l],
                           rwkv_ln_b[l], w_out[l])
        x = x + rms_norm(mix, ln_mix_post[l])
        x = x + 0.5 * rms_norm(swiglu(rms_norm(x, ln_ffn2_pre[l]), w_ffn2_in[l], w_ffn2_out[l]),
                               ln_ffn2_post[l])
        gate = jax.nn.sigmoid(rms_norm(x, ln_ple_pre[l]) @ w_ple_gate[l])
        x = x + rms_norm(gate * (p[l] @ w_ple_proj[l]), ln_ple_post[l])
    return x


DEPTH_2 = 1

N_HEADS_A = 8
N_KV_A = 2
GQA_GROUP = N_HEADS_A // N_KV_A
N_HEADS_B = 8
WIDTH_A = N_HEADS_A * HEAD_DIM
WIDTH_B = N_HEADS_B * HEAD_DIM
KV_WIDTH_A = N_KV_A * HEAD_DIM
IN_WIDTH = WIDTH_A + 2 * KV_WIDTH_A + 3 * WIDTH_B
CONV_WIDTH = 3
GRID_W = 64
ROPE_THETA_2 = 10000.0
ROPE_AXIS_DIM = HEAD_DIM // 2
Q_BLOCK = 128
DIL_BLOCK = 64
DILATED_PATTERNS = ((128, 1), (512, 4), (2048, 16))
NEG_INF_2 = -1e30


def rms_norm_2(x, g):
    xf = x.astype(jnp.float32)
    y = xf * lax.rsqrt(jnp.mean(xf * xf, axis=-1, keepdims=True) + NORM_EPS)
    return (y * g.astype(jnp.float32)).astype(x.dtype)

def axial_rope_tables(seq_len):
    rows = seq_len // GRID_W
    row = jnp.repeat(jnp.arange(rows, dtype=jnp.float32), GRID_W)
    col = jnp.tile(jnp.arange(GRID_W, dtype=jnp.float32), rows)
    inv = ROPE_THETA_2 ** (-jnp.arange(0, ROPE_AXIS_DIM, 2, dtype=jnp.float32) / ROPE_AXIS_DIM)
    ang_r = row[:, None] * inv[None, :]
    ang_c = col[:, None] * inv[None, :]
    return jnp.cos(ang_r), jnp.sin(ang_r), jnp.cos(ang_c), jnp.sin(ang_c)

def _rotate(u, c, s):
    half = u.shape[-1] // 2
    u1, u2 = u[..., :half], u[..., half:]
    c = c[:, None, :]
    s = s[:, None, :]
    return jnp.concatenate([u1 * c - u2 * s, u2 * c + u1 * s], axis=-1)

def apply_axial_rope(x, tables):
    cos_r, sin_r, cos_c, sin_c = tables
    xf = x.astype(jnp.float32)
    out = jnp.concatenate([_rotate(xf[..., :ROPE_AXIS_DIM], cos_r, sin_r),
                           _rotate(xf[..., ROPE_AXIS_DIM:], cos_c, sin_c)], axis=-1)
    return out.astype(x.dtype)

def global_gqa_attention(q, k, v):
    b, s = q.shape[0], q.shape[1]
    nb = s // Q_BLOCK
    qg = q.reshape(b, nb, Q_BLOCK, N_KV_A, GQA_GROUP, HEAD_DIM).transpose(1, 0, 2, 3, 4, 5)
    scale = HEAD_DIM ** -0.5

    def block(qb):
        sc = jnp.einsum('bqkgd,bskd->bkgqs', qb, k, preferred_element_type=jnp.float32) * scale
        p = jax.nn.softmax(sc, axis=-1)
        return jnp.einsum('bkgqs,bskd->bqkgd', p.astype(v.dtype), v)

    o = lax.map(block, qg)
    return o.transpose(1, 0, 2, 3, 4, 5).reshape(b, s, WIDTH_A)

def alibi_slopes(n_heads):
    return 2.0 ** (-8.0 * jnp.arange(1, n_heads + 1, dtype=jnp.float32) / n_heads)

def dilated_window_attention(q, k, v, window, dilation, slopes):
    b, s, h, hd = q.shape
    d = dilation
    n_side = (window // 2) // d
    L = s // d
    nb = -(-L // DIL_BLOCK)
    Lp = nb * DIL_BLOCK

    def strided(a):
        return a.reshape(b, L, d, h, hd).transpose(0, 2, 1, 3, 4)

    qs = jnp.pad(strided(q), ((0, 0), (0, 0), (0, Lp - L), (0, 0), (0, 0)))
    qb = qs.reshape(b, d, nb, DIL_BLOCK, h, hd)

    def banded(a):
        ap = jnp.pad(strided(a), ((0, 0), (0, 0), (DIL_BLOCK, Lp - L + DIL_BLOCK), (0, 0), (0, 0)))
        ap = ap.reshape(b, d, nb + 2, DIL_BLOCK, h, hd)
        return jnp.concatenate([ap[:, :, :-2], ap[:, :, 1:-1], ap[:, :, 2:]], axis=3)

    kw = banded(k)
    vw = banded(v)

    qi = jnp.arange(DIL_BLOCK)[:, None]
    kj = jnp.arange(3 * DIL_BLOCK)[None, :]
    off = kj - DIL_BLOCK - qi
    key_idx = jnp.arange(nb)[:, None, None] * DIL_BLOCK - DIL_BLOCK + kj[None]
    valid = (jnp.abs(off) <= n_side)[None] & (key_idx >= 0) & (key_idx < L)
    dist = (jnp.abs(off) * d).astype(jnp.float32)
    bias = jnp.where(valid[:, None], -slopes[None, :, None, None] * dist[None, None],
                     NEG_INF_2)

    sc = jnp.einsum('brnqhd,brnkhd->brnhqk', qb, kw, preferred_element_type=jnp.float32)
    sc = sc * (hd ** -0.5) + bias[None, None]
    lse = jax.nn.logsumexp(sc, axis=-1)
    p = jnp.exp(sc - lse[..., None])
    o = jnp.einsum('brnhqk,brnkhd->brnqhd', p.astype(v.dtype), vw)

    o = o.reshape(b, d, Lp, h, hd)[:, :, :L].transpose(0, 2, 1, 3, 4).reshape(b, s, h, hd)
    lse = lse.transpose(0, 1, 2, 4, 3).reshape(b, d, Lp, h)[:, :, :L]
    lse = lse.transpose(0, 2, 1, 3).reshape(b, s, h)
    return o, lse

def dilated_mixture_attention(q, k, v):
    slopes = alibi_slopes(N_HEADS_B)
    outs, lses = [], []
    for window, dilation in DILATED_PATTERNS:
        o, lse = dilated_window_attention(q, k, v, window, dilation, slopes)
        outs.append(o)
        lses.append(lse)
    w = jax.nn.softmax(jnp.stack(lses, axis=0), axis=0)
    o = jnp.sum(w[..., None].astype(q.dtype) * jnp.stack(outs, axis=0), axis=0)
    return o.reshape(q.shape[0], q.shape[1], WIDTH_B)

def conv_ffn(h, w_up, conv_w, conv_b, w_down):
    u = h @ w_up
    c = u.shape[-1]
    u = lax.conv_general_dilated(u, conv_w[:, None, :].astype(u.dtype), window_strides=(1,),
                                 padding=((CONV_WIDTH // 2, CONV_WIDTH // 2),),
                                 dimension_numbers=('NWC', 'WIO', 'NWC'),
                                 feature_group_count=c) + conv_b
    gate, val = u[..., :D_FF], u[..., D_FF:]
    return (jax.nn.gelu(gate) * val) @ w_down

def second_inputs(seed: int = 0) -> dict:
    key = jax.random.key(seed)
    ks = jax.random.split(key, 16)
    f32 = jnp.float32

    def gain(k, n):
        return 1.0 + 0.05 * jax.random.normal(k, (n,), f32)

    return {
        "x": jax.random.normal(ks[0], (BATCH, SEQ, D_MODEL), f32),
        "norm1_g": gain(ks[1], D_MODEL),
        "w_in": jax.random.normal(ks[2], (D_MODEL, IN_WIDTH), f32) * D_MODEL ** -0.5,
        "qa_norm_g": gain(ks[3], HEAD_DIM),
        "ka_norm_g": gain(ks[4], HEAD_DIM),
        "qb_norm_g": gain(ks[5], HEAD_DIM),
        "kb_norm_g": gain(ks[6], HEAD_DIM),
        "outa_norm_g": gain(ks[7], WIDTH_A),
        "outb_norm_g": gain(ks[8], WIDTH_B),
        "w_out": jax.random.normal(ks[9], (WIDTH_A + WIDTH_B, D_MODEL), f32) * (WIDTH_A + WIDTH_B) ** -0.5,
        "norm2_g": gain(ks[10], D_MODEL),
        "w_up": jax.random.normal(ks[11], (D_MODEL, 2 * D_FF), f32) * D_MODEL ** -0.5,
        "conv_w": jax.random.normal(ks[12], (CONV_WIDTH, 2 * D_FF), f32) * CONV_WIDTH ** -0.5,
        "conv_b": 0.02 * jax.random.normal(ks[13], (2 * D_FF,), f32),
        "w_down": jax.random.normal(ks[14], (D_FF, D_MODEL), f32) * D_FF ** -0.5,
    }

def second_block(x, norm1_g, w_in, qa_norm_g, ka_norm_g, qb_norm_g, kb_norm_g,
              outa_norm_g, outb_norm_g, w_out, norm2_g, w_up, conv_w, conv_b, w_down):
    b, s, _ = x.shape
    tables = axial_rope_tables(s)
    for _layer in range(DEPTH_2):
        hn = rms_norm_2(x, norm1_g)
        proj = hn @ w_in
        o1 = WIDTH_A
        o2 = o1 + KV_WIDTH_A
        o3 = o2 + KV_WIDTH_A
        o4 = o3 + WIDTH_B
        o5 = o4 + WIDTH_B
        qa = proj[..., :o1].reshape(b, s, N_HEADS_A, HEAD_DIM)
        ka = proj[..., o1:o2].reshape(b, s, N_KV_A, HEAD_DIM)
        va = proj[..., o2:o3].reshape(b, s, N_KV_A, HEAD_DIM)
        qb = proj[..., o3:o4].reshape(b, s, N_HEADS_B, HEAD_DIM)
        kb = proj[..., o4:o5].reshape(b, s, N_HEADS_B, HEAD_DIM)
        vb = proj[..., o5:].reshape(b, s, N_HEADS_B, HEAD_DIM)

        qa = apply_axial_rope(rms_norm_2(qa, qa_norm_g), tables)
        ka = apply_axial_rope(rms_norm_2(ka, ka_norm_g), tables)
        out_a = global_gqa_attention(qa, ka, va)

        out_b = dilated_mixture_attention(rms_norm_2(qb, qb_norm_g), rms_norm_2(kb, kb_norm_g), vb)

        mixed = jnp.concatenate([rms_norm_2(out_a, outa_norm_g), rms_norm_2(out_b, outb_norm_g)], axis=-1)
        x = x + mixed @ w_out

        x = x + conv_ffn(rms_norm_2(x, norm2_g), w_up, conv_w, conv_b, w_down)
    return x


def setup_inputs(seed=0):
    out = dict(first_inputs(seed))
    for name, value in second_inputs(seed + 1).items():
        if name != "x":
            out[name + "_2"] = value
    return out


def reference(
    x, p, positions, ln_ffn1_pre, ln_ffn1_post, w_ffn1_in, w_ffn1_out, ln_mix_pre, w_in,
    attn_sinks, mlstm_conv, mlstm_i_bias, mlstm_f_bias, mlstm_norm, rwkv_mu, rwkv_w0, rwkv_w_up,
    rwkv_a0, rwkv_a_up, rwkv_g_up, rwkv_k_k, rwkv_k_a, rwkv_r_k, rwkv_ln_w, rwkv_ln_b, w_out,
    ln_mix_post, ln_ffn2_pre, ln_ffn2_post, w_ffn2_in, w_ffn2_out, ln_ple_pre, w_ple_gate,
    w_ple_proj, ln_ple_post, norm1_g_2, w_in_2, qa_norm_g_2, ka_norm_g_2, qb_norm_g_2,
    kb_norm_g_2, outa_norm_g_2, outb_norm_g_2, w_out_2, norm2_g_2, w_up_2, conv_w_2, conv_b_2,
    w_down_2,
):
    x = first_block(
        x, p, positions, ln_ffn1_pre, ln_ffn1_post, w_ffn1_in, w_ffn1_out, ln_mix_pre, w_in,
        attn_sinks, mlstm_conv, mlstm_i_bias, mlstm_f_bias, mlstm_norm, rwkv_mu, rwkv_w0,
        rwkv_w_up, rwkv_a0, rwkv_a_up, rwkv_g_up, rwkv_k_k, rwkv_k_a, rwkv_r_k, rwkv_ln_w,
        rwkv_ln_b, w_out, ln_mix_post, ln_ffn2_pre, ln_ffn2_post, w_ffn2_in, w_ffn2_out,
        ln_ple_pre, w_ple_gate, w_ple_proj, ln_ple_post,
    )
    return second_block(
        x, norm1_g_2, w_in_2, qa_norm_g_2, ka_norm_g_2, qb_norm_g_2, kb_norm_g_2, outa_norm_g_2,
        outb_norm_g_2, w_out_2, norm2_g_2, w_up_2, conv_w_2, conv_b_2, w_down_2,
    )


_drawn_inputs = setup_inputs


def setup_inputs(seed=0):
    import zlib

    import numpy as np

    out = dict(_drawn_inputs(seed))
    spreads = {}
    factors = {'attn_sinks': 6.024,
     'mlstm_i_bias': 8.0,
     'rwkv_k_k': 7.556,
     'rwkv_ln_b': 5.182,
     'ln_ffn2_post': 2.792,
     'ln_ple_pre': 3.942,
     'qa_norm_g_2': 8.0,
     'ka_norm_g_2': 8.0,
     'qb_norm_g_2': 6.523,
     'kb_norm_g_2': 8.0,
     'outa_norm_g_2': 4.639,
     'outb_norm_g_2': 4.156,
     'norm2_g_2': 3.239,
     'conv_b_2': 8.0}
    for name, (base, spread) in spreads.items():
        noise = np.random.default_rng([zlib.crc32(name.encode()), seed]).standard_normal(out[name].shape)
        drawn = base * np.exp(spread * noise) if base else spread * noise
        out[name] = __import__('jax').numpy.asarray(drawn.astype(out[name].dtype))
    for name, factor in factors.items():
        out[name] = (out[name] * factor).astype(out[name].dtype)
    return out
```

```python
from contextlib import ExitStack

import numpy as np

import concourse.bass as bass
from concourse import mybir

F32 = mybir.dt.float32
I32 = mybir.dt.int32
ACT = mybir.ActivationFunctionType
ALU = mybir.AluOpType
AX = mybir.AxisListType.X

P = 128
S = 512
D = 1024
KD = D // P
FF = 2816
KF = FF // P
DEPTH = 2
DH = 64
NT = S // P
HALF = KF // 2
SLOTS = 4
NORM_EPS = 1e-6
GN_EPS = 64e-5
NEG = -1e30
CHUNK = 64
NCH = S // CHUNK
DECAY = float(np.exp(-0.5))
ROPE_DIM = DH // 4
TWO_PI = 2.0 * np.pi
MIX_TILES = 22
PLE = 256

VEC = {}
_at = 0
for _name, _n in (("ffn1_pre", 8), ("ffn1_post", 8), ("mix_pre", 8), ("mix_post", 8), ("ffn2_pre", 8),
                  ("ffn2_post", 8), ("ple_pre", 8), ("ple_post", 8), ("conv", 16), ("m_norm", 2), ("mu", 8),
                  ("w0", 2), ("a0", 2), ("k_k", 2), ("k_a", 2), ("r_k", 2), ("ln_w", 2), ("ln_b", 2),
                  ("sinks", 8), ("i_bias", 1), ("f_bias", 1)):
    VEC[_name] = _at
    _at += _n
NVEC = _at
VEC2 = {}
_at = 0
for _name, _n in (("norm1", 8), ("qa", 1), ("ka", 1), ("qb", 1), ("kb", 1), ("outa", 4), ("outb", 4), ("norm2", 8),
                  ("conv", 2 * 4 * KF)):
    VEC2[_name] = _at
    _at += _n
NVEC2 = _at

MATS = ("ident", "ones", "halves", "rope_turn", "swap", "axial_turn", "strict_low", "strict_up", "incl_up", "causal")


class Stage:

    def __init__(self, nc, name):
        self.nc, self.name, self.ctx, self.sems = nc, name, ExitStack(), []

    def __enter__(self):
        self.ctx.__enter__()
        return self

    def sb(self, name, shape, dt=F32):
        return self.ctx.enter_context(self.nc.sbuf_tensor(f"{self.name}_{name}", shape, dt))

    def sem(self, name):
        s = self.ctx.enter_context(self.nc.semaphore(f"{self.name}_{name}"))
        self.sems.append(s)
        return s

    def __exit__(self, *e):
        if e[0] is None:
            self.nc.all_engine_barrier()
            for s in self.sems:
                self.nc.gpsimd.sem_clear(s)
            self.nc.all_engine_barrier()
        return self.ctx.__exit__(*e)


class Chain:

    def __init__(self, eng, sem):
        self.eng, self.sem, self.n = eng, sem, 0

    def mark(self, ins):
        self.n += 1
        ins.then_inc(self.sem, 1)

    def wait(self):
        if self.n:
            self.eng.wait_ge(self.sem, self.n)

    def link(self, ins):
        self.mark(ins)
        self.wait()


class Chip:
    pass


class PreNorm:

    def __init__(self, st, c):
        self.c = c
        self.squared, self.summed = st.sem("pre_squared"), st.sem("pre_summed")
        self.rooted, self.inverted, self.h_ready = st.sem("pre_rooted"), st.sem("pre_inverted"), st.sem("h_ready")
        self.rs = st.sb("pre_rs", [P, S])

    def scalar(self, act, nc):
        c = self.c
        for k in range(KD):
            nc.scalar.activation(c.h[:, k, :], c.x[:, k, :], ACT.Square).then_inc(self.squared, 1)
        act.wait_ge(self.summed, 1)
        nc.scalar.activation(self.rs[:, :], c.ps[:, 7, :], ACT.Sqrt, bias=c.eps[:, 0:1],
                             scale=1.0 / D).then_inc(self.rooted, 1)

    def tensor(self, pe, nc):
        c = self.c
        for k in range(KD):
            pe.wait_ge(self.squared, k + 1)
            m = nc.tensor.matmul(c.ps[:, 7, :], c.mat["ones"], c.h[:, k, :], start=(k == 0), stop=(k == KD - 1))
        m.then_inc(self.summed, 1)

    def vector(self, dve, nc, gain):
        c = self.c
        dve.wait_ge(self.rooted, 1)
        nc.vector.reciprocal(self.rs[:, :], self.rs[:, :]).then_inc(self.inverted, 1)
        dve.wait_ge(self.inverted, 1)
        for k in range(KD):
            nc.vector.scalar_tensor_tensor(out=c.h[:, k, :], in0=c.x[:, k, :], scalar=gain[:, k:k + 1],
                                           in1=self.rs[:, :], op0=ALU.mult, op1=ALU.mult).then_inc(self.h_ready, 1)


class PostNorm:

    def __init__(self, st, c, factor, lead):
        self.c, self.factor, self.lead = c, factor, lead
        self.y = st.sb("y", [P, KD, S])
        self.sq = c.h
        self.y_ready, self.sq_ready = st.sem("y_ready"), st.sem("sq_ready")
        self.summed, self.rooted, self.inverted = st.sem("post_summed"), st.sem("post_rooted"), st.sem("post_inverted")
        self.scaled, self.added = st.sem("post_scaled"), st.sem("x_added")
        self.rs = st.sb("post_rs", [P, S])

    def tensor(self, pe, nc):
        c = self.c
        for k in range(KD):
            pe.wait_ge(self.sq_ready, k + 1)
            m = nc.tensor.matmul(c.ps[:, 7, :], c.mat["ones"], self.sq[:, k, :], start=(k == 0), stop=(k == KD - 1))
        m.then_inc(self.summed, 1)

    def scalar(self, act, nc):
        c = self.c
        act.wait_ge(self.summed, 1)
        nc.scalar.activation(self.rs[:, :], c.ps[:, 7, :], ACT.Sqrt, bias=c.eps[:, 0:1],
                             scale=1.0 / D).then_inc(self.rooted, 1)

    def vector(self, dve, nc, gain):
        c = self.c
        dve.wait_ge(self.rooted, 1)
        nc.vector.reciprocal(self.rs[:, :], self.rs[:, :]).then_inc(self.inverted, 1)
        dve.wait_ge(self.inverted, 1)
        dve.wait_ge(self.y_ready, self.lead + KD)
        for k in range(KD):
            nc.vector.scalar_tensor_tensor(out=self.y[:, k, :], in0=self.y[:, k, :], scalar=gain[:, k:k + 1],
                                           in1=self.rs[:, :], op0=ALU.mult, op1=ALU.mult).then_inc(self.scaled, 1)
        for k in range(KD):
            dve.wait_ge(self.scaled, k + 1)
            nc.vector.scalar_tensor_tensor(out=c.x[:, k, :], in0=self.y[:, k, :], scalar=self.factor,
                                           in1=c.x[:, k, :], op0=ALU.mult, op1=ALU.add).then_inc(self.added, 1)


class Weights:

    def __init__(self, st, width):
        self.ring = st.sb("w_ring", [P, SLOTS, width])
        self.ready = [st.sem(f"w_ready{s}") for s in range(SLOTS)]


def ffn_stage(nc, c, name, l, w_in, w_out, pre, post_gain):
    with Stage(nc, name) as st:
        norm, post = PreNorm(st, c), PostNorm(st, c, 0.5, SLOTS)
        W = Weights(st, HALF * P)
        act_t = st.sb("act", [P, KF, S])
        silu = st.sb("silu", [P, 2, S])
        done = st.sem("mm_done")
        silu_ready = st.sem("silu_ready")
        act_ready = st.sem("act_ready")
        IN, OUT = 2 * KF // SLOTS, 2 * KD // (2 * SLOTS)
        with nc.Block() as block:
            @block.sync
            def _(sp):
                with sp.Fori(0, IN) as it:
                    for s in range(SLOTS):
                        sp.wait_ge(done, it * SLOTS + s + 1)
                        sp.dma_start(W.ring[:, s, 0:D], w_in[l, it * SLOTS + s]).then_inc(W.ready[s], 16)
                with sp.Fori(0, OUT) as it:
                    for n in range(2 * SLOTS):
                        s = n % SLOTS
                        sp.wait_ge(done, it * (2 * SLOTS) + (2 * KF + n + 1))
                        sp.dma_start(W.ring[:, s, :], w_out[l, it * (2 * SLOTS) + n]).then_inc(W.ready[s], 16)

            @block.tensor
            def _(pe):
                pe.sem_inc(done, SLOTS)
                norm.tensor(pe, nc)
                pe.wait_ge(norm.h_ready, KD)
                with pe.Fori(0, IN) as it:
                    for s in range(SLOTS):
                        pe.wait_ge(W.ready[s], it * 16 + 16)
                        pe.wait_ge(act_ready if s % 2 else silu_ready, it * 2 + s // 2 + 1)
                        for k in range(KD):
                            m = nc.tensor.matmul(c.ps[:, s, :], W.ring[:, s, k * P:(k + 1) * P], c.h[:, k, :],
                                                 start=(k == 0), stop=(k == KD - 1))
                        m.then_inc(done, 1)
                pe.wait_ge(act_ready, 2 + KF)
                with pe.Fori(0, OUT) as it:
                    for b in range(SLOTS):
                        pe.wait_ge(post.y_ready, it * SLOTS + b + 1)
                        for half in range(2):
                            n = 2 * b + half
                            s = n % SLOTS
                            pe.wait_ge(W.ready[s], it * 32 + 16 * (IN + 1 + n // SLOTS))
                            for k in range(HALF):
                                m = nc.tensor.matmul(c.ps[:, b, :], W.ring[:, s, k * P:(k + 1) * P],
                                                     act_t[:, half * HALF + k, :], start=(half == 0 and k == 0),
                                                     stop=(half == 1 and k == HALF - 1))
                            m.then_inc(done, 1)
                post.tensor(pe, nc)

            @block.scalar
            def _(act):
                act.sem_inc(silu_ready, 2)
                norm.scalar(act, nc)
                with act.Fori(0, IN) as it:
                    for q in range(2):
                        act.wait_ge(done, it * SLOTS + (SLOTS + 2 * q + 1))
                        act.wait_ge(act_ready, it * 2 + q + 1)
                        nc.scalar.activation(silu[:, q, :], c.ps[:, 2 * q, :], ACT.Silu).then_inc(silu_ready, 1)
                with act.Fori(0, OUT) as it:
                    for b in range(SLOTS):
                        act.wait_ge(post.y_ready, it * SLOTS + (SLOTS + b + 1))
                        nc.scalar.activation(post.sq[:, it * SLOTS + b, :], post.y[:, it * SLOTS + b, :],
                                             ACT.Square).then_inc(post.sq_ready, 1)
                post.scalar(act, nc)

            @block.vector
            def _(dve):
                dve.sem_inc(act_ready, 2)
                dve.sem_inc(post.y_ready, SLOTS)
                norm.vector(dve, nc, pre)
                with dve.Fori(0, IN) as it:
                    for q in range(2):
                        dve.wait_ge(silu_ready, it * 2 + q + 3)
                        dve.wait_ge(done, it * SLOTS + (SLOTS + 2 * q + 2))
                        nc.vector.tensor_tensor(act_t[:, it * 2 + q, :], silu[:, q, :], c.ps[:, 2 * q + 1, :],
                                                ALU.mult).then_inc(act_ready, 1)
                with dve.Fori(0, OUT) as it:
                    for b in range(SLOTS):
                        dve.wait_ge(done, it * (2 * SLOTS) + (SLOTS + 2 * KF + 2 * b + 2))
                        nc.vector.tensor_copy(post.y[:, it * SLOTS + b, :], c.ps[:, b, :]).then_inc(post.y_ready, 1)
                post.vector(dve, nc, post_gain)


def mix_out_stage(nc, c, l, w_out):
    ITERS = KD // SLOTS
    with Stage(nc, "mixout") as st:
        post = PostNorm(st, c, 1.0, SLOTS)
        post.sq = st.sb("sq", [P, KD, S])
        W = Weights(st, D)
        done = st.sem("mm_done")
        with nc.Block() as block:
            @block.sync
            def _(sp):
                with sp.Fori(0, ITERS) as it:
                    for s in range(SLOTS):
                        sp.wait_ge(done, it * SLOTS + s + 1)
                        sp.dma_start(W.ring[:, s, 0:D], w_out[l, it * SLOTS + s]).then_inc(W.ready[s], 16)

            @block.tensor
            def _(pe):
                pe.sem_inc(done, SLOTS)
                with pe.Fori(0, ITERS) as it:
                    for s in range(SLOTS):
                        pe.wait_ge(W.ready[s], it * 16 + 16)
                        pe.wait_ge(post.y_ready, it * SLOTS + s + 1)
                        for k in range(KD):
                            m = nc.tensor.matmul(c.ps[:, s, :], W.ring[:, s, k * P:(k + 1) * P], c.h[:, k, :],
                                                 start=(k == 0), stop=(k == KD - 1))
                        m.then_inc(done, 1)
                post.tensor(pe, nc)

            @block.scalar
            def _(act):
                with act.Fori(0, ITERS) as it:
                    for b in range(SLOTS):
                        act.wait_ge(post.y_ready, it * SLOTS + (SLOTS + b + 1))
                        nc.scalar.activation(post.sq[:, it * SLOTS + b, :], post.y[:, it * SLOTS + b, :],
                                             ACT.Square).then_inc(post.sq_ready, 1)
                post.scalar(act, nc)

            @block.vector
            def _(dve):
                dve.sem_inc(post.y_ready, SLOTS)
                with dve.Fori(0, ITERS) as it:
                    for b in range(SLOTS):
                        dve.wait_ge(done, it * SLOTS + (SLOTS + b + 1))
                        nc.vector.tensor_copy(post.y[:, it * SLOTS + b, :], c.ps[:, b, :]).then_inc(post.y_ready, 1)
                post.vector(dve, nc, c.vec[:, VEC["mix_post"]:])


def ple_stage(nc, c, l, w_gate, w_proj, p_t):
    KP = PLE // P
    with Stage(nc, "ple") as st:
        norm, post = PreNorm(st, c), PostNorm(st, c, 1.0, 0)
        post.sq = st.sb("sq", [P, KD, S])
        W = Weights(st, D)
        proj_w = st.sb("proj_w", [P, KD, KP * P])
        pt = st.sb("pt", [P, KP, S])
        gate = st.sb("gate", [P, 2, S])
        p_loaded, done, gate_ready = st.sem("p_loaded"), st.sem("mm_done"), st.sem("gate_ready")
        with nc.Block() as block:
            @block.sync
            def _(sp):
                sp.dma_start(proj_w[:, :, :], w_proj[l]).then_inc(p_loaded, 16)
                sp.dma_start(pt[:, :, :], p_t[l]).then_inc(p_loaded, 16)
                for j in range(KD):
                    if j >= SLOTS:
                        sp.wait_ge(done, j - SLOTS + 1)
                    sp.dma_start(W.ring[:, j % SLOTS, 0:D], w_gate[l, j]).then_inc(W.ready[j % SLOTS], 16)

            @block.tensor
            def _(pe):
                norm.tensor(pe, nc)
                pe.wait_ge(p_loaded, 32)
                pe.wait_ge(norm.h_ready, KD)
                for j in range(KD):
                    s, q = j % SLOTS, j % 2
                    if j >= 2:
                        pe.wait_ge(post.y_ready, j - 1)
                    pe.wait_ge(W.ready[s], 16 * (j // SLOTS + 1))
                    for k in range(KP):
                        nc.tensor.matmul(c.ps[:, 2 * q + 1, :], proj_w[:, j, k * P:(k + 1) * P], pt[:, k, :],
                                         start=(k == 0), stop=(k == KP - 1))
                    for k in range(KD):
                        m = nc.tensor.matmul(c.ps[:, 2 * q, :], W.ring[:, s, k * P:(k + 1) * P], c.h[:, k, :],
                                             start=(k == 0), stop=(k == KD - 1))
                    m.then_inc(done, 1)
                post.tensor(pe, nc)

            @block.scalar
            def _(act):
                norm.scalar(act, nc)
                for j in range(KD):
                    act.wait_ge(done, j + 1)
                    if j >= 2:
                        act.wait_ge(post.y_ready, j - 1)
                    nc.scalar.activation(gate[:, j % 2, :], c.ps[:, 2 * (j % 2), :], ACT.Sigmoid).then_inc(gate_ready, 1)
                for j in range(KD):
                    act.wait_ge(post.y_ready, j + 1)
                    nc.scalar.activation(post.sq[:, j, :], post.y[:, j, :], ACT.Square).then_inc(post.sq_ready, 1)
                post.scalar(act, nc)

            @block.vector
            def _(dve):
                norm.vector(dve, nc, c.vec[:, VEC["ple_pre"]:])
                for j in range(KD):
                    dve.wait_ge(gate_ready, j + 1)
                    nc.vector.tensor_tensor(post.y[:, j, :], gate[:, j % 2, :], c.ps[:, 2 * (j % 2) + 1, :],
                                            ALU.mult).then_inc(post.y_ready, 1)
                post.vector(dve, nc, c.vec[:, VEC["ple_post"]:])


def rope_stage(nc, c, positions, inv_freq):
    MAGIC = 1.5 * 2.0 ** 23
    C1 = 6.28125
    C2 = round((TWO_PI - C1) * 2 ** 20) / 2 ** 20
    C3 = float(TWO_PI - C1 - C2)
    EDGE = 3.1415925
    with Stage(nc, "rope") as st:
        pos_i, pos = st.sb("pos_i", [P, S], I32), st.sb("pos", [P, S])
        ang, turns, freq = st.sb("ang", [P, S]), st.sb("turns", [P, S]), st.sb("freq", [P, 1])
        half_pi = st.sb("half_pi", [P, 1])
        loaded, reduced, sines = st.sem("loaded"), st.sem("reduced"), st.sem("sines")
        chain_s = st.sem("dve_chain")
        with nc.Block() as block:
            @block.sync
            def _(sp):
                sp.dma_start(pos_i[:, :], positions).then_inc(loaded, 16)
                sp.dma_start(freq[:, :], inv_freq).then_inc(loaded, 16)

            @block.vector
            def _(dve):
                ch = Chain(dve, chain_s)
                ch.mark(nc.vector.memset(half_pi[:, :], float(np.pi / 2)))
                dve.wait_ge(loaded, 32)
                ch.link(nc.vector.tensor_copy(pos[:, :], pos_i[:, :]))
                ch.link(nc.vector.tensor_scalar(ang[:, :], pos[:, :], freq[:, 0:1], None, ALU.mult))
                ch.link(nc.vector.tensor_scalar(turns[:, :], ang[:, :], 1.0 / TWO_PI, MAGIC, ALU.mult, ALU.add))
                ch.link(nc.vector.tensor_scalar(turns[:, :], turns[:, :], MAGIC, None, ALU.subtract))
                for part in (C1, C2, C3):
                    ch.link(nc.vector.scalar_tensor_tensor(out=ang[:, :], in0=turns[:, :], scalar=-part,
                                                           in1=ang[:, :], op0=ALU.mult, op1=ALU.add))
                nc.vector.tensor_scalar(ang[:, :], ang[:, :], EDGE, -EDGE, ALU.min, ALU.max).then_inc(reduced, 1)

            @block.scalar
            def _(act):
                act.wait_ge(reduced, 1)
                nc.scalar.activation(c.rope[:, 1, :], ang[:, :], ACT.Sin).then_inc(sines, 1)
                nc.scalar.activation(pos[:, :], ang[:, :], ACT.Abs).then_inc(sines, 1)
                act.wait_ge(sines, 2)
                nc.scalar.activation(c.rope[:, 0, :], pos[:, :], ACT.Sin, bias=half_pi[:, 0:1],
                                     scale=-1.0).then_inc(sines, 1)


R_T, K_T, V_T, WA_T, G_T, AQ_T, AK_T, AV_T, MQ_T, MV_T, MO_T = 0, 2, 4, 6, 7, 8, 12, 13, 14, 18, 20


def proj_stage(nc, c, name, w_in, w_gates, tiles, gain):
    FULL = tiles // SLOTS
    assert tiles % SLOTS == 2
    with Stage(nc, name) as st:
        norm = PreNorm(st, c)
        W = Weights(st, D)
        gate_w = st.sb("gate_w", [P, KD, 8])
        done = st.sem("mm_done")
        even, odd = st.sem("even_copied"), st.sem("odd_copied")
        gates_loaded = st.sem("gates_loaded")
        with nc.Block() as block:
            @block.sync
            def _(sp):
                if w_gates is not None:
                    sp.dma_start(gate_w[:, :, :], w_gates).then_inc(gates_loaded, 16)
                with sp.Fori(0, FULL) as it:
                    for s in range(SLOTS):
                        sp.wait_ge(done, it * SLOTS + s + 1)
                        sp.dma_start(W.ring[:, s, :], w_in(it * SLOTS + s)).then_inc(W.ready[s], 16)
                for s in range(2):
                    sp.wait_ge(done, FULL * SLOTS + s + 1)
                    sp.dma_start(W.ring[:, s, :], w_in(FULL * SLOTS + s)).then_inc(W.ready[s], 16)

            @block.tensor
            def _(pe):
                pe.sem_inc(done, SLOTS)
                norm.tensor(pe, nc)
                pe.wait_ge(norm.h_ready, KD)

                def tile(s, uses, ready):
                    pe.wait_ge(W.ready[s], ready)
                    pe.wait_ge(odd if s % 2 else even, uses)
                    for k in range(KD):
                        m = nc.tensor.matmul(c.ps[:, s, :], W.ring[:, s, k * P:(k + 1) * P], c.h[:, k, :],
                                             start=(k == 0), stop=(k == KD - 1))
                    m.then_inc(done, 1)

                with pe.Fori(0, FULL) as it:
                    for s in range(SLOTS):
                        tile(s, it * 2 + s // 2 + 1, it * 16 + 16)
                for s in range(2):
                    tile(s, FULL * 2 + 1, FULL * 16 + 16)
                if w_gates is None:
                    return
                pe.wait_ge(gates_loaded, 16)
                for g in range(2):
                    pe.wait_ge(odd if g else even, FULL * 2 + 2)
                    for k in range(KD):
                        m = nc.tensor.matmul(c.ps[0:4, 2 + g, :], gate_w[:, k, 4 * g:4 * g + 4], c.h[:, k, :],
                                             start=(k == 0), stop=(k == KD - 1))
                    m.then_inc(done, 1)

            @block.scalar
            def _(act):
                act.sem_inc(even, 2)
                norm.scalar(act, nc)
                with act.Fori(0, FULL) as it:
                    for s in (0, 2):
                        act.wait_ge(done, it * SLOTS + (SLOTS + s + 1))
                        nc.scalar.copy(c.proj[:, it * SLOTS + s, :], c.ps[:, s, :]).then_inc(even, 1)
                act.wait_ge(done, SLOTS + FULL * SLOTS + 1)
                nc.scalar.copy(c.proj[:, FULL * SLOTS, :], c.ps[:, 0, :]).then_inc(even, 1)
                if w_gates is None:
                    return
                act.wait_ge(done, SLOTS + FULL * SLOTS + 3)
                nc.scalar.copy(c.gates[0:4, 0, :], c.ps[0:4, 2, :]).then_inc(even, 1)

            @block.vector
            def _(dve):
                dve.sem_inc(odd, 2)
                norm.vector(dve, nc, gain)
                with dve.Fori(0, FULL) as it:
                    for s in (1, 3):
                        dve.wait_ge(done, it * SLOTS + (SLOTS + s + 1))
                        nc.vector.tensor_copy(c.proj[:, it * SLOTS + s, :], c.ps[:, s, :]).then_inc(odd, 1)
                dve.wait_ge(done, SLOTS + FULL * SLOTS + 2)
                nc.vector.tensor_copy(c.proj[:, FULL * SLOTS + 1, :], c.ps[:, 1, :]).then_inc(odd, 1)
                if w_gates is None:
                    return
                dve.wait_ge(done, SLOTS + FULL * SLOTS + 4)
                nc.vector.tensor_copy(c.gates[0:4, 1, :], c.ps[0:4, 3, :]).then_inc(odd, 1)


HEADS, GROUP, WIN = 8, 4, 128


def window_attention_stage(nc, c, window_mask):
    with Stage(nc, "attn") as st:
        q_rot = st.sb("q_rot", [P, 4, S])
        keys = st.sb("keys", [P, 2, WIN + S])
        turned_sin = st.sb("turned_sin", [P, 5, S])
        v_tok = st.sb("v_tok", [P, NT, P])
        mask = st.sb("mask", [P, 2, S])
        masked = st.sb("masked", [P, 2, 4, 2 * WIN])
        probs = st.sb("probs", [P, 2, 4, 2 * WIN])
        probs_t = st.sb("probs_t", [P, 2, 2, S])
        row_max, neg_max = st.sb("row_max", [P, HEADS, 4]), st.sb("neg_max", [P, HEADS, 4])
        row_sum, sink_exp = st.sb("row_sum", [P, HEADS, 4]), st.sb("sink_exp", [P, HEADS, 4])
        loaded, turned, v_turned, v_copied = st.sem("loaded"), st.sem("turned"), st.sem("v_turned"), st.sem("v_copied")
        roped, swapped, swap_copied = st.sem("roped"), st.sem("swapped"), st.sem("swap_copied")
        scored, scores_read, max_ready = st.sem("scored"), st.sem("scores_read"), st.sem("max_ready")
        exps, normed, transposed = st.sem("exps"), st.sem("normed"), st.sem("transposed")
        pt_copied, pv_done, out_copied = st.sem("pt_copied"), st.sem("pv_done"), st.sem("out_copied")
        chain_s = st.sem("dve_chain")
        with nc.Block() as block:
            @block.sync
            def _(sp):
                sp.dma_start(mask[:, :, :], window_mask).then_inc(loaded, 16)

            @block.tensor
            def _(pe):
                for t in range(5):
                    nc.tensor.matmul(c.ps[:, t, :], c.mat["rope_turn"], c.proj[:, AQ_T + t, :],
                                     start=True, stop=True).then_inc(turned, 1)
                for n in range(NT):
                    m = nc.tensor.transpose(c.ps[:, 5, n * P:(n + 1) * P], c.proj[:, AV_T, n * P:(n + 1) * P],
                                            c.mat["ident"])
                m.then_inc(v_turned, 1)
                pe.wait_ge(roped, 5)
                nc.tensor.matmul(c.ps[:, 6, :], c.mat["swap"], keys[:, 0, WIN:WIN + S],
                                 start=True, stop=True).then_inc(swapped, 1)
                pe.wait_ge(v_copied, 1)
                pe.wait_ge(swap_copied, 1)

                def scores(h):
                    q, p0 = h % 2, DH * (h % 2)
                    variant = 0 if h // GROUP == h % 2 else 1
                    if h >= 2:
                        pe.wait_ge(scores_read, 2 * (h - 1))
                    for n in range(NT):
                        m = nc.tensor.matmul(c.ps[:, 2 * q + n // 2, (n % 2) * 2 * WIN:(n % 2 + 1) * 2 * WIN],
                                             q_rot[p0:p0 + DH, h // 2, n * P:(n + 1) * P],
                                             keys[p0:p0 + DH, variant, n * P:n * P + 2 * WIN], start=True, stop=True)
                    m.then_inc(scored, 1)

                def turn_probs(h):
                    pe.wait_ge(normed, 4 * (h + 1))
                    if h >= 1:
                        pe.wait_ge(pt_copied, 2 * h)
                    for n in range(NT):
                        for half in range(2):
                            if n or half:
                                m = nc.tensor.transpose(c.ps[:, 4 + half, n * P:(n + 1) * P],
                                                        probs[:, h % 2, n, half * WIN:(half + 1) * WIN],
                                                        c.mat["ident"])
                    m.then_inc(transposed, 1)

                def values(h):
                    t, p0, v0 = h // 2, DH * (h % 2), DH * (h // GROUP)
                    pe.wait_ge(pt_copied, 2 * (h + 1))
                    if h % 2 == 0 and t >= 2:
                        pe.wait_ge(out_copied, t - 1)
                    for n in range(NT):
                        o = c.ps[p0:p0 + DH, 6 + t % 2, n * P:(n + 1) * P]
                        m = nc.tensor.matmul(o, v_tok[:, n, v0:v0 + DH], probs_t[:, h % 2, 1, n * P:(n + 1) * P],
                                             start=True, stop=(n == 0))
                        if n:
                            m = nc.tensor.matmul(o, v_tok[:, n - 1, v0:v0 + DH],
                                                 probs_t[:, h % 2, 0, n * P:(n + 1) * P], start=False, stop=True)
                    m.then_inc(pv_done, 1)

                for h in range(HEADS + 1):
                    if h < HEADS:
                        scores(h)
                    if h >= 1:
                        turn_probs(h - 1)
                        values(h - 1)

            @block.scalar
            def _(act):
                act.wait_ge(v_turned, 1)
                nc.scalar.copy(v_tok[:, :, :], c.ps[:, 5, :]).then_inc(v_copied, 1)
                act.wait_ge(swapped, 1)
                nc.scalar.copy(keys[:, 1, WIN:WIN + S], c.ps[:, 6, :]).then_inc(swap_copied, 1)

                def exponents(h):
                    act.wait_ge(max_ready, h + 1)
                    if h >= 2:
                        act.wait_ge(transposed, h - 1)
                    for n in range(NT):
                        nc.scalar.activation(probs[:, h % 2, n, :], masked[:, h % 2, n, :], ACT.Exp,
                                             bias=neg_max[:, h, n:n + 1],
                                             accum_out=row_sum[:, h, n:n + 1]).then_inc(exps, 1)
                    nc.scalar.activation(sink_exp[:, h, :], neg_max[:, h, :], ACT.Exp,
                                         bias=c.vec[:, VEC["sinks"] + h:VEC["sinks"] + h + 1]).then_inc(exps, 1)

                def copy_turned(h):
                    act.wait_ge(transposed, h + 1)
                    if h >= 2:
                        act.wait_ge(pv_done, h - 1)
                    nc.scalar.copy(probs_t[:, h % 2, 0, WIN:S], c.ps[:, 4, WIN:S]).then_inc(pt_copied, 1)
                    nc.scalar.copy(probs_t[:, h % 2, 1, :], c.ps[:, 5, :]).then_inc(pt_copied, 1)

                for h in range(HEADS + 1):
                    if h < HEADS:
                        exponents(h)
                    if h >= 1:
                        copy_turned(h - 1)

            @block.vector
            def _(dve):
                ch = Chain(dve, chain_s)
                for v in range(2):
                    ch.mark(nc.vector.memset(keys[:, v, 0:WIN], 0.0))
                for t in range(5):
                    dst = q_rot[:, t, :] if t < 4 else keys[:, 0, WIN:WIN + S]
                    ch.mark(nc.vector.tensor_tensor(dst, c.proj[:, AQ_T + t, :], c.rope[:, 0, :], ALU.mult))
                    dve.wait_ge(turned, t + 1)
                    ch.link(nc.vector.tensor_tensor(turned_sin[:, t, :], c.ps[:, t, :], c.rope[:, 1, :], ALU.mult))
                    nc.vector.tensor_tensor(dst, dst, turned_sin[:, t, :], ALU.add).then_inc(roped, 1)
                dve.wait_ge(roped, 5)
                dve.wait_ge(loaded, 16)

                def maxima(h):
                    dve.wait_ge(scored, h + 1)
                    if h >= 2:
                        dve.wait_ge(exps, 5 * (h - 1))
                    for b in range(2):
                        nc.vector.scalar_tensor_tensor(
                            out=masked[:, h % 2, 2 * b:2 * b + 2, :], in0=c.ps[:, 2 * (h % 2) + b, :],
                            scalar=DH ** -0.5, in1=mask[:, b, :], op0=ALU.mult, op1=ALU.add).then_inc(scores_read, 1)
                    dve.wait_ge(scores_read, 2 * (h + 1))
                    ch.link(nc.vector.tensor_reduce(row_max[:, h, :], masked[:, h % 2, :, :], AX, ALU.max))
                    nc.vector.tensor_scalar(neg_max[:, h, :], row_max[:, h, :],
                                            c.vec[:, VEC["sinks"] + h:VEC["sinks"] + h + 1], -1.0,
                                            ALU.max, ALU.mult).then_inc(max_ready, 1)

                def normalise(h):
                    dve.wait_ge(exps, 5 * (h + 1))
                    ch.link(nc.vector.tensor_tensor(row_sum[:, h, :], row_sum[:, h, :], sink_exp[:, h, :], ALU.add))
                    ch.link(nc.vector.reciprocal(row_sum[:, h, :], row_sum[:, h, :]))
                    for n in range(NT):
                        nc.vector.tensor_scalar(probs[:, h % 2, n, :], probs[:, h % 2, n, :], row_sum[:, h, n:n + 1],
                                                None, ALU.mult).then_inc(normed, 1)

                def copy_out(t):
                    dve.wait_ge(pv_done, 2 * (t + 1))
                    nc.vector.tensor_copy(c.h[:, t, :], c.ps[:, 6 + t % 2, :]).then_inc(out_copied, 1)

                for h in range(HEADS + 1):
                    if h < HEADS:
                        maxima(h)
                    if h >= 1:
                        normalise(h - 1)
                    if h >= 3 and h % 2 == 1:
                        copy_out((h - 3) // 2)
                copy_out(HEADS // 2 - 1)


M_HEADS, CAP = 4, 15.0


def mlstm_stage(nc, c, selectors):
    with Stage(nc, "mlstm") as st:
        qk = st.sb("qk", [P, 4, S])
        g_tanh, soft = st.sb("g_tanh", [4, 2, S]), st.sb("soft", [4, S])
        neg_g, u, run_max = st.sb("neg_g", [4, S]), st.sb("u", [4, S]), st.sb("run_max", [4, S])
        floor, zeros = st.sb("floor", [4, S]), st.sb("zeros", [4, S])
        select = st.sb("select", [4, 6, P])
        u_col = st.sb("u_col", [P, NT, M_HEADS])
        max_all = st.sb("max_all", [P, M_HEADS, S])
        floor_all = st.sb("floor_all", [P, 2, S])
        v_tok = st.sb("v_tok", [P, NT, 2 * P])
        below, weight, weighted_s = st.sb("below", [P, 2, S]), st.sb("weight", [P, 2, S]), st.sb("weighted", [P, 2, S])
        den, hid, sq = st.sb("den", [P, 2, S]), st.sb("hid", [P, 2, S]), st.sb("sq", [P, 2, S])
        o_gate = st.sb("o_gate", [P, 2, S])
        loaded, conv_done, qk_ready = st.sem("loaded"), st.sem("conv_done"), st.sem("qk_ready")
        biased, tanhed, exped, softened = st.sem("biased"), st.sem("tanhed"), st.sem("exped"), st.sem("softened")
        u_ready, max_ready, low_ready, floored = st.sem("u_ready"), st.sem("max_ready"), st.sem("low_ready"), st.sem("floored")
        made, copied = st.sem("made"), st.sem("copied")
        s_done, below_ready, w_ready = st.sem("s_done"), st.sem("below_ready"), st.sem("w_ready")
        weighted, nd_done = st.sem("weighted_ready"), st.sem("nd_done")
        den_abs, hid_ready, squared = st.sem("den_abs"), st.sem("hid_ready"), st.sem("squared")
        summed, rooted, o_ready = st.sem("summed"), st.sem("rooted"), st.sem("o_ready")
        chain_s = st.sem("dve_chain")
        ITEMS = [(h, s) for h in range(M_HEADS) for s in range(NT)]
        with nc.Block() as block:
            @block.sync
            def _(sp):
                sp.dma_start(select[:, :, :], selectors).then_inc(loaded, 16)

            @block.tensor
            def _(pe):
                for half in range(2):
                    for n in range(2):
                        for j in range(2):
                            m = nc.tensor.transpose(c.ps[:, 5 + half, (2 * n + j) * P:(2 * n + j + 1) * P],
                                                    c.proj[:, MV_T + j, (2 * half + n) * P:(2 * half + n + 1) * P],
                                                    c.mat["ident"])
                    m.then_inc(made, 1)
                pe.wait_ge(loaded, 16)
                pe.wait_ge(u_ready, 1)
                for n in range(NT):
                    m = nc.tensor.matmul(c.ps[:, 0, n * M_HEADS:(n + 1) * M_HEADS], u[:, n * P:(n + 1) * P],
                                         c.mats[0:4, MATS.index("ident"), 0:4], start=True, stop=True)
                m.then_inc(made, 1)
                pe.wait_ge(max_ready, 1)
                for h in range(M_HEADS):
                    nc.tensor.matmul(c.ps[:, 1 + h, :], select[:, h, :], run_max[:, :],
                                     start=True, stop=True).then_inc(made, 1)
                pe.wait_ge(floored, 1)
                nc.tensor.matmul(c.ps[:, 7, :], select[:, 4, :], floor[:, :], start=True, stop=True).then_inc(made, 1)
                pe.wait_ge(copied, 1)
                nc.tensor.matmul(c.ps[:, 5, :], select[:, 5, :], floor[:, :], start=True, stop=True).then_inc(made, 1)
                pe.wait_ge(qk_ready, 4)
                pe.wait_ge(copied, 9)

                def scores(i):
                    h, s = ITEMS[i]
                    p0 = DH * (h % 2)
                    if i >= 2:
                        pe.wait_ge(weighted, i - 1)
                    nc.tensor.matmul(c.ps[:, i % 2, 0:S - s * P], qk[p0:p0 + DH, 2 + h // 2, s * P:(s + 1) * P],
                                     qk[p0:p0 + DH, h // 2, s * P:S], start=True, stop=True).then_inc(s_done, 1)

                def sums(i):
                    h, s = ITEMS[i]
                    p0, j = DH * (h % 2), h // 2
                    pe.wait_ge(weighted, i + 1)
                    rhs = weighted_s[:, i % 2, 0:S - s * P]
                    nc.tensor.matmul(c.ps[p0:p0 + DH, 2 + j, s * P:S], v_tok[:, s, h * DH:(h + 1) * DH], rhs,
                                     start=(s == 0), stop=(s == NT - 1))
                    nc.tensor.matmul(c.ps[p0:p0 + DH, 4 + j, s * P:S], c.mats[:, MATS.index("ones"), 0:DH], rhs,
                                     start=(s == 0), stop=(s == NT - 1)).then_inc(nd_done, 1)

                for i in range(len(ITEMS) + 1):
                    if i < len(ITEMS):
                        scores(i)
                    if i >= 1:
                        sums(i - 1)
                for j in range(2):
                    pe.wait_ge(squared, j + 1)
                    nc.tensor.matmul(c.ps[:, 6 + j, :], c.mat["halves"], sq[:, j, :], start=True,
                                     stop=True).then_inc(summed, 1)

            @block.scalar
            def _(act):
                act.wait_ge(biased, 2)
                nc.scalar.activation(g_tanh[:, :, :], c.gates[0:4, :, :], ACT.Tanh, scale=1.0 / CAP).then_inc(tanhed, 1)
                act.wait_ge(tanhed, 1)
                nc.scalar.activation(soft[:, :], g_tanh[:, 1, :], ACT.Exp, scale=-CAP).then_inc(exped, 1)
                act.wait_ge(exped, 1)
                nc.scalar.activation(soft[:, :], soft[:, :], ACT.Ln, bias=1.0).then_inc(softened, 1)
                for t in range(4):
                    act.wait_ge(conv_done, t + 1)
                    nc.scalar.activation(qk[:, t, :], qk[:, t, :], ACT.Silu).then_inc(qk_ready, 1)
                act.wait_ge(made, 1)
                nc.scalar.copy(v_tok[:, 0:2, :], c.ps[:, 5, :]).then_inc(copied, 1)
                act.wait_ge(made, 2)
                nc.scalar.copy(v_tok[:, 2:4, :], c.ps[:, 6, :]).then_inc(copied, 1)
                act.wait_ge(made, 3)
                nc.scalar.copy(u_col[:, :, :], c.ps[:, 0, 0:NT * M_HEADS]).then_inc(copied, 1)
                for h in range(M_HEADS):
                    act.wait_ge(made, 4 + h)
                    nc.scalar.copy(max_all[:, h, :], c.ps[:, 1 + h, :]).then_inc(copied, 1)
                act.wait_ge(low_ready, 1)
                nc.scalar.activation(floor[:, :], floor[:, :], ACT.Exp).then_inc(floored, 1)
                act.wait_ge(made, 8)
                nc.scalar.copy(floor_all[:, 0, :], c.ps[:, 7, :]).then_inc(copied, 1)
                act.wait_ge(made, 9)
                nc.scalar.copy(floor_all[:, 1, :], c.ps[:, 5, :]).then_inc(copied, 1)
                for i, (h, s) in enumerate(ITEMS):
                    act.wait_ge(below_ready, i + 1)
                    if i >= 2:
                        act.wait_ge(weighted, i - 1)
                    nc.scalar.activation(weight[:, i % 2, 0:S - s * P], below[:, i % 2, 0:S - s * P], ACT.Exp,
                                         scale=-1.0).then_inc(w_ready, 1)
                act.wait_ge(nd_done, len(ITEMS))
                for j in range(2):
                    nc.scalar.activation(den[:, j, :], c.ps[:, 4 + j, :], ACT.Abs).then_inc(den_abs, 1)
                for j in range(2):
                    nc.scalar.activation(o_gate[:, j, :], c.proj[:, MO_T + j, :], ACT.Sigmoid).then_inc(o_ready, 1)
                for j in range(2):
                    act.wait_ge(hid_ready, j + 1)
                    nc.scalar.activation(sq[:, j, :], hid[:, j, :], ACT.Square).then_inc(squared, 1)
                for j in range(2):
                    act.wait_ge(summed, j + 1)
                    nc.scalar.activation(den[:, j, :], c.ps[:, 6 + j, :], ACT.Sqrt, bias=c.eps[:, 0:1],
                                         scale=1.0 / DH).then_inc(rooted, 1)

            @block.vector
            def _(dve):
                ch = Chain(dve, chain_s)
                for g, name in ((0, "i_bias"), (1, "f_bias")):
                    nc.vector.tensor_scalar(c.gates[0:4, g, :], c.gates[0:4, g, :], c.vec[0:4, VEC[name]:VEC[name] + 1],
                                            None, ALU.add).then_inc(biased, 1)
                ch.mark(nc.vector.memset(zeros[:, :], 0.0))
                tap = lambda n, t: c.vec[:, VEC["conv"] + 4 * n + t:VEC["conv"] + 4 * n + t + 1]
                for t in range(4):
                    ch.mark(nc.vector.tensor_scalar(qk[:, t, :], c.proj[:, MQ_T + t, :], tap(3, t), None, ALU.mult))
                for back in range(1, 4):
                    ch.wait()
                    for t in range(4):
                        ins = nc.vector.scalar_tensor_tensor(
                            out=qk[:, t, back:S], in0=c.proj[:, MQ_T + t, 0:S - back], scalar=tap(3 - back, t),
                            in1=qk[:, t, back:S], op0=ALU.mult, op1=ALU.add)
                        if back == 3:
                            ins.then_inc(conv_done, 1)
                        else:
                            ch.mark(ins)
                dve.wait_ge(softened, 1)
                ch.link(nc.vector.tensor_tensor_scan(neg_g[:, :], soft[:, :], zeros[:, :], 0.0, ALU.add, ALU.add))
                nc.vector.scalar_tensor_tensor(out=u[:, :], in0=g_tanh[:, 0, :], scalar=CAP, in1=neg_g[:, :],
                                               op0=ALU.mult, op1=ALU.add).then_inc(u_ready, 1)
                dve.wait_ge(u_ready, 1)
                nc.vector.tensor_tensor_scan(run_max[:, :], u[:, :], u[:, :], NEG, ALU.max,
                                             ALU.max).then_inc(max_ready, 1)
                dve.wait_ge(max_ready, 1)
                nc.vector.tensor_tensor(floor[:, :], neg_g[:, :], run_max[:, :], ALU.subtract).then_inc(low_ready, 1)
                dve.wait_ge(copied, 9)

                def exponent(i):
                    h, s = ITEMS[i]
                    if i >= 2:
                        dve.wait_ge(w_ready, i - 1)
                    col = u_col[:, s, h:h + 1]
                    nc.vector.tensor_scalar(below[:, i % 2, 0:S - s * P], max_all[:, h, s * P:S], col, col,
                                            ALU.max, ALU.subtract).then_inc(below_ready, 1)

                exponent(0)
                for i, (h, s) in enumerate(ITEMS):
                    if i + 1 < len(ITEMS):
                        exponent(i + 1)
                    dve.wait_ge(w_ready, i + 1)
                    ch.link(nc.vector.tensor_tensor(weight[:, i % 2, 0:P], weight[:, i % 2, 0:P], c.mat["causal"],
                                                    ALU.mult))
                    dve.wait_ge(s_done, i + 1)
                    if i >= 2:
                        dve.wait_ge(nd_done, i - 1)
                    nc.vector.scalar_tensor_tensor(out=weighted_s[:, i % 2, 0:S - s * P],
                                                   in0=c.ps[:, i % 2, 0:S - s * P], scalar=DH ** -0.5,
                                                   in1=weight[:, i % 2, 0:S - s * P], op0=ALU.mult,
                                                   op1=ALU.mult).then_inc(weighted, 1)
                for j in range(2):
                    dve.wait_ge(den_abs, j + 1)
                    ch.link(nc.vector.tensor_tensor(den[:, j, :], den[:, j, :], floor_all[:, j, :], ALU.max))
                    ch.link(nc.vector.reciprocal(den[:, j, :], den[:, j, :]))
                    nc.vector.tensor_tensor(hid[:, j, :], c.ps[:, 2 + j, :], den[:, j, :], ALU.mult).then_inc(hid_ready, 1)
                dve.wait_ge(hid_ready, 2)
                dve.wait_ge(o_ready, 2)
                for j in range(2):
                    dve.wait_ge(rooted, j + 1)
                    ch.link(nc.vector.reciprocal(den[:, j, :], den[:, j, :]))
                    ch.link(nc.vector.scalar_tensor_tensor(
                        out=hid[:, j, :], in0=hid[:, j, :], scalar=c.vec[:, VEC["m_norm"] + j:VEC["m_norm"] + j + 1],
                        in1=den[:, j, :], op0=ALU.mult, op1=ALU.mult))
                    ch.link(nc.vector.tensor_tensor(c.h[:, 4 + j, :], hid[:, j, :], o_gate[:, j, :], ALU.mult))


R_HEADS = 4
QA, QB, QK, QV = range(4)


def rwkv_stage(nc, c, l, loras, chunk_masks, reset):
    with Stage(nc, "rwkv") as st:
        mix = st.sb("mix", [P, KD, S])
        w_up, g_up = st.sb("w_up", [P, 2 * P]), st.sb("g_up", [P, 2 * P])
        masks = st.sb("masks", [P, 3, 4 * P])
        reset_t = st.sb("reset", [P, S])
        cum_prev, decay_prev, f_a, f_b, f_k, f_r, lora = (c.proj[:, AQ_T + 2 * i:AQ_T + 2 * i + 2, :] for i in range(7))
        sig_w, rate, gate = st.sb("sig_w", [P, 2, S]), st.sb("rate", [P, 2, S]), st.sb("gate", [P, 2, S])
        cum, decay, grow = st.sb("cum", [P, 2, S]), st.sb("decay", [P, 2, S]), st.sb("grow", [P, 2, S])
        kk, sq = st.sb("kk", [P, 2, S]), st.sb("sq", [P, 2, S])
        tok = st.sb("tok", [P, 4, 2 * P])
        N, NT_, akT, rbT, rkT = (st.sb(n, [P, R_HEADS, P]) for n in ("n", "n_t", "ak_t", "rb_t", "rk_t"))
        X = st.sb("x", [P, R_HEADS, P])
        r_prime, y = st.sb("r_prime", [P, 2, S]), st.sb("y", [P, 2, S])
        GH = st.sb("gh", [P, NCH, 2, P])
        state, carried = st.sb("state", [P, NCH + 1, 2, DH]), st.sb("carried", [P, 2, DH])
        loaded, mixed, lora_in, lora_out = st.sem("loaded"), st.sem("mixed"), st.sem("lora_in"), st.sem("lora_out")
        lora_done, cum_ready, decayed = st.sem("lora_done"), st.sem("cum_ready"), st.sem("decayed")
        kk_raw, kk_squared, kk_summed = st.sem("kk_raw"), st.sem("kk_squared"), st.sem("kk_summed")
        kk_floor, kk_root, factors = st.sem("kk_floor"), st.sem("kk_root"), st.sem("factors")
        bonus_in, bonus_sum, bonus_ready = st.sem("bonus_in"), st.sem("bonus_sum"), st.sem("bonus_ready")
        turned, tok_ready, pairs, pairs_masked = st.sem("turned"), st.sem("tok_ready"), st.sem("pairs"), st.sem("pairs_masked")
        av_done, x_ready, a_copied = st.sem("av_done"), st.sem("x_ready"), st.sem("a_copied")
        step_done, powers_copied = st.sem("step_done"), st.sem("powers_copied")
        local_done, local_copied, r_copied = st.sem("local_done"), st.sem("local_copied"), st.sem("r_copied")
        state_done, state_ready, y_state, y_ready = st.sem("state_done"), st.sem("state_ready"), st.sem("y_state"), st.sem("y_ready")
        mean_done, centred, c_squared = st.sem("mean_done"), st.sem("centred"), st.sem("c_squared")
        var_done, var_root = st.sem("var_done"), st.sem("var_root")
        chain_s = st.sem("dve_chain")
        STEPS = 6
        head = lambda h: (h // 2, slice(DH * (h % 2), DH * (h % 2) + DH))
        vcol = lambda name, j: c.vec[:, VEC[name] + j:VEC[name] + j + 1]
        with nc.Block() as block:
            @block.sync
            def _(sp):
                sp.dma_start(w_up[:, :], loras[l, 0]).then_inc(loaded, 16)
                sp.dma_start(g_up[:, :], loras[l, 1]).then_inc(loaded, 16)
                sp.dma_start(reset_t[:, :], reset).then_inc(loaded, 16)
                sp.dma_start(masks[:, :, :], chunk_masks).then_inc(loaded, 16)

            @block.tensor
            def _(pe):
                pe.wait_ge(loaded, 64)
                pe.wait_ge(lora_in, 2)
                pe.wait_ge(mixed, 8)
                for j in range(2):
                    nc.tensor.matmul(c.ps[:, j, :], w_up[0:DH, j * P:(j + 1) * P], lora[0:DH, 0, :],
                                     start=True, stop=True).then_inc(lora_done, 1)
                for j in range(2):
                    nc.tensor.matmul(c.ps[:, 2 + j, :], w_up[DH:P, j * P:(j + 1) * P], mix[DH:P, WA_T, :],
                                     start=True, stop=True).then_inc(lora_done, 1)
                for j in range(2):
                    nc.tensor.matmul(c.ps[:, 4 + j, :], g_up[:, j * P:(j + 1) * P], lora[:, 1, :],
                                     start=True, stop=True).then_inc(lora_done, 1)
                for j in range(2):
                    pe.wait_ge(kk_squared, j + 1)
                    nc.tensor.matmul(c.ps[:, 6 + j, :], c.mat["halves"], sq[:, j, :], start=True,
                                     stop=True).then_inc(kk_summed, 1)
                pe.wait_ge(lora_out, 6)
                for j in range(2):
                    pe.wait_ge(bonus_in, j + 1)
                    nc.tensor.matmul(c.ps[:, j, :], c.mat["halves"], sq[:, j, :], start=True,
                                     stop=True).then_inc(bonus_sum, 1)
                pe.wait_ge(factors, 8)
                pe.wait_ge(bonus_ready, 2)
                for t in range(NT):
                    cols = slice(t * P, (t + 1) * P)
                    if t:
                        pe.wait_ge(local_copied, 3 * t)
                        pe.wait_ge(r_copied, t)
                    for q, src in ((QA, f_a), (QB, f_b), (QK, f_k), (QV, None)):
                        for j in range(2):
                            i = 2 * q + j
                            m = nc.tensor.transpose(c.ps[:, i // 4, (i % 4) * P:(i % 4 + 1) * P],
                                                    src[:, j, cols] if src is not None else mix[:, V_T + j, cols],
                                                    c.mat["ident"])
                    m.then_inc(turned, 1)
                    for b, (left, right) in enumerate(((f_a, f_b), (f_b, f_a), (f_k, f_a), (f_b, f_r), (f_k, f_r))):
                        for q in range(2):
                            rows = slice(DH * q, DH * q + DH)
                            for j in range(2):
                                at = (b % 2) * 2 * P + j * P
                                m = nc.tensor.matmul(c.ps[:, 2 + 3 * q + b // 2, at:at + P], left[rows, j, cols],
                                                     right[rows, j, cols], start=True, stop=True)
                            m.then_inc(pairs, 1)
                    pe.wait_ge(tok_ready, 2 * (t + 1))
                    pe.wait_ge(pairs_masked, 10 * (t + 1))
                    for h in range(R_HEADS):
                        m = nc.tensor.matmul(c.ps[:, 1, h * DH:(h + 1) * DH], akT[:, h, :],
                                             tok[:, QV, h * DH:(h + 1) * DH], start=True, stop=True)
                    m.then_inc(av_done, 1)
                    pe.wait_ge(a_copied, t + 1)
                    for i in range(STEPS):
                        pe.wait_ge(x_ready, (STEPS + 1) * t + i + 1)
                        if i:
                            pe.wait_ge(powers_copied, 2 * ((STEPS - 1) * t + i))
                        for h in range(R_HEADS):
                            m = nc.tensor.matmul(c.ps[:, 0, h * P:(h + 1) * P], NT_[:, h, :], X[:, h, :],
                                                 start=True, stop=True)
                        if i < STEPS - 1:
                            for h in range(R_HEADS):
                                nc.tensor.matmul(c.ps[:, 1, h * P:(h + 1) * P], NT_[:, h, :], N[:, h, :],
                                                 start=True, stop=True)
                            for h in range(R_HEADS):
                                m = nc.tensor.matmul(c.ps[:, 2, h * P:(h + 1) * P], N[:, h, :], NT_[:, h, :],
                                                     start=True, stop=True)
                        m.then_inc(step_done, 1)
                    pe.wait_ge(x_ready, (STEPS + 1) * (t + 1))
                    for h in range(R_HEADS):
                        j, rows = head(h)
                        m = nc.tensor.matmul(c.ps[rows, 3, j * P:(j + 1) * P], X[:, h, DH:P], rbT[:, h, :],
                                             start=True, stop=True)
                    m.then_inc(local_done, 1)
                    for h in range(R_HEADS):
                        j, rows = head(h)
                        o = c.ps[rows, 4, j * P:(j + 1) * P]
                        nc.tensor.matmul(o, X[:, h, 0:DH], rbT[:, h, :], start=True, stop=False)
                        m = nc.tensor.matmul(o, tok[:, QV, h * DH:(h + 1) * DH], rkT[:, h, :], start=False, stop=True)
                    m.then_inc(local_done, 1)
                    for half in range(2):
                        tk = slice(half * CHUNK, (half + 1) * CHUNK)
                        for h in range(R_HEADS):
                            j, rows = head(h)
                            at, hc = j * P, slice(h * DH, (h + 1) * DH)
                            nc.tensor.matmul(c.ps[rows, 5 + half, at:at + DH], X[tk, h, DH:P], tok[tk, QB, hc],
                                             start=True, stop=True)
                            o = c.ps[rows, 5 + half, at + DH:at + P]
                            nc.tensor.matmul(o, tok[tk, QB, hc], X[tk, h, 0:DH], start=True, stop=False)
                            m = nc.tensor.matmul(o, tok[tk, QK, hc], tok[tk, QV, hc], start=False, stop=True)
                        m.then_inc(local_done, 1)
                pe.wait_ge(local_copied, 3 * NT)
                for n in range(NCH):
                    pe.wait_ge(state_ready, n + 1)
                    for h in range(R_HEADS):
                        j, rows = head(h)
                        m = nc.tensor.matmul(c.ps[rows, 6 + n % 2, j * DH:(j + 1) * DH], GH[rows, n, j, 0:DH],
                                             state[rows, n, j, :], start=True, stop=True)
                    m.then_inc(state_done, 1)
                pe.wait_ge(r_copied, NT)
                for j in range(2):
                    for n in range(NCH):
                        for half in range(2):
                            rows = slice(half * DH, half * DH + DH)
                            m = nc.tensor.matmul(c.ps[rows, j, n * CHUNK:(n + 1) * CHUNK], state[rows, n, j, :],
                                                 r_prime[rows, j, n * CHUNK:(n + 1) * CHUNK], start=True, stop=True)
                    m.then_inc(y_state, 1)
                for j in range(2):
                    pe.wait_ge(y_ready, j + 1)
                    nc.tensor.matmul(c.ps[:, 2 + j, :], c.mat["halves"], y[:, j, :], start=True,
                                     stop=True).then_inc(mean_done, 1)
                for j in range(2):
                    pe.wait_ge(c_squared, j + 1)
                    nc.tensor.matmul(c.ps[:, 4 + j, :], c.mat["halves"], sq[:, j, :], start=True,
                                     stop=True).then_inc(var_done, 1)

            @block.scalar
            def _(act):
                act.wait_ge(mixed, 1)
                nc.scalar.activation(lora[0:DH, 0, :], mix[0:DH, WA_T, :], ACT.Tanh).then_inc(lora_in, 1)
                act.wait_ge(mixed, 2)
                nc.scalar.activation(lora[:, 1, :], mix[:, G_T, :], ACT.Sigmoid).then_inc(lora_in, 1)
                for j in range(2):
                    act.wait_ge(lora_done, j + 1)
                    nc.scalar.activation(sig_w[:, j, :], c.ps[:, j, :], ACT.Sigmoid, bias=vcol("w0", j)).then_inc(lora_out, 1)
                for j in range(2):
                    act.wait_ge(lora_done, 2 + j + 1)
                    nc.scalar.activation(rate[:, j, :], c.ps[:, 2 + j, :], ACT.Sigmoid, bias=vcol("a0", j)).then_inc(lora_out, 1)
                for j in range(2):
                    act.wait_ge(lora_done, 4 + j + 1)
                    nc.scalar.copy(gate[:, j, :], c.ps[:, 4 + j, :]).then_inc(lora_out, 1)
                for j in range(2):
                    act.wait_ge(kk_raw, j + 1)
                    nc.scalar.activation(sq[:, j, :], kk[:, j, :], ACT.Square).then_inc(kk_squared, 1)
                for j in range(2):
                    act.wait_ge(cum_ready, 2 * (j + 1))
                    nc.scalar.activation(decay[:, j, :], cum[:, j, :], ACT.Exp, scale=-DECAY).then_inc(decayed, 1)
                    nc.scalar.activation(grow[:, j, :], cum[:, j, :], ACT.Exp, scale=DECAY).then_inc(decayed, 1)
                    nc.scalar.activation(decay_prev[:, j, :], cum_prev[:, j, :], ACT.Exp, scale=-DECAY).then_inc(decayed, 1)
                for j in range(2):
                    act.wait_ge(kk_floor, j + 1)
                    nc.scalar.activation(cum_prev[:, j, :], cum[:, j, :], ACT.Sqrt).then_inc(kk_root, 1)
                for t in range(NT):
                    act.wait_ge(turned, t + 1)
                    if t:
                        act.wait_ge(local_done, 4 * t)
                    for b in range(2):
                        nc.scalar.copy(tok[:, 2 * b:2 * b + 2, :], c.ps[:, b, :]).then_inc(tok_ready, 1)
                    act.wait_ge(tok_ready, 2 * (t + 1))
                    nc.scalar.copy(X[:, :, DH:P], tok[:, QA, :].rearrange("p (h d) -> p h d", h=R_HEADS)).then_inc(a_copied, 1)
                    for i in range(STEPS - 1):
                        act.wait_ge(step_done, STEPS * t + i + 1)
                        nc.scalar.copy(N[:, :, :], c.ps[:, 1, :]).then_inc(powers_copied, 1)
                        nc.scalar.copy(NT_[:, :, :], c.ps[:, 2, :]).then_inc(powers_copied, 1)
                    act.wait_ge(local_done, 4 * t + 2)
                    nc.scalar.copy(y[:, :, t * P:(t + 1) * P],
                                   c.ps[:, 4, 0:2 * P].rearrange("p (j n) -> p j n", j=2)).then_inc(local_copied, 1)
                    for half in range(2):
                        act.wait_ge(local_done, 4 * t + 3 + half)
                        nc.scalar.copy(GH[:, 2 * t + half, :, :], c.ps[:, 5 + half, 0:2 * P]).then_inc(local_copied, 1)
                for j in range(2):
                    act.wait_ge(centred, j + 1)
                    nc.scalar.activation(sq[:, j, :], y[:, j, :], ACT.Square).then_inc(c_squared, 1)
                for j in range(2):
                    act.wait_ge(var_done, j + 1)
                    nc.scalar.activation(cum[:, j, :], c.ps[:, 4 + j, :], ACT.Sqrt, bias=c.eps[:, 1:2],
                                         scale=1.0 / DH).then_inc(var_root, 1)

            @block.vector
            def _(dve):
                ch = Chain(dve, chain_s)
                ORDER = (WA_T, G_T, 2, 3, 0, 1, 4, 5)
                for t in ORDER:
                    u = c.proj[:, R_T + t, :]
                    ch.mark(nc.vector.tensor_tensor(mix[:, t, 1:S], u[:, 0:S - 1], u[:, 1:S], ALU.subtract))
                    ch.mark(nc.vector.tensor_scalar(mix[:, t, 0:1], u[:, 0:1], -1.0, None, ALU.mult))
                ch.wait()
                for t in ORDER:
                    nc.vector.scalar_tensor_tensor(out=mix[:, t, :], in0=mix[:, t, :], scalar=vcol("mu", t),
                                                   in1=c.proj[:, R_T + t, :], op0=ALU.mult, op1=ALU.add).then_inc(mixed, 1)
                ch.mark(nc.vector.memset(state[:, 0, :, :], 0.0))
                dve.wait_ge(mixed, 8)
                for j in range(2):
                    nc.vector.tensor_scalar(kk[:, j, :], mix[:, K_T + j, :], vcol("k_k", j), None, ALU.mult).then_inc(kk_raw, 1)
                dve.wait_ge(loaded, 64)
                for j in range(2):
                    dve.wait_ge(lora_out, j + 1)
                    nc.vector.tensor_tensor_scan(cum[:, j, :], reset_t[:, :], sig_w[:, j, :], 0.0, ALU.mult,
                                                 ALU.add).then_inc(cum_ready, 1)
                    dve.wait_ge(cum_ready, 2 * j + 1)
                    nc.vector.tensor_tensor(cum_prev[:, j, :], cum[:, j, :], sig_w[:, j, :], ALU.subtract).then_inc(cum_ready, 1)
                dve.wait_ge(decayed, 6)
                for j in range(2):
                    dve.wait_ge(kk_summed, j + 1)
                    nc.vector.tensor_scalar(cum[:, j, :], c.ps[:, 6 + j, :], 1e-24, None, ALU.max).then_inc(kk_floor, 1)
                dve.wait_ge(lora_out, 6)
                for j in range(2):
                    ch.link(nc.vector.tensor_scalar(sig_w[:, j, :], rate[:, j, :], 1.0, vcol("k_a", j),
                                                    ALU.subtract, ALU.mult))
                    ch.link(nc.vector.scalar_tensor_tensor(out=sig_w[:, j, :], in0=sig_w[:, j, :], scalar=1.0,
                                                           in1=mix[:, K_T + j, :], op0=ALU.add, op1=ALU.mult))
                    nc.vector.tensor_tensor(f_k[:, j, :], sig_w[:, j, :], grow[:, j, :], ALU.mult).then_inc(factors, 1)
                    nc.vector.tensor_tensor(f_r[:, j, :], mix[:, R_T + j, :], decay[:, j, :], ALU.mult).then_inc(factors, 1)
                    dve.wait_ge(kk_summed, j + 1)
                    nc.vector.scalar_tensor_tensor(out=sq[:, j, :], in0=mix[:, R_T + j, :], scalar=vcol("r_k", j),
                                                   in1=sig_w[:, j, :], op0=ALU.mult, op1=ALU.mult).then_inc(bonus_in, 1)
                for j in range(2):
                    dve.wait_ge(kk_root, j + 1)
                    ch.link(nc.vector.reciprocal(cum_prev[:, j, :], cum_prev[:, j, :]))
                    ch.link(nc.vector.tensor_tensor(kk[:, j, :], kk[:, j, :], cum_prev[:, j, :], ALU.mult))
                    nc.vector.scalar_tensor_tensor(out=f_a[:, j, :], in0=kk[:, j, :], scalar=-1.0,
                                                   in1=decay_prev[:, j, :], op0=ALU.mult, op1=ALU.mult).then_inc(factors, 1)
                    ch.link(nc.vector.tensor_tensor(rate[:, j, :], rate[:, j, :], kk[:, j, :], ALU.mult))
                    nc.vector.tensor_tensor(f_b[:, j, :], rate[:, j, :], grow[:, j, :], ALU.mult).then_inc(factors, 1)
                for j in range(2):
                    dve.wait_ge(bonus_sum, j + 1)
                    dve.wait_ge(factors, 8)
                    nc.vector.tensor_tensor(kk[:, j, :], c.ps[:, j, :], mix[:, V_T + j, :], ALU.mult).then_inc(bonus_ready, 1)
                for t in range(NT):
                    for b, (dst, mask) in enumerate(((N, 0), (NT_, 1), (akT, 1), (rbT, 2), (rkT, 2))):
                        for q in range(2):
                            dve.wait_ge(pairs, 10 * t + 2 * min(b | 1, 4) + q + 1)
                            at = (b % 2) * 2 * P
                            nc.vector.tensor_tensor(
                                dst[:, q::2, :],
                                c.ps[:, 2 + 3 * q + b // 2, at:at + 2 * P].rearrange("p (j n) -> p j n", j=2),
                                masks[:, mask, 0:2 * P].rearrange("p (j n) -> p j n", j=2),
                                ALU.mult).then_inc(pairs_masked, 1)
                    dve.wait_ge(av_done, t + 1)
                    nc.vector.tensor_copy(X[:, :, 0:DH], c.ps[:, 1, 0:R_HEADS * DH].rearrange(
                        "p (h d) -> p h d", h=R_HEADS)).then_inc(x_ready, 1)
                    dve.wait_ge(a_copied, t + 1)
                    dve.wait_ge(x_ready, (STEPS + 1) * t + 1)
                    for i in range(STEPS):
                        dve.wait_ge(step_done, STEPS * t + i + 1)
                        nc.vector.tensor_tensor(X[:, :, :].rearrange("p h n -> p (h n)"),
                                                X[:, :, :].rearrange("p h n -> p (h n)"), c.ps[:, 0, :],
                                                ALU.add).then_inc(x_ready, 1)
                        dve.wait_ge(x_ready, (STEPS + 1) * t + i + 2)
                    dve.wait_ge(local_done, 4 * t + 1)
                    nc.vector.tensor_tensor(r_prime[:, :, t * P:(t + 1) * P],
                                            c.ps[:, 3, 0:2 * P].rearrange("p (j n) -> p j n", j=2),
                                            f_r[:, :, t * P:(t + 1) * P], ALU.add).then_inc(r_copied, 1)
                    dve.wait_ge(local_done, 4 * t + 4)
                dve.wait_ge(local_copied, 3 * NT)
                ch.wait()
                dve.sem_inc(state_ready, 1)
                for n in range(NCH):
                    if n:
                        dve.wait_ge(state_ready, n + 1)
                    ch.link(nc.vector.tensor_tensor(carried[:, :, :], state[:, n, :, :], GH[:, n, :, DH:P], ALU.add))
                    dve.wait_ge(state_done, n + 1)
                    ch.link(nc.vector.tensor_tensor(carried[:, :, :], carried[:, :, :],
                                                    c.ps[:, 6 + n % 2, 0:P].rearrange("p (j d) -> p j d", j=2), ALU.add))
                    end = (n + 1) * CHUNK
                    ch.mark(nc.vector.tensor_scalar(state[:, n + 1, 0, :], carried[:, 0, :], decay[:, 0, end - 1:end],
                                                    None, ALU.mult))
                    ch.link(nc.vector.tensor_scalar(state[:, n + 1, 1, :], carried[:, 1, :], decay[:, 1, end - 1:end],
                                                    None, ALU.mult))
                    dve.sem_inc(state_ready, 1)
                for j in range(2):
                    dve.wait_ge(y_state, j + 1)
                    nc.vector.tensor_tensor(y[:, j, :], y[:, j, :], c.ps[:, j, :], ALU.add).then_inc(y_ready, 1)
                dve.wait_ge(y_ready, 2)
                for j in range(2):
                    dve.wait_ge(mean_done, j + 1)
                    nc.vector.scalar_tensor_tensor(out=y[:, j, :], in0=c.ps[:, 2 + j, :], scalar=-1.0 / DH,
                                                   in1=y[:, j, :], op0=ALU.mult, op1=ALU.add).then_inc(centred, 1)
                dve.wait_ge(centred, 2)
                dve.wait_ge(c_squared, 2)
                for j in range(2):
                    dve.wait_ge(var_root, j + 1)
                    ch.link(nc.vector.reciprocal(cum[:, j, :], cum[:, j, :]))
                    ch.link(nc.vector.scalar_tensor_tensor(out=y[:, j, :], in0=y[:, j, :], scalar=vcol("ln_w", j),
                                                           in1=cum[:, j, :], op0=ALU.mult, op1=ALU.mult))
                    ch.link(nc.vector.scalar_tensor_tensor(out=y[:, j, :], in0=y[:, j, :], scalar=vcol("ln_b", j),
                                                           in1=kk[:, j, :], op0=ALU.add, op1=ALU.add))
                    ch.link(nc.vector.tensor_tensor(c.h[:, 6 + j, :], y[:, j, :], gate[:, j, :], ALU.mult))


SECOND_TILES = 18
A_Q, A_K, A_V, B_Q, B_K, B_V = 0, 4, 5, 6, 10, 14
SPAN = 2 * S - P


def head_norm_stage(nc, c):
    TILES = [(A_Q + t, "qa") for t in range(4)] + [(A_K, "ka")] + [(B_Q + t, "qb") for t in range(4)] + \
            [(B_K + t, "kb") for t in range(4)]
    with Stage(nc, "headnorm") as st:
        sq, root = st.sb("sq", [P, 2, S]), st.sb("root", [P, 2, S])
        turned_sin = st.sb("turned_sin", [P, 5, S])
        squared, summed, rooted, normed = st.sem("squared"), st.sem("summed"), st.sem("rooted"), st.sem("normed")
        turned, roped, swapped = st.sem("turned"), st.sem("roped"), st.sem("swapped")
        v_turned, v_copied, k_copied = st.sem("v_turned"), st.sem("v_copied"), st.sem("k_copied")
        chain_s = st.sem("dve_chain")
        with nc.Block() as block:
            @block.tensor
            def _(pe):
                for i in range(len(TILES)):
                    pe.wait_ge(squared, i + 1)
                    if i >= 2:
                        pe.wait_ge(rooted, i - 1)
                    nc.tensor.matmul(c.ps[:, i % 2, :], c.mat["halves"], sq[:, i % 2, :], start=True,
                                     stop=True).then_inc(summed, 1)
                for j in range(5):
                    if j >= 2:
                        pe.wait_ge(v_copied, j - 1)
                    for n in range(NT):
                        m = nc.tensor.transpose(c.ps[:, 2 + j % 2, n * P:(n + 1) * P],
                                                c.proj[:, A_V if j == 4 else B_V + j, n * P:(n + 1) * P], c.mat["ident"])
                    m.then_inc(v_turned, 1)
                for t in range(5):
                    pe.wait_ge(normed, t + 1)
                    if t == 4:
                        pe.wait_ge(rooted, len(TILES))
                    nc.tensor.matmul(c.ps[:, (4 + t) % 8, :], c.mat["axial_turn"], c.proj[:, t, :], start=True,
                                     stop=True).then_inc(turned, 1)
                pe.wait_ge(roped, 5)
                nc.tensor.matmul(c.ps[:, 1, :], c.mat["swap"], c.proj[:, A_K, :], start=True,
                                 stop=True).then_inc(swapped, 1)

            @block.scalar
            def _(act):
                def square(i):
                    if i >= 2:
                        act.wait_ge(summed, i - 1)
                    nc.scalar.activation(sq[:, i % 2, :], c.proj[:, TILES[i][0], :], ACT.Square).then_inc(squared, 1)

                square(0)
                for i in range(len(TILES)):
                    if i + 1 < len(TILES):
                        square(i + 1)
                    act.wait_ge(summed, i + 1)
                    if i >= 2:
                        act.wait_ge(normed, i - 1)
                    nc.scalar.activation(root[:, i % 2, :], c.ps[:, i % 2, :], ACT.Sqrt, bias=c.eps[:, 0:1],
                                         scale=1.0 / DH).then_inc(rooted, 1)
                for j in range(5):
                    act.wait_ge(v_turned, j + 1)
                    dst = c.va_tok[:, :, :] if j == 4 else c.vb_tok[:, :, j * P:(j + 1) * P]
                    nc.scalar.copy(dst, c.ps[:, 2 + j % 2, :].rearrange("p (n d) -> p n d", n=NT)).then_inc(v_copied, 1)
                act.wait_ge(swapped, 1)
                nc.scalar.copy(c.k_swap[:, :], c.ps[:, 1, :]).then_inc(k_copied, 1)

            @block.vector
            def _(dve):
                ch = Chain(dve, chain_s)
                for i, (t, gain) in enumerate(TILES):
                    dve.wait_ge(rooted, i + 1)
                    ch.link(nc.vector.reciprocal(root[:, i % 2, :], root[:, i % 2, :]))
                    nc.vector.scalar_tensor_tensor(out=c.proj[:, t, :], in0=c.proj[:, t, :],
                                                   scalar=c.vec[:, VEC2[gain]:VEC2[gain] + 1], in1=root[:, i % 2, :],
                                                   op0=ALU.mult, op1=ALU.mult).then_inc(normed, 1)
                for t in range(5):
                    dve.wait_ge(turned, t + 1)
                    ch.mark(nc.vector.tensor_tensor(turned_sin[:, t, :], c.ps[:, (4 + t) % 8, :], c.rope[:, 1, :], ALU.mult))
                    ch.link(nc.vector.tensor_tensor(c.proj[:, t, :], c.proj[:, t, :], c.rope[:, 0, :], ALU.mult))
                    nc.vector.tensor_tensor(c.proj[:, t, :], c.proj[:, t, :], turned_sin[:, t, :], ALU.add).then_inc(roped, 1)


def full_attention_stage(nc, c, biases):
    STEPS = 2 * HEADS * NT
    with Stage(nc, "attn2") as st:
        bias = st.sb("bias", [P, 2, SPAN])
        biased = st.sb("biased", [P, 2, S])
        probs, probs_t = st.sb("probs", [P, 2, S]), st.sb("probs_t", [P, 2, NT, S])
        row_max, neg_max, row_sum = (st.sb(n, [P, STEPS]) for n in ("row_max", "neg_max", "row_sum"))
        loaded = [st.sem(f"bias_loaded{b}") for b in range(2)]
        scored, biased_ready, max_ready, exps = st.sem("scored"), st.sem("biased"), st.sem("max_ready"), st.sem("exps")
        normed, transposed, pt_copied = st.sem("normed"), st.sem("transposed"), st.sem("pt_copied")
        pv_done, out_copied = st.sem("pv_done"), st.sem("out_copied")
        chain_s = st.sem("dve_chain")

        def operands(h):
            rows = slice(DH * (h % 2), DH * (h % 2) + DH)
            if h < HEADS:
                k = c.proj[rows, A_K, :] if h // GROUP == h % 2 else c.k_swap[rows, :]
                return rows, c.proj[rows, A_Q + h // 2, :], k, c.va_tok[:, :, DH * (h // GROUP):DH * (h // GROUP) + DH]
            h -= HEADS
            return rows, c.proj[rows, B_Q + h // 2, :], c.proj[rows, B_K + h // 2, :], c.vb_tok[:, :, DH * h:DH * h + DH]

        with nc.Block() as block:
            @block.sync
            def _(sp):
                for h in range(HEADS):
                    if h >= 2:
                        sp.wait_ge(biased_ready, NT * (h - 1))
                    sp.dma_start(bias[:, h % 2, :], biases[h]).then_inc(loaded[h % 2], 16)

            @block.tensor
            def _(pe):
                def scores(s):
                    h, i = s // NT, s % NT
                    rows, q, k, _ = operands(h)
                    if s >= 2:
                        if (s - 2) // NT < HEADS:
                            pe.wait_ge(exps, s - 1)
                        else:
                            pe.wait_ge(biased_ready, s - 1 - NT * HEADS)
                    nc.tensor.matmul(c.ps[:, s % 2, :], q[:, i * P:(i + 1) * P], k, start=True,
                                     stop=True).then_inc(scored, 1)

                def turn_probs(s):
                    pe.wait_ge(normed, s + 1)
                    if s >= 2:
                        pe.wait_ge(pt_copied, s - 1)
                    for n in range(NT):
                        m = nc.tensor.transpose(c.ps[:, 2 + s % 2, n * P:(n + 1) * P],
                                                probs[:, s % 2, n * P:(n + 1) * P], c.mat["ident"])
                    m.then_inc(transposed, 1)

                def values(h):
                    rows, _, _, v = operands(h)
                    t = h // 2
                    pe.wait_ge(pt_copied, NT * (h + 1))
                    if h % 2 == 0 and t >= 2:
                        pe.wait_ge(out_copied, t - 1)
                    for n in range(NT):
                        m = nc.tensor.matmul(c.ps[rows, 4 + t % 2, :], v[:, n, :], probs_t[:, h % 2, n, :],
                                             start=(n == 0), stop=(n == NT - 1))
                    m.then_inc(pv_done, 1)

                for s in range(STEPS + 2):
                    if s < STEPS:
                        scores(s)
                    if 1 <= s <= STEPS:
                        turn_probs(s - 1)
                    if s >= 2 and (s - 2) % NT == NT - 1:
                        values((s - 2) // NT)

            @block.scalar
            def _(act):
                def exponents(s):
                    act.wait_ge(max_ready, s + 1)
                    if s >= 2:
                        act.wait_ge(transposed, s - 1)
                    first = s // NT < HEADS
                    nc.scalar.activation(probs[:, s % 2, :], c.ps[:, s % 2, :] if first else biased[:, s % 2, :],
                                         ACT.Exp, bias=neg_max[:, s:s + 1], scale=DH ** -0.5 if first else 1.0,
                                         accum_out=row_sum[:, s:s + 1]).then_inc(exps, 1)

                def copy_turned(s):
                    h, i = s // NT, s % NT
                    act.wait_ge(transposed, s + 1)
                    if h >= 2:
                        act.wait_ge(pv_done, h - 1)
                    nc.scalar.copy(probs_t[:, h % 2, :, i * P:(i + 1) * P],
                                   c.ps[:, 2 + s % 2, :].rearrange("p (n q) -> p n q", n=NT)).then_inc(pt_copied, 1)

                for s in range(STEPS + 1):
                    if s < STEPS:
                        exponents(s)
                    if s >= 1:
                        copy_turned(s - 1)

            @block.vector
            def _(dve):
                ch = Chain(dve, chain_s)

                def maxima(s):
                    h, i = s // NT, s % NT
                    dve.wait_ge(scored, s + 1)
                    src, scale = c.ps[:, s % 2, :], -DH ** -0.5
                    if h >= HEADS:
                        b = h - HEADS
                        dve.wait_ge(loaded[b % 2], 16 * (b // 2 + 1))
                        dve.wait_ge(exps, s - 1)
                        start = (NT - 1 - i) * P
                        nc.vector.scalar_tensor_tensor(out=biased[:, s % 2, :], in0=src, scalar=DH ** -0.5,
                                                       in1=bias[:, b % 2, start:start + S], op0=ALU.mult,
                                                       op1=ALU.add).then_inc(biased_ready, 1)
                        dve.wait_ge(biased_ready, s + 1 - NT * HEADS)
                        src, scale = biased[:, s % 2, :], -1.0
                    ch.link(nc.vector.tensor_reduce(row_max[:, s:s + 1], src, AX, ALU.max))
                    nc.vector.tensor_scalar(neg_max[:, s:s + 1], row_max[:, s:s + 1], scale, None,
                                            ALU.mult).then_inc(max_ready, 1)

                def normalise(s):
                    dve.wait_ge(exps, s + 1)
                    ch.link(nc.vector.reciprocal(row_sum[:, s:s + 1], row_sum[:, s:s + 1]))
                    nc.vector.tensor_scalar(probs[:, s % 2, :], probs[:, s % 2, :], row_sum[:, s:s + 1], None,
                                            ALU.mult).then_inc(normed, 1)

                def copy_out(t):
                    dve.wait_ge(pv_done, 2 * (t + 1))
                    nc.vector.tensor_copy(c.h[:, t, :], c.ps[:, 4 + t % 2, :]).then_inc(out_copied, 1)

                for s in range(STEPS + 1):
                    if s < STEPS:
                        maxima(s)
                    if s >= 1:
                        normalise(s - 1)
                    if s >= 2 * NT + 4 and (s - 4) % (2 * NT) == 0:
                        copy_out((s - 4) // (2 * NT) - 1)
                copy_out(HEADS - 1)


def second_out_stage(nc, c, w_out):
    ITERS, HT = KD // SLOTS, KD // 2
    with Stage(nc, "out2") as st:
        W = Weights(st, D)
        sq, root = st.sb("sq", [P, KD, S]), st.sb("root", [P, 2, S])
        squared, summed, rooted, inverted = st.sem("squared"), st.sem("summed"), st.sem("rooted"), st.sem("inverted")
        h_ready = st.sem("h_ready")
        done, added = st.sem("mm_done"), st.sem("x_added")
        with nc.Block() as block:
            @block.sync
            def _(sp):
                with sp.Fori(0, ITERS) as it:
                    for s in range(SLOTS):
                        sp.wait_ge(done, it * SLOTS + s + 1)
                        sp.dma_start(W.ring[:, s, :], w_out[it * SLOTS + s]).then_inc(W.ready[s], 16)

            @block.tensor
            def _(pe):
                pe.sem_inc(done, SLOTS)
                for k in range(KD):
                    pe.wait_ge(squared, k + 1)
                    m = nc.tensor.matmul(c.ps[:, 6 + k // HT, :], c.mat["ones"], sq[:, k, :], start=(k % HT == 0),
                                         stop=(k % HT == HT - 1))
                    if k % HT == HT - 1:
                        m.then_inc(summed, 1)
                pe.wait_ge(h_ready, KD)
                with pe.Fori(0, ITERS) as it:
                    for s in range(SLOTS):
                        pe.wait_ge(W.ready[s], it * 16 + 16)
                        pe.wait_ge(added, it * SLOTS + s + 1)
                        for k in range(KD):
                            m = nc.tensor.matmul(c.ps[:, s, :], W.ring[:, s, k * P:(k + 1) * P], c.h[:, k, :],
                                                 start=(k == 0), stop=(k == KD - 1))
                        m.then_inc(done, 1)

            @block.scalar
            def _(act):
                for k in range(KD):
                    nc.scalar.activation(sq[:, k, :], c.h[:, k, :], ACT.Square).then_inc(squared, 1)
                for g in range(2):
                    act.wait_ge(summed, g + 1)
                    nc.scalar.activation(root[:, g, :], c.ps[:, 6 + g, :], ACT.Sqrt, bias=c.eps[:, 0:1],
                                         scale=1.0 / (HT * P)).then_inc(rooted, 1)

            @block.vector
            def _(dve):
                dve.sem_inc(added, SLOTS)
                for g in range(2):
                    dve.wait_ge(rooted, g + 1)
                    nc.vector.reciprocal(root[:, g, :], root[:, g, :]).then_inc(inverted, 1)
                    dve.wait_ge(inverted, g + 1)
                    for k in range(HT * g, HT * g + HT):
                        at = VEC2["outa"] + k
                        nc.vector.scalar_tensor_tensor(out=c.h[:, k, :], in0=c.h[:, k, :], scalar=c.vec[:, at:at + 1],
                                                       in1=root[:, g, :], op0=ALU.mult, op1=ALU.mult).then_inc(h_ready, 1)
                with dve.Fori(0, ITERS) as it:
                    for b in range(SLOTS):
                        dve.wait_ge(done, it * SLOTS + (SLOTS + b + 1))
                        nc.vector.tensor_tensor(c.x[:, it * SLOTS + b, :], c.x[:, it * SLOTS + b, :], c.ps[:, b, :],
                                                ALU.add).then_inc(added, 1)


def conv_ffn_stage(nc, c, w_up, w_down):
    with Stage(nc, "convffn") as st:
        norm = PreNorm(st, c)
        W = Weights(st, HALF * P)
        act_t = st.sb("act", [P, KF, S])
        conv, gelu = st.sb("conv", [P, SLOTS, S]), st.sb("gelu", [P, 2, S])
        done = st.sem("mm_done")
        middle, side = st.sem("middle_tap"), st.sem("side_tap")
        conv_ready = st.sem("conv_ready")
        gelu_ready = st.sem("gelu_ready")
        act_ready = st.sem("act_ready")
        added = st.sem("x_added")
        IN, OUT = 2 * KF // SLOTS, 2 * KD // (2 * SLOTS)
        with nc.Block() as block:
            @block.sync
            def _(sp):
                with sp.Fori(0, IN) as it:
                    for s in range(SLOTS):
                        sp.wait_ge(done, it * SLOTS + s + 1)
                        sp.dma_start(W.ring[:, s, 0:D], w_up[it * SLOTS + s]).then_inc(W.ready[s], 16)
                with sp.Fori(0, OUT) as it:
                    for n in range(2 * SLOTS):
                        s = n % SLOTS
                        sp.wait_ge(done, it * (2 * SLOTS) + (2 * KF + n + 1))
                        sp.dma_start(W.ring[:, s, :], w_down[it * (2 * SLOTS) + n]).then_inc(W.ready[s], 16)

            @block.tensor
            def _(pe):
                pe.sem_inc(done, SLOTS)
                norm.tensor(pe, nc)
                pe.wait_ge(norm.h_ready, KD)
                with pe.Fori(0, IN) as it:
                    for s in range(SLOTS):
                        pe.wait_ge(W.ready[s], it * 16 + 16)
                        pe.wait_ge(conv_ready, it * SLOTS + s + 1)
                        for k in range(KD):
                            m = nc.tensor.matmul(c.ps[:, s, :], W.ring[:, s, k * P:(k + 1) * P], c.h[:, k, :],
                                                 start=(k == 0), stop=(k == KD - 1))
                        m.then_inc(done, 1)
                pe.wait_ge(act_ready, 2 + KF)
                with pe.Fori(0, OUT) as it:
                    for b in range(SLOTS):
                        pe.wait_ge(added, it * SLOTS + b + 1)
                        for half in range(2):
                            n = 2 * b + half
                            s = n % SLOTS
                            pe.wait_ge(W.ready[s], it * 32 + 16 * (IN + 1 + n // SLOTS))
                            for k in range(HALF):
                                m = nc.tensor.matmul(c.ps[:, b, :], W.ring[:, s, k * P:(k + 1) * P],
                                                     act_t[:, half * HALF + k, :], start=(half == 0 and k == 0),
                                                     stop=(half == 1 and k == HALF - 1))
                            m.then_inc(done, 1)

            vec = lambda it, s, i: c.vec[:, bass.ds(it * (4 * SLOTS) + (VEC2["conv"] + 4 * s + i), 1)]

            @block.scalar
            def _(act):
                norm.scalar(act, nc)
                with act.Fori(0, IN) as it:
                    for s in range(SLOTS):
                        act.wait_ge(done, it * SLOTS + (SLOTS + s + 1))
                        act.wait_ge(act_ready, it * 2 + s // 2 + 1)
                        nc.scalar.activation(conv[:, s, :], c.ps[:, s, :], ACT.Identity, bias=vec(it, s, 3),
                                             scale=vec(it, s, 1)).then_inc(middle, 1)
                    for q in range(2):
                        act.wait_ge(conv_ready, it * SLOTS + (SLOTS + 2 * q + 1))
                        nc.scalar.activation(gelu[:, q, :], conv[:, 2 * q, :], ACT.Gelu_apprx_tanh).then_inc(gelu_ready, 1)

            @block.vector
            def _(dve):
                dve.sem_inc(conv_ready, SLOTS)
                dve.sem_inc(act_ready, 2)
                dve.sem_inc(added, SLOTS)
                norm.vector(dve, nc, c.vec[:, VEC2["norm2"]:])
                with dve.Fori(0, IN) as it:
                    for s in range(SLOTS):
                        dve.wait_ge(middle, it * SLOTS + s + 1)
                        nc.vector.scalar_tensor_tensor(out=conv[:, s, 1:S], in0=c.ps[:, s, 0:S - 1], scalar=vec(it, s, 0),
                                                       in1=conv[:, s, 1:S], op0=ALU.mult, op1=ALU.add).then_inc(side, 1)
                        dve.wait_ge(side, it * SLOTS + s + 1)
                        nc.vector.scalar_tensor_tensor(out=conv[:, s, 0:S - 1], in0=c.ps[:, s, 1:S], scalar=vec(it, s, 2),
                                                       in1=conv[:, s, 0:S - 1], op0=ALU.mult,
                                                       op1=ALU.add).then_inc(conv_ready, 1)
                    for q in range(2):
                        dve.wait_ge(gelu_ready, it * 2 + q + 1)
                        dve.wait_ge(conv_ready, it * SLOTS + (SLOTS + 2 * q + 2))
                        nc.vector.tensor_tensor(act_t[:, it * 2 + q, :], gelu[:, q, :], conv[:, 2 * q + 1, :],
                                                ALU.mult).then_inc(act_ready, 1)
                with dve.Fori(0, OUT) as it:
                    for b in range(SLOTS):
                        dve.wait_ge(done, it * (2 * SLOTS) + (SLOTS + 2 * KF + 2 * b + 2))
                        nc.vector.tensor_tensor(c.x[:, it * SLOTS + b, :], c.x[:, it * SLOTS + b, :], c.ps[:, b, :],
                                                ALU.add).then_inc(added, 1)


def load_stage(nc, c, x_t, mats):
    with Stage(nc, "load") as st:
        loaded, made = st.sem("loaded"), st.sem("made")
        with nc.Block() as block:
            @block.sync
            def _(sp):
                sp.dma_start(c.x[:, :, :], x_t).then_inc(loaded, 16)
                sp.dma_start(c.mats[:, :, :], mats).then_inc(loaded, 16)
                sp.wait_ge(loaded, 32)

            @block.vector
            def _(dve):
                nc.vector.memset(c.eps[:, 0:1], NORM_EPS).then_inc(made, 1)
                nc.vector.memset(c.eps[:, 1:2], GN_EPS).then_inc(made, 1)
                dve.wait_ge(made, 2)


def vec_stage(nc, c, l, vecs, rope=None):
    with Stage(nc, "vec") as st:
        loaded = st.sem("loaded")
        with nc.Block() as block:
            @block.sync
            def _(sp):
                sp.dma_start(c.vec[:, 0:vecs.shape[-1]], vecs[l] if l is not None else vecs).then_inc(loaded, 16)
                if rope is not None:
                    sp.dma_start(c.rope[:, :, :], rope).then_inc(loaded, 16)
                sp.wait_ge(loaded, 16 if rope is None else 32)


def store_stage(nc, c, out):
    with Stage(nc, "store") as st:
        stored = st.sem("stored")
        with nc.Block() as block:
            @block.sync
            def _(sp):
                sp.dma_start(out, c.x[:, :, :]).then_inc(stored, 16)
                sp.wait_ge(stored, 16)


def build(nc, a, out):
    c = Chip()
    with ExitStack() as ctx:
        def sb(name, shape, dt=F32):
            return ctx.enter_context(nc.sbuf_tensor(name, shape, dt))

        c.ps = ctx.enter_context(nc.psum_tensor("ps", [P, 8, S], F32))
        c.x, c.h = sb("x", [P, KD, S]), sb("h", [P, KD, S])
        c.mats = sb("mats", [P, len(MATS), P])
        c.mat = {m: c.mats[:, i, :] for i, m in enumerate(MATS)}
        c.vec = sb("vec", [P, max(NVEC, NVEC2)])
        c.eps = sb("eps", [P, 2])
        c.rope = sb("rope", [P, 2, S])
        load_stage(nc, c, a["x"], a["mats"])
        rope_stage(nc, c, a["positions"], a["inv_freq"])
        with nc.Fori(0, DEPTH) as l:
            vec_stage(nc, c, l, a["vecs"])
            ffn_stage(nc, c, "ffn1", l, a["w_ffn1_in"], a["w_ffn1_out"], c.vec[:, VEC["ffn1_pre"]:],
                      c.vec[:, VEC["ffn1_post"]:])
            with ExitStack() as mix:
                c.proj = mix.enter_context(nc.sbuf_tensor("proj", [P, MIX_TILES, S], F32))
                c.gates = mix.enter_context(nc.sbuf_tensor("gates", [4, 2, S], F32))
                proj_stage(nc, c, "mixproj", lambda n: a["w_in"][l, n], a["w_gates"][l], MIX_TILES,
                           c.vec[:, VEC["mix_pre"]:])
                window_attention_stage(nc, c, a["window_mask"])
                mlstm_stage(nc, c, a["selectors"])
                rwkv_stage(nc, c, l, a["loras"], a["chunk_masks"], a["reset"])
            mix_out_stage(nc, c, l, a["w_out"])
            ffn_stage(nc, c, "ffn2", l, a["w_ffn2_in"], a["w_ffn2_out"], c.vec[:, VEC["ffn2_pre"]:],
                      c.vec[:, VEC["ffn2_post"]:])
            ple_stage(nc, c, l, a["w_ple_gate"], a["w_ple_proj"], a["p"])
        vec_stage(nc, c, None, a["vecs_2"], a["axial"])
        with ExitStack() as second:
            def sb2(name, shape):
                return second.enter_context(nc.sbuf_tensor(name, shape, F32))

            c.proj = sb2("proj_2", [P, SECOND_TILES, S])
            c.va_tok, c.vb_tok, c.k_swap = sb2("va_tok", [P, NT, P]), sb2("vb_tok", [P, NT, 4 * P]), sb2("k_swap", [P, S])
            proj_stage(nc, c, "proj2", lambda n: a["w_in_2"][n], None, SECOND_TILES, c.vec[:, VEC2["norm1"]:])
            head_norm_stage(nc, c)
            full_attention_stage(nc, c, a["biases"])
        second_out_stage(nc, c, a["w_out_2"])
        conv_ffn_stage(nc, c, a["w_up_2"], a["w_down_2"])
        store_stage(nc, c, out)


def columns(w):
    k, n = w.shape
    return np.ascontiguousarray(w.reshape(k // P, P, n // P, P).transpose(2, 1, 0, 3)).reshape(n // P, P, -1)


def halves(w):
    t = columns(w)
    return np.ascontiguousarray(t.reshape(t.shape[0], P, 2, -1).transpose(0, 2, 1, 3)).reshape(2 * t.shape[0], P, -1)


def gate_up(w):
    t = columns(w)
    n = t.shape[0] // 2
    return np.ascontiguousarray(np.stack([t[:n], t[n:]], 1)).reshape(2 * n, P, -1)


def per_partition(v):
    return v.reshape(-1, P).T


def shape_matrices():
    i = np.arange(P)
    row, col = i[:, None], i[None, :]
    same_half, same_chunk = row // DH == col // DH, row // CHUNK == col // CHUNK
    turn = np.zeros((P, P), np.float32)
    axial = np.zeros((P, P), np.float32)
    for m in range(P):
        d = m % DH
        if d < ROPE_DIM // 2:
            turn[m + ROPE_DIM // 2, m] = -1.0
        elif d < ROPE_DIM:
            turn[m - ROPE_DIM // 2, m] = 1.0
        if d % 32 < 16:
            axial[m + 16, m] = -1.0
        else:
            axial[m - 16, m] = 1.0
    m = {"ident": row == col, "ones": (row >= 0) & (col >= 0), "halves": same_half, "rope_turn": turn,
         "swap": (row + DH) % P == col, "axial_turn": axial, "strict_low": same_chunk & (row > col),
         "strict_up": same_chunk & (row < col), "incl_up": same_chunk & (row <= col), "causal": row <= col}
    return np.ascontiguousarray(np.stack([np.asarray(m[n], np.float32) for n in MATS], 1))


def layouts(inputs):
    f = {n: np.asarray(v) for n, v in inputs.items()}
    a = {}
    feature_tiles = lambda t: np.ascontiguousarray(t.T.reshape(-1, P, S).transpose(1, 0, 2))
    each = lambda fn, w: np.stack([fn(w[l]) for l in range(DEPTH)])
    a["x"] = feature_tiles(f["x"][0])
    a["p"] = np.stack([feature_tiles(f["p"][l, 0]) for l in range(DEPTH)])
    a["mats"] = shape_matrices()
    for n in ("ffn1", "ffn2"):
        a[f"w_{n}_in"] = each(gate_up, f[f"w_{n}_in"])
        a[f"w_{n}_out"] = each(halves, f[f"w_{n}_out"])
    a["w_ple_gate"] = each(columns, f["w_ple_gate"])
    a["w_ple_proj"] = each(lambda w: np.ascontiguousarray(columns(w).transpose(1, 0, 2)), f["w_ple_proj"])
    vecs = np.zeros((DEPTH, P, NVEC), np.float32)
    for l in range(DEPTH):
        def put(name, cols):
            vecs[l, :cols.shape[0], VEC[name]:VEC[name] + cols.shape[1]] = cols
        for n in ("ffn1", "mix", "ffn2", "ple"):
            put(n + "_pre", per_partition(f[f"ln_{n}_pre"][l]))
            put(n + "_post", per_partition(f[f"ln_{n}_post"][l]))
        for t in range(4):
            put_at = f["mlstm_conv"][l][t]
            vecs[l, :, VEC["conv"] + 4 * t:VEC["conv"] + 4 * t + 4] = per_partition(put_at)
        put("m_norm", per_partition(f["mlstm_norm"][l]))
        for n in ("mu", "w0", "a0", "k_k", "k_a", "ln_w", "ln_b"):
            put(n, per_partition(f["rwkv_" + n][l]))
        put("r_k", per_partition(f["rwkv_r_k"][l].reshape(-1)))
        put("sinks", np.broadcast_to(f["attn_sinks"][l], (P, 8)))
        put("i_bias", f["mlstm_i_bias"][l][:, None])
        put("f_bias", f["mlstm_f_bias"][l][:, None])
    a["vecs"] = vecs
    attn_cols, rwkv_at = 768, 768 + 1032
    pick = np.r_[rwkv_at:rwkv_at + 1024, 0:attn_cols + 1024]
    a["w_in"] = each(lambda w: columns(w[:, pick]), f["w_in"])
    a["w_gates"] = each(lambda w: w[:, rwkv_at - 8:rwkv_at].reshape(KD, P, 8).transpose(1, 0, 2), f["w_in"])
    a["w_out"] = each(columns, f["w_out"])
    a["loras"] = np.stack([np.stack([np.concatenate([f["rwkv_w_up"][l], f["rwkv_a_up"][l]]), f["rwkv_g_up"][l]])
                           for l in range(DEPTH)])
    a["positions"] = np.broadcast_to(f["positions"].astype(np.int32, copy=False), (P, S))
    d = np.arange(P) % DH
    inv = 500000.0 ** (-2.0 * (d % (ROPE_DIM // 2)) / ROPE_DIM)
    a["inv_freq"] = np.where(d < ROPE_DIM, inv, 0.0).astype(np.float32)[:, None]
    lag = np.arange(P)[:, None] + WIN - np.arange(2 * WIN)[None, :]
    band = (lag >= 0) & (lag < WIN)
    blocks = np.stack([band & ((n > 0) | (np.arange(2 * WIN) >= WIN)) for n in range(NT)], 1)
    a["window_mask"] = np.where(blocks, 0.0, NEG).astype(np.float32).reshape(P, 2, S)
    sel = np.zeros((4, 6, P), np.float32)
    for h in range(4):
        sel[h, h] = 1.0
        sel[h, 4 + h // 2, DH * (h % 2):DH * (h % 2) + DH] = 1.0
    a["selectors"] = sel
    m = a["mats"]
    a["chunk_masks"] = np.stack([np.tile(m[:, MATS.index(n)], 4) for n in ("strict_low", "strict_up", "incl_up")], 1)
    a["reset"] = np.broadcast_to((np.arange(S) % CHUNK != 0).astype(np.float32), (P, S))
    a["w_in_2"], a["w_out_2"] = columns(f["w_in_2"]), columns(f["w_out_2"])
    a["w_up_2"], a["w_down_2"] = gate_up(f["w_up_2"]), halves(f["w_down_2"])
    v2 = np.zeros((P, NVEC2), np.float32)
    for name, n in (("norm1", "norm1_g_2"), ("outa", "outa_norm_g_2"), ("outb", "outb_norm_g_2"), ("norm2", "norm2_g_2")):
        cols = per_partition(f[n])
        v2[:, VEC2[name]:VEC2[name] + cols.shape[1]] = cols
    for name in ("qa", "ka", "qb", "kb"):
        v2[:, VEC2[name]] = np.concatenate([f[f"{name}_norm_g_2"]] * 2)
    taps = np.concatenate([f["conv_w_2"], f["conv_b_2"][None]])
    v2[:, VEC2["conv"]:] = taps.reshape(4, 2, KF, P).transpose(3, 2, 1, 0).reshape(P, -1)
    a["vecs_2"] = v2
    token, d = np.arange(S), np.arange(P) % DH
    place = np.where(d[:, None] < 32, token[None] // 64, token[None] % 64)
    angle = place * (10000.0 ** (-2.0 * (d % 16) / 32))[:, None]
    a["axial"] = np.stack([np.cos(angle), np.sin(angle)], 1).astype(np.float32)
    apart = np.abs(np.arange(P)[:, None] + (NT - 1) * P - np.arange(SPAN)[None, :])
    count = sum((apart % step == 0) & (apart <= window // 2) for window, step in ((128, 1), (512, 4), (2048, 16)))
    held = np.where(count > 0, np.log(np.maximum(count, 1)), NEG)
    a["biases"] = np.stack([held - 2.0 ** -(h + 1) * apart for h in range(8)]).astype(np.float32)
    return a


def kernel(**inputs):
    import concourse.bacc as bacc
    from concourse.bass_utils import run_bass_kernel_spmd

    nc = bacc.Bacc("TRN2", target_bir_lowering=False, num_devices=1)
    arrays = {f"in_{n}": np.ascontiguousarray(v) for n, v in layouts(inputs).items()}
    aps = {n[3:]: nc.dram_tensor(n, v.shape, mybir.dt.from_np(v.dtype), kind="ExternalInput").ap()
           for n, v in arrays.items()}
    out = nc.dram_tensor("out", (P, KD, S), F32, kind="ExternalOutput").ap()
    build(nc, aps, out)
    run = run_bass_kernel_spmd(nc, [arrays], core_ids=[0])
    y = run.results[0]["out"]
    return np.ascontiguousarray(np.asarray(y).transpose(1, 0, 2).reshape(D, S).T).reshape(1, S, D)
```

```python
from contextlib import ExitStack

import numpy as np

import concourse.bass as bass
from concourse import mybir

F32 = mybir.dt.float32
I32 = mybir.dt.int32
F32R = mybir.dt.float32r
ACT = mybir.ActivationFunctionType
ALU = mybir.AluOpType
AX = mybir.AxisListType.X

P = 128
S = 512
D = 1024
KD = D // P
FF = 2816
KF = FF // P
DEPTH = 2
DH = 64
NT = S // P
SLOTS = 4
NORM_EPS = 1e-6
GN_EPS = 64e-5
NEG = -1e30
CHUNK = 64
NCH = S // CHUNK
DECAY = float(np.exp(-0.5))
ROPE_DIM = DH // 4
TWO_PI = 2.0 * np.pi
MIX_TILES = 22
PLE = 256

VEC = {}
_at = 0
for _name, _n in (("ffn1_pre", 8), ("ffn1_post", 8), ("mix_pre", 8), ("mix_post", 8), ("ffn2_pre", 8),
                  ("ffn2_post", 8), ("ple_pre", 8), ("ple_post", 8), ("conv", 16), ("m_norm", 2), ("mu", 8),
                  ("w0", 2), ("a0", 2), ("k_k", 2), ("k_a", 2), ("r_k", 2), ("ln_w", 2), ("ln_b", 2),
                  ("sinks", 8), ("i_bias", 1), ("f_bias", 1)):
    VEC[_name] = _at
    _at += _n
NVEC = _at
VEC2 = {}
_at = 0
for _name, _n in (("norm1", 8), ("qa", 1), ("ka", 1), ("qb", 1), ("kb", 1), ("outa", 4), ("outb", 4), ("norm2", 8),
                  ("conv", 2 * 4 * KF)):
    VEC2[_name] = _at
    _at += _n
NVEC2 = _at

MATS = ("ident", "ones", "halves", "rope_turn", "swap", "axial_turn", "strict_low", "strict_up", "incl_up", "causal")


class Stage:

    def __init__(self, nc, name):
        self.nc, self.name, self.ctx, self.sems = nc, name, ExitStack(), []

    def __enter__(self):
        self.ctx.__enter__()
        return self

    def sb(self, name, shape, dt=F32):
        return self.ctx.enter_context(self.nc.sbuf_tensor(f"{self.name}_{name}", shape, dt))

    def sem(self, name):
        s = self.ctx.enter_context(self.nc.semaphore(f"{self.name}_{name}"))
        self.sems.append(s)
        return s

    def __exit__(self, *e):
        if e[0] is None:
            self.nc.all_engine_barrier()
            for s in self.sems:
                self.nc.gpsimd.sem_clear(s)
            self.nc.all_engine_barrier()
        return self.ctx.__exit__(*e)


class Chain:

    def __init__(self, eng, sem):
        self.eng, self.sem, self.n = eng, sem, 0

    def mark(self, ins):
        self.n += 1
        ins.then_inc(self.sem, 1)

    def wait(self):
        if self.n:
            self.eng.wait_ge(self.sem, self.n)

    def link(self, ins):
        self.mark(ins)
        self.wait()


class Chip:
    pass


POST_BANK = 7


class Spread:

    def __init__(self, st, c, name, sums, features, banks, diag=None):
        self.c, self.sums, self.features, self.banks = c, sums, features, banks
        G = len(banks)
        self.root, self.inv = st.sb(f"{name}_root", [P, NT, G]), st.sb(f"{name}_inv", [P, NT, G])
        self.diag = diag if diag is not None else st.sb(f"{name}_diag", [P, NT, P])
        self.rooted, self.inverted = st.sem(f"{name}_rooted"), st.sem(f"{name}_inverted")
        self.diag_ready, self.spread = st.sem(f"{name}_diag_ready"), st.sem(f"{name}_spread")

    def scalar(self, act, nc):
        nc.scalar.activation(self.root[:, :, :], self.sums, ACT.Sqrt, bias=self.c.eps[:, 0:1],
                             scale=1.0 / self.features).then_inc(self.rooted, 1)

    def vector(self, dve, nc):
        dve.wait_ge(self.rooted, 1)
        nc.vector.reciprocal(self.inv[:, :, :], self.root[:, :, :]).then_inc(self.inverted, 1)
        dve.wait_ge(self.inverted, 1)
        for g in range(len(self.banks)):
            if g:
                dve.wait_ge(self.spread, g)
            nc.vector.tensor_tensor(self.diag[:, :, :], self.c.mat["ident"].unsqueeze(1).to_broadcast([P, NT, P]),
                                    self.inv[:, :, g:g + 1].to_broadcast([P, NT, P]), ALU.mult).then_inc(self.diag_ready, 1)

    def tensor(self, pe, nc):
        for g, bank in enumerate(self.banks):
            pe.wait_ge(self.diag_ready, g + 1)
            nc.tensor.matmul(self.c.ps[:, bank, :], self.c.mat["ones"], self.diag[:, :, :], start=True,
                             stop=True).then_inc(self.spread, 1)


class Entry:

    def __init__(self, st, c, src, gain, groups, post):
        self.c, self.src, self.gain, self.groups, self.post = c, src, gain, groups, post
        self.hi, self.lo = st.sb("h_hi", [P, KD, S], F32R), st.sb("h_lo", [P, KD, S], F32R)
        self.hi_ready, self.lo_ready = st.sem("h_hi_ready"), st.sem("h_lo_ready")
        if post:
            self.post_factor = Spread(st, c, "post", c.ps[:, POST_BANK, 0:NT].unsqueeze(2), D, [POST_BANK])
            self.scaled, self.x_ready = st.sem("post_scaled"), st.sem("x_ready")
        if groups:
            self.sq = st.sb("sq", [P, 2, S])
            self.squared, self.summed, self.rs_ready = st.sem("squared"), st.sem("summed"), st.sem("rs_ready")
            G = len(groups)
            self.sum_banks = range(2 + G, 2 + G + NT)
            self.pre = Spread(st, c, "pre", c.ps[:, 2 + G:2 + G + NT, 0:G], P * len(groups[0]),
                              range(6, 6 + G), self.post_factor.diag if post else None)
            self.rs = st.sb("rs", [P, len(groups), S])

    def scalar_post(self, act, nc):
        if self.post:
            self.post_factor.scalar(act, nc)

    def scalar_tiles(self, act, nc):
        for k in range(KD):
            if self.post:
                act.wait_ge(self.x_ready, k + 1)
            if self.gain is None:
                nc.scalar.copy(self.hi[:, k, :], self.src[:, k, :]).then_inc(self.hi_ready, 1)
            else:
                nc.scalar.activation(self.hi[:, k, :], self.src[:, k, :], ACT.Copy,
                                     scale=self.gain[:, k:k + 1]).then_inc(self.hi_ready, 1)
            if self.groups:
                if k >= 2:
                    act.wait_ge(self.summed, k - 1)
                nc.scalar.activation(self.sq[:, k % 2, :], self.src[:, k, :], ACT.Square).then_inc(self.squared, 1)

    def scalar_root(self, act, nc):
        if self.groups:
            act.wait_ge(self.summed, KD)
            self.pre.scalar(act, nc)

    def scalar_factor(self, act, nc):
        for g in range(len(self.groups)):
            act.wait_ge(self.pre.spread, g + 1)
            nc.scalar.copy(self.rs[:, g, :], self.c.ps[:, self.pre.banks[g], :]).then_inc(self.rs_ready, 1)

    def vector_post(self, dve, nc):
        if self.post:
            self.post_factor.vector(dve, nc)
            dve.wait_ge(self.post_factor.spread, 1)

    def vector_step(self, dve, nc, i):
        c = self.c
        if self.post and i < KD:
            nc.vector.tensor_tensor(c.y[:, i, :], c.y[:, i, :], c.ps[:, POST_BANK, :], ALU.mult).then_inc(self.scaled, 1)
        k = i - 1
        if self.post and 0 <= k < KD:
            dve.wait_ge(self.scaled, k + 1)
            nc.vector.tensor_tensor(c.x[:, k, :], c.x[:, k, :], c.y[:, k, :], ALU.add).then_inc(self.x_ready, 1)
        k = i - 2
        if 0 <= k < KD:
            dve.wait_ge(self.hi_ready, k + 1)
            if self.post:
                dve.wait_ge(self.x_ready, k + 1)
            if self.gain is None:
                m = nc.vector.tensor_tensor(self.lo[:, k, :], self.src[:, k, :], self.hi[:, k, :].bitcast(F32), ALU.subtract)
            else:
                m = nc.vector.scalar_tensor_tensor(out=self.lo[:, k, :], in0=self.src[:, k, :], scalar=self.gain[:, k:k + 1],
                                                   in1=self.hi[:, k, :].bitcast(F32), op0=ALU.mult, op1=ALU.subtract)
            m.then_inc(self.lo_ready, 1)

    def vector_factor(self, dve, nc):
        if self.groups:
            self.pre.vector(dve, nc)

    def tensor_post(self, pe, nc):
        if self.post:
            self.post_factor.tensor(pe, nc)

    def tensor_sums(self, pe, nc, k):
        for g, ks in enumerate(self.groups):
            if k in ks:
                pe.wait_ge(self.squared, k + 1)
                for n, bank in enumerate(self.sum_banks):
                    m = nc.tensor.matmul(self.c.ps[:, bank, g:g + 1], self.sq[:, k % 2, n * P:(n + 1) * P],
                                         self.c.mats[:, MATS.index("ones"), 0:1], start=(k == ks[0]), stop=(k == ks[-1]))
                m.then_inc(self.summed, 1)

    def tensor_factor(self, pe, nc):
        if self.groups:
            self.pre.tensor(pe, nc)


class Exit:

    def __init__(self, st, c, gain, factor, sq=None):
        self.c, self.gain, self.factor = c, gain, factor
        self.sq = sq if sq is not None else st.sb("y_sq", [P, 2, S])
        self.total = st.sb("y_total", [P, S])
        self.y_squared, self.y_ready, self.added = st.sem("y_squared"), st.sem("y_ready"), st.sem("y_added")

    def scalar(self, act, nc, y, it, j):
        act.wait_ge(self.added, it + (j + 1))
        nc.scalar.activation(self.sq[:, j % 2, :], y, ACT.Square).then_inc(self.y_squared, 1)

    def vector_start(self, dve, nc):
        dve.sem_inc(self.added, 1)
        nc.vector.memset(self.total[:, :], 0.0).then_inc(self.added, 1)

    def vector(self, dve, nc, y, it, j, freed=None):
        dve.wait_ge(self.y_squared, it + (j + 1))
        m = nc.vector.tensor_scalar(self.c.y[:, it + j, :], y, self.gain(it + j), self.factor, ALU.mult, ALU.mult)
        m.then_inc(freed if freed is not None else self.y_ready, 1)
        dve.wait_ge(self.added, it + (j + 2))
        nc.vector.tensor_tensor(self.total[:, :], self.total[:, :], self.sq[:, j % 2, :], ALU.add).then_inc(self.added, 1)

    def tensor(self, pe, nc):
        pe.wait_ge(self.added, KD + 2)
        for n in range(NT):
            nc.tensor.matmul(self.c.ps[:, POST_BANK, n:n + 1], self.total[:, n * P:(n + 1) * P],
                             self.c.mats[:, MATS.index("ones"), 0:1], start=True, stop=True)


class Weights:

    def __init__(self, st):
        self.raw = st.sb("w_raw", [P, SLOTS, D])
        self.hi, self.lo = st.sb("w_hi", [P, 2, D], F32R), st.sb("w_lo", [P, 2, D], F32R)
        self.raw_ready = [st.sem(f"w_raw_ready{s}") for s in range(SLOTS)]
        self.hi_ready, self.lo_ready, self.done = st.sem("w_hi_ready"), st.sem("w_lo_ready"), st.sem("mm_done")

    def load(self, sp, it, n, src, width=D):
        s = n % SLOTS
        if n >= SLOTS:
            sp.wait_ge(self.lo_ready, it + (n - SLOTS + 1))
        sp.dma_start(self.raw[:, s, 0:width], src).then_inc(self.raw_ready[s], 16)

    def split_hi(self, act, nc, it, n, width=D):
        s = n % SLOTS
        act.wait_ge(self.raw_ready[s], it * (16 // SLOTS) + 16 * (n // SLOTS + 1))
        if n >= 2:
            act.wait_ge(self.done, it + (n - 1))
        nc.scalar.copy(self.hi[:, n % 2, 0:width], self.raw[:, s, 0:width]).then_inc(self.hi_ready, 1)

    def split_lo(self, dve, nc, it, n, width=D):
        s = n % SLOTS
        dve.wait_ge(self.hi_ready, it + (n + 1))
        nc.vector.tensor_tensor(self.lo[:, n % 2, 0:width], self.raw[:, s, 0:width],
                                self.hi[:, n % 2, 0:width].bitcast(F32), ALU.subtract).then_inc(self.lo_ready, 1)

    def terms(self, n, k, hi, lo):
        w = slice(k * P, (k + 1) * P)
        return ((self.hi[:, n % 2, w], hi), (self.hi[:, n % 2, w], lo), (self.lo[:, n % 2, w], hi))

    def multiply(self, nc, out, n, ks, hi, lo, k0=0, start=True, stop=True):
        for k in range(ks):
            for i, (w, h) in enumerate(self.terms(n, k, hi[:, k0 + k, :], lo[:, k0 + k, :])):
                m = nc.tensor.matmul(out, w, h, start=(start and k == 0 and i == 0), stop=(stop and k == ks - 1 and i == 2))
        return m


def first_products(pe, nc, c, W, entry, outs):
    entry.tensor_post(pe, nc)
    pe.wait_ge(W.lo_ready, 2)
    for k in range(KD):
        pe.wait_ge(entry.lo_ready, k + 1)
        for n in range(2):
            out, start, stop = outs[n](k)
            for i, (w, h) in enumerate(W.terms(n, k, entry.hi[:, k, :], entry.lo[:, k, :])):
                m = nc.tensor.matmul(out, w, h, start=(start and i == 0), stop=(stop and i == 2))
            if k == KD - 1:
                m.then_inc(W.done, 1)
        if k:
            entry.tensor_sums(pe, nc, k - 1)
    entry.tensor_sums(pe, nc, KD - 1)


def whole(c, bank):
    return lambda k: (c.ps[:, bank, :], k == 0, k == KD - 1)


def first_scalar(act, nc, W, entry):
    entry.scalar_post(act, nc)
    W.split_hi(act, nc, 0, 0)
    W.split_hi(act, nc, 0, 1)
    entry.scalar_tiles(act, nc)
    W.split_hi(act, nc, 0, 2)
    entry.scalar_root(act, nc)
    W.split_hi(act, nc, 0, 3)
    entry.scalar_factor(act, nc)


def first_vector(dve, nc, W, entry):
    entry.vector_post(dve, nc)
    for i in range(KD + 2):
        entry.vector_step(dve, nc, i)
        if i in (1, 2):
            W.split_lo(dve, nc, 0, i - 1)
    W.split_lo(dve, nc, 0, 2)
    entry.vector_factor(dve, nc)
    W.split_lo(dve, nc, 0, 3)
    if entry.groups:
        dve.wait_ge(entry.rs_ready, len(entry.groups))


ALL = [tuple(range(KD))]

PIECES = ((0, 6), (6, 6), (12, 5), (17, 5))
PIECE = 6 * P
UP = 2 * KF
LOOPS = (UP - SLOTS) // SLOTS


def load_ffn(sp, W, w_in, w_out):
    for n in range(SLOTS):
        W.load(sp, 0, n, w_in(n))
    with sp.Fori(0, LOOPS) as it:
        for n in range(SLOTS, 2 * SLOTS):
            W.load(sp, it * SLOTS, n, w_in(it * SLOTS + n))
    with sp.Fori(0, KD) as j:
        for i, (_, ks) in enumerate(PIECES):
            W.load(sp, j * SLOTS, UP + i, w_out(j * SLOTS + i)[:, 0:ks * P], ks * P)


def ffn_tensor(pe, nc, c, W, entry, a_hi, a_lo, act_ready, freed):
    first_products(pe, nc, c, W, entry, [whole(c, n) for n in range(2)])

    def tile(it, n):
        pe.wait_ge(W.lo_ready, it + (n + 1))
        if n >= SLOTS:
            pe.wait_ge(freed, it + (n - SLOTS + 1))
        W.multiply(nc, c.ps[:, n % SLOTS, :], n, KD, entry.hi, entry.lo).then_inc(W.done, 1)

    tile(0, 2)
    entry.tensor_factor(pe, nc)
    tile(0, 3)
    with pe.Fori(0, LOOPS) as it:
        for n in range(SLOTS, 2 * SLOTS):
            tile(it * SLOTS, n)
    with pe.Fori(0, KD // 2) as it:
        for b in range(2):
            pe.wait_ge(freed, it * 2 + (UP - 1 + b))
            for i, (k0, ks) in enumerate(PIECES):
                n = UP + SLOTS * b + i
                pe.wait_ge(W.lo_ready, it * (2 * SLOTS) + (n + 1))
                pe.wait_ge(act_ready, k0 + ks)
                W.multiply(nc, c.ps[:, b, :], n, ks, a_hi, a_lo, k0, start=(i == 0),
                           stop=(i == len(PIECES) - 1)).then_inc(W.done, 1)


def down_splits(eng, split, evacuate):
    def output(it, b, last):
        for i in range(1, SLOTS):
            split(it * SLOTS, UP + SLOTS * b + i, PIECES[i][1] * P)
        if not last:
            split(it * SLOTS, UP + SLOTS * (b + 1), PIECES[0][1] * P)
        evacuate(it, b, UP + SLOTS * b + SLOTS)

    with eng.Fori(0, KD // 2 - 1) as it:
        for b in range(2):
            output(it * 2, b, False)
    output(0, KD - 2, False)
    output(0, KD - 1, True)


def ffn_stage(nc, c, name, l, w_in, w_out, pre, post_at, from_post):
    with Stage(nc, name) as st:
        entry = Entry(st, c, c.x, pre, ALL, from_post)
        leave = Exit(st, c, lambda j: c.vec[:, bass.ds(j + post_at, 1)], 0.5, entry.sq)
        W = Weights(st)
        a_hi, a_lo = st.sb("a_hi", [P, KF, S], F32R), st.sb("a_lo", [P, KF, S], F32R)
        gate, up = c.y[:, 0:2, :], c.y[:, 2, :]
        freed = st.sem("banks_read")
        silu_ready = st.sem("silu_ready")
        product, act_hi, act_ready = st.sem("product"), st.sem("act_hi_ready"), st.sem("act_ready")
        with nc.Block() as block:
            @block.sync
            def _(sp):
                load_ffn(sp, W, lambda n: w_in[l, n], lambda n: w_out[l, n])

            @block.tensor
            def _(pe):
                ffn_tensor(pe, nc, c, W, entry, a_hi, a_lo, act_ready, freed)
                leave.tensor(pe, nc)

            @block.scalar
            def _(act):
                first_scalar(act, nc, W, entry)

                def silu(it, q):
                    act.wait_ge(freed, it * 2 + (2 * q + 1))
                    nc.scalar.activation(gate[:, q % 2, :], gate[:, q % 2, :], ACT.Silu).then_inc(silu_ready, 1)

                def first_part(it, q):
                    act.wait_ge(product, it + (q + 1))
                    nc.scalar.copy(a_hi[:, it + q, :], gate[:, q % 2, :]).then_inc(act_hi, 1)

                silu(0, 0)
                first_part(0, 0)
                W.split_hi(act, nc, 0, SLOTS)
                silu(0, 1)
                with act.Fori(0, LOOPS) as it:
                    for q in (1, 2):
                        W.split_hi(act, nc, it * SLOTS, 2 * q + 3)
                        first_part(it * 2, q)
                        W.split_hi(act, nc, it * SLOTS, 2 * q + 4)
                        silu(it * 2, q + 1)
                first_part(0, KF - 1)

                def squares(it, j, products):
                    act.wait_ge(W.done, it * SLOTS + products)
                    leave.scalar(act, nc, c.ps[:, j % 2, :], it, j)

                down_splits(act, lambda it, n, w: W.split_hi(act, nc, it, n, w), squares)

            @block.vector
            def _(dve):
                leave.vector_start(dve, nc)
                first_vector(dve, nc, W, entry)

                def scale_gate(it, q):
                    dve.wait_ge(W.done, it * 2 + (2 * q + 1))
                    nc.vector.tensor_tensor(gate[:, q % 2, :], c.ps[:, 2 * q % SLOTS, :], entry.rs[:, 0, :],
                                            ALU.mult).then_inc(freed, 1)

                def multiply(it, q):
                    dve.wait_ge(W.done, it * 2 + (2 * q + 2))
                    nc.vector.tensor_tensor(up, c.ps[:, (2 * q + 1) % SLOTS, :], entry.rs[:, 0, :],
                                            ALU.mult).then_inc(freed, 1)
                    dve.wait_ge(silu_ready, it + (q + 1))
                    dve.wait_ge(freed, it * 2 + (2 * q + 2))
                    nc.vector.tensor_tensor(gate[:, q % 2, :], gate[:, q % 2, :], up, ALU.mult).then_inc(product, 1)

                def rest(it, q):
                    dve.wait_ge(act_hi, it + (q + 1))
                    nc.vector.tensor_tensor(a_lo[:, it + q, :], gate[:, q % 2, :], a_hi[:, it + q, :].bitcast(F32),
                                            ALU.subtract).then_inc(act_ready, 1)

                scale_gate(0, 0)
                multiply(0, 0)
                W.split_lo(dve, nc, 0, SLOTS)
                scale_gate(0, 1)
                rest(0, 0)
                with dve.Fori(0, LOOPS) as it:
                    for q in (1, 2):
                        W.split_lo(dve, nc, it * SLOTS, 2 * q + 3)
                        multiply(it * 2, q)
                        W.split_lo(dve, nc, it * SLOTS, 2 * q + 4)
                        scale_gate(it * 2, q + 1)
                        rest(it * 2, q)
                multiply(0, KF - 1)
                rest(0, KF - 1)

                def outputs(it, j, products):
                    leave.vector(dve, nc, c.ps[:, j % 2, :], it, j, freed)

                down_splits(dve, lambda it, n, w: W.split_lo(dve, nc, it, n, w), outputs)


def eight_products(pe, nc, c, W, entry, freed):
    for n in range(2, KD):
        pe.wait_ge(W.lo_ready, n + 1)
        if n >= SLOTS:
            pe.wait_ge(freed, n - SLOTS + 1)
        W.multiply(nc, c.ps[:, n % SLOTS, :], n, KD, entry.hi, entry.lo).then_inc(W.done, 1)
        if n == 2:
            entry.tensor_factor(pe, nc)


def mix_out_stage(nc, c, l, w_out):
    with Stage(nc, "mixout") as st:
        entry = Entry(st, c, c.y, None, (), False)
        leave = Exit(st, c, lambda j: c.vec[:, VEC["mix_post"] + j:VEC["mix_post"] + j + 1], 1.0)
        W = Weights(st)
        freed = st.sem("banks_read")
        with nc.Block() as block:
            @block.sync
            def _(sp):
                for n in range(KD):
                    W.load(sp, 0, n, w_out[l, n])

            @block.tensor
            def _(pe):
                first_products(pe, nc, c, W, entry, [whole(c, n) for n in range(2)])
                eight_products(pe, nc, c, W, entry, freed)
                leave.tensor(pe, nc)

            @block.scalar
            def _(act):
                first_scalar(act, nc, W, entry)
                for j in range(KD):
                    if SLOTS <= j + 3 < KD:
                        W.split_hi(act, nc, 0, j + 3)
                    act.wait_ge(W.done, j + 1)
                    leave.scalar(act, nc, c.ps[:, j % SLOTS, :], 0, j)

            @block.vector
            def _(dve):
                leave.vector_start(dve, nc)
                first_vector(dve, nc, W, entry)
                for j in range(KD):
                    if SLOTS <= j + 3 < KD:
                        W.split_lo(dve, nc, 0, j + 3)
                    leave.vector(dve, nc, c.ps[:, j % SLOTS, :], 0, j, freed)


def ple_stage(nc, c, l, w_gate, w_proj, p_t):
    KP = PLE // P
    with Stage(nc, "ple") as st:
        entry = Entry(st, c, c.x, c.vec[:, VEC["ple_pre"]:], ALL, True)
        leave = Exit(st, c, lambda j: c.vec[:, VEC["ple_post"] + j:VEC["ple_post"] + j + 1], 1.0)
        W = Weights(st)
        proj_w, pt = st.sb("proj_w", [P, KD, KP * P]), st.sb("pt", [P, KP, S])
        wp_hi, wp_lo = st.sb("proj_w_hi", [P, KD, KP * P], F32R), st.sb("proj_w_lo", [P, KD, KP * P], F32R)
        p_hi, p_lo = st.sb("p_hi", [P, KP, S], F32R), st.sb("p_lo", [P, KP, S], F32R)
        gate, y = st.sb("gate", [P, 2, S]), st.sb("y", [P, 2, S])
        p_loaded, p_hi_ready, p_ready = st.sem("p_loaded"), st.sem("p_hi_ready"), st.sem("p_ready")
        freed, p_done, gate_ready, gated = st.sem("banks_read"), st.sem("p_done"), st.sem("gate_ready"), st.sem("gated")
        with nc.Block() as block:
            @block.sync
            def _(sp):
                W.load(sp, 0, 0, w_gate[l, 0])
                W.load(sp, 0, 1, w_gate[l, 1])
                sp.dma_start(proj_w[:, :, :], w_proj[l]).then_inc(p_loaded, 16)
                sp.dma_start(pt[:, :, :], p_t[l]).then_inc(p_loaded, 16)
                for n in range(2, KD):
                    W.load(sp, 0, n, w_gate[l, n])

            @block.tensor
            def _(pe):
                first_products(pe, nc, c, W, entry, [whole(c, n) for n in range(2)])
                pe.wait_ge(p_ready, 2)

                def from_p(j):
                    if j >= 2:
                        pe.wait_ge(gated, j - 1)
                    for k in range(KP):
                        w = slice(k * P, (k + 1) * P)
                        for i, (a, b) in enumerate(((wp_hi, p_hi), (wp_hi, p_lo), (wp_lo, p_hi))):
                            m = nc.tensor.matmul(c.ps[:, 4 + j % 2, :], a[:, j, w], b[:, k, :], start=(k == 0 and i == 0),
                                                 stop=(k == KP - 1 and i == 2))
                    m.then_inc(p_done, 1)

                for n in range(2, KD):
                    pe.wait_ge(W.lo_ready, n + 1)
                    if n >= SLOTS:
                        pe.wait_ge(freed, n - SLOTS + 1)
                    W.multiply(nc, c.ps[:, n % SLOTS, :], n, KD, entry.hi, entry.lo).then_inc(W.done, 1)
                    if n == 2:
                        entry.tensor_factor(pe, nc)
                        from_p(0)
                        from_p(1)
                    else:
                        from_p(n - 1)
                from_p(KD - 1)
                leave.tensor(pe, nc)

            @block.scalar
            def _(act):
                entry.scalar_post(act, nc)
                W.split_hi(act, nc, 0, 0)
                W.split_hi(act, nc, 0, 1)
                act.wait_ge(p_loaded, 32)
                nc.scalar.copy(wp_hi[:, :, :], proj_w[:, :, :]).then_inc(p_hi_ready, 1)
                nc.scalar.copy(p_hi[:, :, :], pt[:, :, :]).then_inc(p_hi_ready, 1)
                entry.scalar_tiles(act, nc)
                W.split_hi(act, nc, 0, 2)
                entry.scalar_root(act, nc)
                W.split_hi(act, nc, 0, 3)
                entry.scalar_factor(act, nc)

                def squares(j):
                    act.wait_ge(gated, j + 1)
                    leave.scalar(act, nc, y[:, j % 2, :], 0, j)

                for j in range(KD):
                    if SLOTS <= j + 3 < KD:
                        W.split_hi(act, nc, 0, j + 3)
                    act.wait_ge(freed, j + 1)
                    nc.scalar.activation(gate[:, j % 2, :], gate[:, j % 2, :], ACT.Sigmoid).then_inc(gate_ready, 1)
                    if j:
                        squares(j - 1)
                squares(KD - 1)

            @block.vector
            def _(dve):
                leave.vector_start(dve, nc)
                entry.vector_post(dve, nc)
                for i in range(KD + 2):
                    entry.vector_step(dve, nc, i)
                    if i in (1, 2):
                        W.split_lo(dve, nc, 0, i - 1)
                W.split_lo(dve, nc, 0, 2)
                dve.wait_ge(p_hi_ready, 2)
                nc.vector.tensor_tensor(wp_lo[:, :, :], proj_w[:, :, :], wp_hi[:, :, :].bitcast(F32),
                                        ALU.subtract).then_inc(p_ready, 1)
                nc.vector.tensor_tensor(p_lo[:, :, :], pt[:, :, :], p_hi[:, :, :].bitcast(F32),
                                        ALU.subtract).then_inc(p_ready, 1)
                entry.vector_factor(dve, nc)
                W.split_lo(dve, nc, 0, 3)
                dve.wait_ge(entry.rs_ready, 1)

                def gated_product(j):
                    dve.wait_ge(gate_ready, j + 1)
                    dve.wait_ge(p_done, j + 1)
                    nc.vector.tensor_tensor(y[:, j % 2, :], gate[:, j % 2, :], c.ps[:, 4 + j % 2, :],
                                            ALU.mult).then_inc(gated, 1)
                    leave.vector(dve, nc, y[:, j % 2, :], 0, j)

                for j in range(KD):
                    if SLOTS <= j + 3 < KD:
                        W.split_lo(dve, nc, 0, j + 3)
                    dve.wait_ge(W.done, j + 1)
                    nc.vector.tensor_tensor(gate[:, j % 2, :], c.ps[:, j % SLOTS, :], entry.rs[:, 0, :],
                                            ALU.mult).then_inc(freed, 1)
                    if j:
                        gated_product(j - 1)
                gated_product(KD - 1)


def rope_stage(nc, c, positions, inv_freq):
    MAGIC = 1.5 * 2.0 ** 23
    C1 = 6.28125
    C2 = round((TWO_PI - C1) * 2 ** 20) / 2 ** 20
    C3 = float(TWO_PI - C1 - C2)
    EDGE = 3.1415925
    with Stage(nc, "rope") as st:
        pos_i, pos = st.sb("pos_i", [P, S], I32), st.sb("pos", [P, S])
        ang, turns, freq = st.sb("ang", [P, S]), st.sb("turns", [P, S]), st.sb("freq", [P, 1])
        half_pi = st.sb("half_pi", [P, 1])
        loaded, reduced, sines = st.sem("loaded"), st.sem("reduced"), st.sem("sines")
        chain_s = st.sem("dve_chain")
        with nc.Block() as block:
            @block.sync
            def _(sp):
                sp.dma_start(pos_i[:, :], positions).then_inc(loaded, 16)
                sp.dma_start(freq[:, :], inv_freq).then_inc(loaded, 16)

            @block.vector
            def _(dve):
                ch = Chain(dve, chain_s)
                ch.mark(nc.vector.memset(half_pi[:, :], float(np.pi / 2)))
                dve.wait_ge(loaded, 32)
                ch.link(nc.vector.tensor_copy(pos[:, :], pos_i[:, :]))
                ch.link(nc.vector.tensor_scalar(ang[:, :], pos[:, :], freq[:, 0:1], None, ALU.mult))
                ch.link(nc.vector.tensor_scalar(turns[:, :], ang[:, :], 1.0 / TWO_PI, MAGIC, ALU.mult, ALU.add))
                ch.link(nc.vector.tensor_scalar(turns[:, :], turns[:, :], MAGIC, None, ALU.subtract))
                for part in (C1, C2, C3):
                    ch.link(nc.vector.scalar_tensor_tensor(out=ang[:, :], in0=turns[:, :], scalar=-part,
                                                           in1=ang[:, :], op0=ALU.mult, op1=ALU.add))
                nc.vector.tensor_scalar(ang[:, :], ang[:, :], EDGE, -EDGE, ALU.min, ALU.max).then_inc(reduced, 1)

            @block.scalar
            def _(act):
                act.wait_ge(reduced, 1)
                nc.scalar.activation(c.rope[:, 1, :], ang[:, :], ACT.Sin).then_inc(sines, 1)
                nc.scalar.activation(pos[:, :], ang[:, :], ACT.Abs).then_inc(sines, 1)
                act.wait_ge(sines, 2)
                nc.scalar.activation(c.rope[:, 0, :], pos[:, :], ACT.Sin, bias=half_pi[:, 0:1],
                                     scale=-1.0).then_inc(sines, 1)


R_T, K_T, V_T, WA_T, G_T, AQ_T, AK_T, AV_T, MQ_T, MV_T, MO_T = 0, 2, 4, 6, 7, 8, 12, 13, 14, 18, 20


def proj_stage(nc, c, name, w_in, tiles, gain, gates):
    total = tiles + (1 if gates else 0)
    loops = (total - SLOTS) // SLOTS
    tail = range(SLOTS * (loops + 1), total)
    with Stage(nc, name) as st:
        entry = Entry(st, c, c.x, gain, ALL, True)
        W = Weights(st)
        freed = st.sem("banks_read")
        with nc.Block() as block:
            @block.sync
            def _(sp):
                for n in range(SLOTS):
                    W.load(sp, 0, n, w_in(n))
                with sp.Fori(0, loops) as it:
                    for n in range(SLOTS, 2 * SLOTS):
                        W.load(sp, it * SLOTS, n, w_in(it * SLOTS + n))
                for n in tail:
                    W.load(sp, 0, n, w_in(n))

            @block.tensor
            def _(pe):
                first_products(pe, nc, c, W, entry, [whole(c, n) for n in range(2)])

                def tile(it, n):
                    pe.wait_ge(W.lo_ready, it + (n + 1))
                    if n >= SLOTS:
                        pe.wait_ge(freed, it + (n - SLOTS + 1))
                    W.multiply(nc, c.ps[:, n % SLOTS, :], n, KD, entry.hi, entry.lo).then_inc(W.done, 1)

                tile(0, 2)
                entry.tensor_factor(pe, nc)
                tile(0, 3)
                with pe.Fori(0, loops) as it:
                    for n in range(SLOTS, 2 * SLOTS):
                        tile(it * SLOTS, n)
                for n in tail:
                    tile(0, n)

            @block.scalar
            def _(act):
                first_scalar(act, nc, W, entry)
                with act.Fori(0, loops) as it:
                    for n in range(SLOTS, 2 * SLOTS):
                        W.split_hi(act, nc, it * SLOTS, n)
                for n in tail:
                    W.split_hi(act, nc, 0, n)

            @block.vector
            def _(dve):
                first_vector(dve, nc, W, entry)

                def store(it, n):
                    dve.wait_ge(W.done, it + (n + 1))
                    b = n % SLOTS
                    if gates and isinstance(it, int) and it + n == tiles:
                        for g in range(2):
                            rows = slice(32 * g, 32 * g + 4)
                            nc.vector.tensor_tensor(c.gates[0:4, g, :], c.ps[rows, b, :], entry.rs[rows, 0, :],
                                                    ALU.mult).then_inc(freed, 1)
                    else:
                        nc.vector.tensor_tensor(c.proj[:, it + n, :], c.ps[:, b, :], entry.rs[:, 0, :],
                                                ALU.mult).then_inc(freed, 1)

                for n in range(2):
                    store(0, n)
                with dve.Fori(0, loops) as it:
                    for n in range(SLOTS, 2 * SLOTS):
                        W.split_lo(dve, nc, it * SLOTS, n)
                        store(it * SLOTS, n - 2)
                for n in tail:
                    W.split_lo(dve, nc, 0, n)
                    store(0, n - 2)
                for n in (total - 2, total - 1):
                    store(0, n)


HEADS, GROUP, WIN = 8, 4, 128


def window_attention_stage(nc, c, window_mask):
    with Stage(nc, "attn") as st:
        q_rot = st.sb("q_rot", [P, 4, S])
        keys = st.sb("keys", [P, 2, WIN + S])
        turned_sin = st.sb("turned_sin", [P, 5, S])
        v_tok = st.sb("v_tok", [P, NT, P])
        mask = st.sb("mask", [P, 2, S])
        masked = st.sb("masked", [P, 2, 4, 2 * WIN])
        probs = st.sb("probs", [P, 2, 4, 2 * WIN])
        probs_t = st.sb("probs_t", [P, 2, 2, S])
        row_max, neg_max = st.sb("row_max", [P, HEADS, 4]), st.sb("neg_max", [P, HEADS, 4])
        row_sum, sink_exp = st.sb("row_sum", [P, HEADS, 4]), st.sb("sink_exp", [P, HEADS, 4])
        loaded, turned, v_turned, v_copied = st.sem("loaded"), st.sem("turned"), st.sem("v_turned"), st.sem("v_copied")
        roped, swapped, swap_copied = st.sem("roped"), st.sem("swapped"), st.sem("swap_copied")
        scored, scores_read, max_ready = st.sem("scored"), st.sem("scores_read"), st.sem("max_ready")
        exps, normed, transposed = st.sem("exps"), st.sem("normed"), st.sem("transposed")
        pt_copied, pv_done, out_copied = st.sem("pt_copied"), st.sem("pv_done"), st.sem("out_copied")
        chain_s = st.sem("dve_chain")
        with nc.Block() as block:
            @block.sync
            def _(sp):
                sp.dma_start(mask[:, :, :], window_mask).then_inc(loaded, 16)

            @block.tensor
            def _(pe):
                for t in range(5):
                    nc.tensor.matmul(c.ps[:, t, :], c.mat["rope_turn"], c.proj[:, AQ_T + t, :],
                                     start=True, stop=True).then_inc(turned, 1)
                for n in range(NT):
                    m = nc.tensor.transpose(c.ps[:, 5, n * P:(n + 1) * P], c.proj[:, AV_T, n * P:(n + 1) * P],
                                            c.mat["ident"])
                m.then_inc(v_turned, 1)
                pe.wait_ge(roped, 5)
                nc.tensor.matmul(c.ps[:, 6, :], c.mat["swap"], keys[:, 0, WIN:WIN + S],
                                 start=True, stop=True).then_inc(swapped, 1)
                pe.wait_ge(v_copied, 1)
                pe.wait_ge(swap_copied, 1)

                def scores(h):
                    q, p0 = h % 2, DH * (h % 2)
                    variant = 0 if h // GROUP == h % 2 else 1
                    if h >= 2:
                        pe.wait_ge(scores_read, 2 * (h - 1))
                    for n in range(NT):
                        m = nc.tensor.matmul(c.ps[:, 2 * q + n // 2, (n % 2) * 2 * WIN:(n % 2 + 1) * 2 * WIN],
                                             q_rot[p0:p0 + DH, h // 2, n * P:(n + 1) * P],
                                             keys[p0:p0 + DH, variant, n * P:n * P + 2 * WIN], start=True, stop=True)
                    m.then_inc(scored, 1)

                def turn_probs(h):
                    pe.wait_ge(normed, 4 * (h + 1))
                    if h >= 1:
                        pe.wait_ge(pt_copied, 2 * h)
                    for n in range(NT):
                        for half in range(2):
                            if n or half:
                                m = nc.tensor.transpose(c.ps[:, 4 + half, n * P:(n + 1) * P],
                                                        probs[:, h % 2, n, half * WIN:(half + 1) * WIN],
                                                        c.mat["ident"])
                    m.then_inc(transposed, 1)

                def values(h):
                    t, p0, v0 = h // 2, DH * (h % 2), DH * (h // GROUP)
                    pe.wait_ge(pt_copied, 2 * (h + 1))
                    if h % 2 == 0 and t >= 2:
                        pe.wait_ge(out_copied, t - 1)
                    for n in range(NT):
                        o = c.ps[p0:p0 + DH, 6 + t % 2, n * P:(n + 1) * P]
                        m = nc.tensor.matmul(o, v_tok[:, n, v0:v0 + DH], probs_t[:, h % 2, 1, n * P:(n + 1) * P],
                                             start=True, stop=(n == 0))
                        if n:
                            m = nc.tensor.matmul(o, v_tok[:, n - 1, v0:v0 + DH],
                                                 probs_t[:, h % 2, 0, n * P:(n + 1) * P], start=False, stop=True)
                    m.then_inc(pv_done, 1)

                for h in range(HEADS + 1):
                    if h < HEADS:
                        scores(h)
                    if h >= 1:
                        turn_probs(h - 1)
                        values(h - 1)

            @block.scalar
            def _(act):
                act.wait_ge(v_turned, 1)
                nc.scalar.copy(v_tok[:, :, :], c.ps[:, 5, :]).then_inc(v_copied, 1)
                act.wait_ge(swapped, 1)
                nc.scalar.copy(keys[:, 1, WIN:WIN + S], c.ps[:, 6, :]).then_inc(swap_copied, 1)

                def exponents(h):
                    act.wait_ge(max_ready, h + 1)
                    if h >= 2:
                        act.wait_ge(transposed, h - 1)
                    for n in range(NT):
                        nc.scalar.activation(probs[:, h % 2, n, :], masked[:, h % 2, n, :], ACT.Exp,
                                             bias=neg_max[:, h, n:n + 1],
                                             accum_out=row_sum[:, h, n:n + 1]).then_inc(exps, 1)
                    nc.scalar.activation(sink_exp[:, h, :], neg_max[:, h, :], ACT.Exp,
                                         bias=c.vec[:, VEC["sinks"] + h:VEC["sinks"] + h + 1]).then_inc(exps, 1)

                def copy_turned(h):
                    act.wait_ge(transposed, h + 1)
                    if h >= 2:
                        act.wait_ge(pv_done, h - 1)
                    nc.scalar.copy(probs_t[:, h % 2, 0, WIN:S], c.ps[:, 4, WIN:S]).then_inc(pt_copied, 1)
                    nc.scalar.copy(probs_t[:, h % 2, 1, :], c.ps[:, 5, :]).then_inc(pt_copied, 1)

                for h in range(HEADS + 1):
                    if h < HEADS:
                        exponents(h)
                    if h >= 1:
                        copy_turned(h - 1)

            @block.vector
            def _(dve):
                ch = Chain(dve, chain_s)
                for v in range(2):
                    ch.mark(nc.vector.memset(keys[:, v, 0:WIN], 0.0))
                for t in range(5):
                    dst = q_rot[:, t, :] if t < 4 else keys[:, 0, WIN:WIN + S]
                    ch.mark(nc.vector.tensor_tensor(dst, c.proj[:, AQ_T + t, :], c.rope[:, 0, :], ALU.mult))
                    dve.wait_ge(turned, t + 1)
                    ch.link(nc.vector.tensor_tensor(turned_sin[:, t, :], c.ps[:, t, :], c.rope[:, 1, :], ALU.mult))
                    nc.vector.tensor_tensor(dst, dst, turned_sin[:, t, :], ALU.add).then_inc(roped, 1)
                dve.wait_ge(roped, 5)
                dve.wait_ge(loaded, 16)

                def maxima(h):
                    dve.wait_ge(scored, h + 1)
                    if h >= 2:
                        dve.wait_ge(exps, 5 * (h - 1))
                    for b in range(2):
                        nc.vector.scalar_tensor_tensor(
                            out=masked[:, h % 2, 2 * b:2 * b + 2, :], in0=c.ps[:, 2 * (h % 2) + b, :],
                            scalar=DH ** -0.5, in1=mask[:, b, :], op0=ALU.mult, op1=ALU.add).then_inc(scores_read, 1)
                    dve.wait_ge(scores_read, 2 * (h + 1))
                    ch.link(nc.vector.tensor_reduce(row_max[:, h, :], masked[:, h % 2, :, :], AX, ALU.max))
                    nc.vector.tensor_scalar(neg_max[:, h, :], row_max[:, h, :],
                                            c.vec[:, VEC["sinks"] + h:VEC["sinks"] + h + 1], -1.0,
                                            ALU.max, ALU.mult).then_inc(max_ready, 1)

                def normalise(h):
                    dve.wait_ge(exps, 5 * (h + 1))
                    ch.link(nc.vector.tensor_tensor(row_sum[:, h, :], row_sum[:, h, :], sink_exp[:, h, :], ALU.add))
                    ch.link(nc.vector.reciprocal(row_sum[:, h, :], row_sum[:, h, :]))
                    for n in range(NT):
                        nc.vector.tensor_scalar(probs[:, h % 2, n, :], probs[:, h % 2, n, :], row_sum[:, h, n:n + 1],
                                                None, ALU.mult).then_inc(normed, 1)

                def copy_out(t):
                    dve.wait_ge(pv_done, 2 * (t + 1))
                    nc.vector.tensor_copy(c.y[:, t, :], c.ps[:, 6 + t % 2, :]).then_inc(out_copied, 1)

                for h in range(HEADS + 1):
                    if h < HEADS:
                        maxima(h)
                    if h >= 1:
                        normalise(h - 1)
                    if h >= 3 and h % 2 == 1:
                        copy_out((h - 3) // 2)
                copy_out(HEADS // 2 - 1)


M_HEADS, CAP = 4, 15.0


def mlstm_stage(nc, c, selectors):
    with Stage(nc, "mlstm") as st:
        qk = st.sb("qk", [P, 4, S])
        g_tanh, soft = st.sb("g_tanh", [4, 2, S]), st.sb("soft", [4, S])
        neg_g, u, run_max = st.sb("neg_g", [4, S]), st.sb("u", [4, S]), st.sb("run_max", [4, S])
        floor, zeros = st.sb("floor", [4, S]), st.sb("zeros", [4, S])
        select = st.sb("select", [4, 6, P])
        u_col = st.sb("u_col", [P, NT, M_HEADS])
        max_all = st.sb("max_all", [P, M_HEADS, S])
        floor_all = st.sb("floor_all", [P, 2, S])
        v_tok = st.sb("v_tok", [P, NT, 2 * P])
        below, weight, weighted_s = st.sb("below", [P, 2, S]), st.sb("weight", [P, 2, S]), st.sb("weighted", [P, 2, S])
        den, hid, sq = st.sb("den", [P, 2, S]), st.sb("hid", [P, 2, S]), st.sb("sq", [P, 2, S])
        o_gate = st.sb("o_gate", [P, 2, S])
        loaded, conv_done, qk_ready = st.sem("loaded"), st.sem("conv_done"), st.sem("qk_ready")
        biased, tanhed, exped, softened = st.sem("biased"), st.sem("tanhed"), st.sem("exped"), st.sem("softened")
        u_ready, max_ready, low_ready, floored = st.sem("u_ready"), st.sem("max_ready"), st.sem("low_ready"), st.sem("floored")
        made, copied = st.sem("made"), st.sem("copied")
        s_done, below_ready, w_ready = st.sem("s_done"), st.sem("below_ready"), st.sem("w_ready")
        weighted, nd_done = st.sem("weighted_ready"), st.sem("nd_done")
        den_abs, hid_ready, squared = st.sem("den_abs"), st.sem("hid_ready"), st.sem("squared")
        summed, rooted, o_ready = st.sem("summed"), st.sem("rooted"), st.sem("o_ready")
        chain_s = st.sem("dve_chain")
        ITEMS = [(h, s) for h in range(M_HEADS) for s in range(NT)]
        with nc.Block() as block:
            @block.sync
            def _(sp):
                sp.dma_start(select[:, :, :], selectors).then_inc(loaded, 16)

            @block.tensor
            def _(pe):
                for half in range(2):
                    for n in range(2):
                        for j in range(2):
                            m = nc.tensor.transpose(c.ps[:, 5 + half, (2 * n + j) * P:(2 * n + j + 1) * P],
                                                    c.proj[:, MV_T + j, (2 * half + n) * P:(2 * half + n + 1) * P],
                                                    c.mat["ident"])
                    m.then_inc(made, 1)
                pe.wait_ge(loaded, 16)
                pe.wait_ge(u_ready, 1)
                for n in range(NT):
                    m = nc.tensor.matmul(c.ps[:, 0, n * M_HEADS:(n + 1) * M_HEADS], u[:, n * P:(n + 1) * P],
                                         c.mats[0:4, MATS.index("ident"), 0:4], start=True, stop=True)
                m.then_inc(made, 1)
                pe.wait_ge(max_ready, 1)
                for h in range(M_HEADS):
                    nc.tensor.matmul(c.ps[:, 1 + h, :], select[:, h, :], run_max[:, :],
                                     start=True, stop=True).then_inc(made, 1)
                pe.wait_ge(floored, 1)
                nc.tensor.matmul(c.ps[:, 7, :], select[:, 4, :], floor[:, :], start=True, stop=True).then_inc(made, 1)
                pe.wait_ge(copied, 1)
                nc.tensor.matmul(c.ps[:, 5, :], select[:, 5, :], floor[:, :], start=True, stop=True).then_inc(made, 1)
                pe.wait_ge(qk_ready, 4)
                pe.wait_ge(copied, 9)

                def scores(i):
                    h, s = ITEMS[i]
                    p0 = DH * (h % 2)
                    if i >= 2:
                        pe.wait_ge(weighted, i - 1)
                    nc.tensor.matmul(c.ps[:, i % 2, 0:S - s * P], qk[p0:p0 + DH, 2 + h // 2, s * P:(s + 1) * P],
                                     qk[p0:p0 + DH, h // 2, s * P:S], start=True, stop=True).then_inc(s_done, 1)

                def sums(i):
                    h, s = ITEMS[i]
                    p0, j = DH * (h % 2), h // 2
                    pe.wait_ge(weighted, i + 1)
                    rhs = weighted_s[:, i % 2, 0:S - s * P]
                    nc.tensor.matmul(c.ps[p0:p0 + DH, 2 + j, s * P:S], v_tok[:, s, h * DH:(h + 1) * DH], rhs,
                                     start=(s == 0), stop=(s == NT - 1))
                    nc.tensor.matmul(c.ps[p0:p0 + DH, 4 + j, s * P:S], c.mats[:, MATS.index("ones"), 0:DH], rhs,
                                     start=(s == 0), stop=(s == NT - 1)).then_inc(nd_done, 1)

                for i in range(len(ITEMS) + 1):
                    if i < len(ITEMS):
                        scores(i)
                    if i >= 1:
                        sums(i - 1)
                for j in range(2):
                    pe.wait_ge(squared, j + 1)
                    nc.tensor.matmul(c.ps[:, 6 + j, :], c.mat["halves"], sq[:, j, :], start=True,
                                     stop=True).then_inc(summed, 1)

            @block.scalar
            def _(act):
                act.wait_ge(biased, 2)
                nc.scalar.activation(g_tanh[:, :, :], c.gates[0:4, :, :], ACT.Tanh, scale=1.0 / CAP).then_inc(tanhed, 1)
                act.wait_ge(tanhed, 1)
                nc.scalar.activation(soft[:, :], g_tanh[:, 1, :], ACT.Exp, scale=-CAP).then_inc(exped, 1)
                act.wait_ge(exped, 1)
                nc.scalar.activation(soft[:, :], soft[:, :], ACT.Ln, bias=1.0).then_inc(softened, 1)
                for t in range(4):
                    act.wait_ge(conv_done, t + 1)
                    nc.scalar.activation(qk[:, t, :], qk[:, t, :], ACT.Silu).then_inc(qk_ready, 1)
                act.wait_ge(made, 1)
                nc.scalar.copy(v_tok[:, 0:2, :], c.ps[:, 5, :]).then_inc(copied, 1)
                act.wait_ge(made, 2)
                nc.scalar.copy(v_tok[:, 2:4, :], c.ps[:, 6, :]).then_inc(copied, 1)
                act.wait_ge(made, 3)
                nc.scalar.copy(u_col[:, :, :], c.ps[:, 0, 0:NT * M_HEADS]).then_inc(copied, 1)
                for h in range(M_HEADS):
                    act.wait_ge(made, 4 + h)
                    nc.scalar.copy(max_all[:, h, :], c.ps[:, 1 + h, :]).then_inc(copied, 1)
                act.wait_ge(low_ready, 1)
                nc.scalar.activation(floor[:, :], floor[:, :], ACT.Exp).then_inc(floored, 1)
                act.wait_ge(made, 8)
                nc.scalar.copy(floor_all[:, 0, :], c.ps[:, 7, :]).then_inc(copied, 1)
                act.wait_ge(made, 9)
                nc.scalar.copy(floor_all[:, 1, :], c.ps[:, 5, :]).then_inc(copied, 1)
                for i, (h, s) in enumerate(ITEMS):
                    act.wait_ge(below_ready, i + 1)
                    if i >= 2:
                        act.wait_ge(weighted, i - 1)
                    nc.scalar.activation(weight[:, i % 2, 0:S - s * P], below[:, i % 2, 0:S - s * P], ACT.Exp,
                                         scale=-1.0).then_inc(w_ready, 1)
                act.wait_ge(nd_done, len(ITEMS))
                for j in range(2):
                    nc.scalar.activation(den[:, j, :], c.ps[:, 4 + j, :], ACT.Abs).then_inc(den_abs, 1)
                for j in range(2):
                    nc.scalar.activation(o_gate[:, j, :], c.proj[:, MO_T + j, :], ACT.Sigmoid).then_inc(o_ready, 1)
                for j in range(2):
                    act.wait_ge(hid_ready, j + 1)
                    nc.scalar.activation(sq[:, j, :], hid[:, j, :], ACT.Square).then_inc(squared, 1)
                for j in range(2):
                    act.wait_ge(summed, j + 1)
                    nc.scalar.activation(den[:, j, :], c.ps[:, 6 + j, :], ACT.Sqrt, bias=c.eps[:, 0:1],
                                         scale=1.0 / DH).then_inc(rooted, 1)

            @block.vector
            def _(dve):
                ch = Chain(dve, chain_s)
                for g, name in ((0, "i_bias"), (1, "f_bias")):
                    nc.vector.tensor_scalar(c.gates[0:4, g, :], c.gates[0:4, g, :], c.vec[0:4, VEC[name]:VEC[name] + 1],
                                            None, ALU.add).then_inc(biased, 1)
                ch.mark(nc.vector.memset(zeros[:, :], 0.0))
                tap = lambda n, t: c.vec[:, VEC["conv"] + 4 * n + t:VEC["conv"] + 4 * n + t + 1]
                for t in range(4):
                    ch.mark(nc.vector.tensor_scalar(qk[:, t, :], c.proj[:, MQ_T + t, :], tap(3, t), None, ALU.mult))
                for back in range(1, 4):
                    ch.wait()
                    for t in range(4):
                        ins = nc.vector.scalar_tensor_tensor(
                            out=qk[:, t, back:S], in0=c.proj[:, MQ_T + t, 0:S - back], scalar=tap(3 - back, t),
                            in1=qk[:, t, back:S], op0=ALU.mult, op1=ALU.add)
                        if back == 3:
                            ins.then_inc(conv_done, 1)
                        else:
                            ch.mark(ins)
                dve.wait_ge(softened, 1)
                ch.link(nc.vector.tensor_tensor_scan(neg_g[:, :], soft[:, :], zeros[:, :], 0.0, ALU.add, ALU.add))
                nc.vector.scalar_tensor_tensor(out=u[:, :], in0=g_tanh[:, 0, :], scalar=CAP, in1=neg_g[:, :],
                                               op0=ALU.mult, op1=ALU.add).then_inc(u_ready, 1)
                dve.wait_ge(u_ready, 1)
                nc.vector.tensor_tensor_scan(run_max[:, :], u[:, :], u[:, :], NEG, ALU.max,
                                             ALU.max).then_inc(max_ready, 1)
                dve.wait_ge(max_ready, 1)
                nc.vector.tensor_tensor(floor[:, :], neg_g[:, :], run_max[:, :], ALU.subtract).then_inc(low_ready, 1)
                dve.wait_ge(copied, 9)

                def exponent(i):
                    h, s = ITEMS[i]
                    if i >= 2:
                        dve.wait_ge(w_ready, i - 1)
                    col = u_col[:, s, h:h + 1]
                    nc.vector.tensor_scalar(below[:, i % 2, 0:S - s * P], max_all[:, h, s * P:S], col, col,
                                            ALU.max, ALU.subtract).then_inc(below_ready, 1)

                exponent(0)
                for i, (h, s) in enumerate(ITEMS):
                    if i + 1 < len(ITEMS):
                        exponent(i + 1)
                    dve.wait_ge(w_ready, i + 1)
                    ch.link(nc.vector.tensor_tensor(weight[:, i % 2, 0:P], weight[:, i % 2, 0:P], c.mat["causal"],
                                                    ALU.mult))
                    dve.wait_ge(s_done, i + 1)
                    if i >= 2:
                        dve.wait_ge(nd_done, i - 1)
                    nc.vector.scalar_tensor_tensor(out=weighted_s[:, i % 2, 0:S - s * P],
                                                   in0=c.ps[:, i % 2, 0:S - s * P], scalar=DH ** -0.5,
                                                   in1=weight[:, i % 2, 0:S - s * P], op0=ALU.mult,
                                                   op1=ALU.mult).then_inc(weighted, 1)
                for j in range(2):
                    dve.wait_ge(den_abs, j + 1)
                    ch.link(nc.vector.tensor_tensor(den[:, j, :], den[:, j, :], floor_all[:, j, :], ALU.max))
                    ch.link(nc.vector.reciprocal(den[:, j, :], den[:, j, :]))
                    nc.vector.tensor_tensor(hid[:, j, :], c.ps[:, 2 + j, :], den[:, j, :], ALU.mult).then_inc(hid_ready, 1)
                dve.wait_ge(hid_ready, 2)
                dve.wait_ge(o_ready, 2)
                for j in range(2):
                    dve.wait_ge(rooted, j + 1)
                    ch.link(nc.vector.reciprocal(den[:, j, :], den[:, j, :]))
                    ch.link(nc.vector.scalar_tensor_tensor(
                        out=hid[:, j, :], in0=hid[:, j, :], scalar=c.vec[:, VEC["m_norm"] + j:VEC["m_norm"] + j + 1],
                        in1=den[:, j, :], op0=ALU.mult, op1=ALU.mult))
                    ch.link(nc.vector.tensor_tensor(c.y[:, 4 + j, :], hid[:, j, :], o_gate[:, j, :], ALU.mult))


R_HEADS = 4
QA, QB, QK, QV = range(4)


def rwkv_stage(nc, c, l, loras, chunk_masks, reset):
    with Stage(nc, "rwkv") as st:
        mix = st.sb("mix", [P, KD, S])
        w_up, g_up = st.sb("w_up", [P, 2 * P]), st.sb("g_up", [P, 2 * P])
        masks = st.sb("masks", [P, 3, 4 * P])
        reset_t = st.sb("reset", [P, S])
        cum_prev, decay_prev, f_a, f_b, f_k, f_r, lora = (c.proj[:, AQ_T + 2 * i:AQ_T + 2 * i + 2, :] for i in range(7))
        sig_w, rate, gate = st.sb("sig_w", [P, 2, S]), st.sb("rate", [P, 2, S]), st.sb("gate", [P, 2, S])
        cum, decay, grow = st.sb("cum", [P, 2, S]), st.sb("decay", [P, 2, S]), st.sb("grow", [P, 2, S])
        kk, sq = st.sb("kk", [P, 2, S]), st.sb("sq", [P, 2, S])
        tok = st.sb("tok", [P, 4, 2 * P])
        N, NT_, akT, rbT, rkT = (st.sb(n, [P, R_HEADS, P]) for n in ("n", "n_t", "ak_t", "rb_t", "rk_t"))
        X = st.sb("x", [P, R_HEADS, P])
        r_prime, y = st.sb("r_prime", [P, 2, S]), st.sb("y", [P, 2, S])
        GH = st.sb("gh", [P, NCH, 2, P])
        state, carried = st.sb("state", [P, NCH + 1, 2, DH]), st.sb("carried", [P, 2, DH])
        loaded, mixed, lora_in, lora_out = st.sem("loaded"), st.sem("mixed"), st.sem("lora_in"), st.sem("lora_out")
        lora_done, cum_ready, decayed = st.sem("lora_done"), st.sem("cum_ready"), st.sem("decayed")
        kk_raw, kk_squared, kk_summed = st.sem("kk_raw"), st.sem("kk_squared"), st.sem("kk_summed")
        kk_floor, kk_root, factors = st.sem("kk_floor"), st.sem("kk_root"), st.sem("factors")
        bonus_in, bonus_sum, bonus_ready = st.sem("bonus_in"), st.sem("bonus_sum"), st.sem("bonus_ready")
        turned, tok_ready, pairs, pairs_masked = st.sem("turned"), st.sem("tok_ready"), st.sem("pairs"), st.sem("pairs_masked")
        av_done, x_ready, a_copied = st.sem("av_done"), st.sem("x_ready"), st.sem("a_copied")
        step_done, powers_copied = st.sem("step_done"), st.sem("powers_copied")
        local_done, local_copied, r_copied = st.sem("local_done"), st.sem("local_copied"), st.sem("r_copied")
        state_done, state_ready, y_state, y_ready = st.sem("state_done"), st.sem("state_ready"), st.sem("y_state"), st.sem("y_ready")
        mean_done, centred, c_squared = st.sem("mean_done"), st.sem("centred"), st.sem("c_squared")
        var_done, var_root = st.sem("var_done"), st.sem("var_root")
        chain_s = st.sem("dve_chain")
        STEPS = 6
        head = lambda h: (h // 2, slice(DH * (h % 2), DH * (h % 2) + DH))
        vcol = lambda name, j: c.vec[:, VEC[name] + j:VEC[name] + j + 1]
        with nc.Block() as block:
            @block.sync
            def _(sp):
                sp.dma_start(w_up[:, :], loras[l, 0]).then_inc(loaded, 16)
                sp.dma_start(g_up[:, :], loras[l, 1]).then_inc(loaded, 16)
                sp.dma_start(reset_t[:, :], reset).then_inc(loaded, 16)
                sp.dma_start(masks[:, :, :], chunk_masks).then_inc(loaded, 16)

            @block.tensor
            def _(pe):
                pe.wait_ge(loaded, 64)
                pe.wait_ge(lora_in, 2)
                pe.wait_ge(mixed, 8)
                for j in range(2):
                    nc.tensor.matmul(c.ps[:, j, :], w_up[0:DH, j * P:(j + 1) * P], lora[0:DH, 0, :],
                                     start=True, stop=True).then_inc(lora_done, 1)
                for j in range(2):
                    nc.tensor.matmul(c.ps[:, 2 + j, :], w_up[DH:P, j * P:(j + 1) * P], mix[DH:P, WA_T, :],
                                     start=True, stop=True).then_inc(lora_done, 1)
                for j in range(2):
                    nc.tensor.matmul(c.ps[:, 4 + j, :], g_up[:, j * P:(j + 1) * P], lora[:, 1, :],
                                     start=True, stop=True).then_inc(lora_done, 1)
                for j in range(2):
                    pe.wait_ge(kk_squared, j + 1)
                    nc.tensor.matmul(c.ps[:, 6 + j, :], c.mat["halves"], sq[:, j, :], start=True,
                                     stop=True).then_inc(kk_summed, 1)
                pe.wait_ge(lora_out, 6)
                for j in range(2):
                    pe.wait_ge(bonus_in, j + 1)
                    nc.tensor.matmul(c.ps[:, j, :], c.mat["halves"], sq[:, j, :], start=True,
                                     stop=True).then_inc(bonus_sum, 1)
                pe.wait_ge(factors, 8)
                pe.wait_ge(bonus_ready, 2)
                for t in range(NT):
                    cols = slice(t * P, (t + 1) * P)
                    if t:
                        pe.wait_ge(local_copied, 3 * t)
                        pe.wait_ge(r_copied, t)
                    for q, src in ((QA, f_a), (QB, f_b), (QK, f_k), (QV, None)):
                        for j in range(2):
                            i = 2 * q + j
                            m = nc.tensor.transpose(c.ps[:, i // 4, (i % 4) * P:(i % 4 + 1) * P],
                                                    src[:, j, cols] if src is not None else mix[:, V_T + j, cols],
                                                    c.mat["ident"])
                    m.then_inc(turned, 1)
                    for b, (left, right) in enumerate(((f_a, f_b), (f_b, f_a), (f_k, f_a), (f_b, f_r), (f_k, f_r))):
                        for q in range(2):
                            rows = slice(DH * q, DH * q + DH)
                            for j in range(2):
                                at = (b % 2) * 2 * P + j * P
                                m = nc.tensor.matmul(c.ps[:, 2 + 3 * q + b // 2, at:at + P], left[rows, j, cols],
                                                     right[rows, j, cols], start=True, stop=True)
                            m.then_inc(pairs, 1)
                    pe.wait_ge(tok_ready, 2 * (t + 1))
                    pe.wait_ge(pairs_masked, 10 * (t + 1))
                    for h in range(R_HEADS):
                        m = nc.tensor.matmul(c.ps[:, 1, h * DH:(h + 1) * DH], akT[:, h, :],
                                             tok[:, QV, h * DH:(h + 1) * DH], start=True, stop=True)
                    m.then_inc(av_done, 1)
                    pe.wait_ge(a_copied, t + 1)
                    for i in range(STEPS):
                        pe.wait_ge(x_ready, (STEPS + 1) * t + i + 1)
                        if i:
                            pe.wait_ge(powers_copied, 2 * ((STEPS - 1) * t + i))
                        for h in range(R_HEADS):
                            m = nc.tensor.matmul(c.ps[:, 0, h * P:(h + 1) * P], NT_[:, h, :], X[:, h, :],
                                                 start=True, stop=True)
                        if i < STEPS - 1:
                            for h in range(R_HEADS):
                                nc.tensor.matmul(c.ps[:, 1, h * P:(h + 1) * P], NT_[:, h, :], N[:, h, :],
                                                 start=True, stop=True)
                            for h in range(R_HEADS):
                                m = nc.tensor.matmul(c.ps[:, 2, h * P:(h + 1) * P], N[:, h, :], NT_[:, h, :],
                                                     start=True, stop=True)
                        m.then_inc(step_done, 1)
                    pe.wait_ge(x_ready, (STEPS + 1) * (t + 1))
                    for h in range(R_HEADS):
                        j, rows = head(h)
                        m = nc.tensor.matmul(c.ps[rows, 3, j * P:(j + 1) * P], X[:, h, DH:P], rbT[:, h, :],
                                             start=True, stop=True)
                    m.then_inc(local_done, 1)
                    for h in range(R_HEADS):
                        j, rows = head(h)
                        o = c.ps[rows, 4, j * P:(j + 1) * P]
                        nc.tensor.matmul(o, X[:, h, 0:DH], rbT[:, h, :], start=True, stop=False)
                        m = nc.tensor.matmul(o, tok[:, QV, h * DH:(h + 1) * DH], rkT[:, h, :], start=False, stop=True)
                    m.then_inc(local_done, 1)
                    for half in range(2):
                        tk = slice(half * CHUNK, (half + 1) * CHUNK)
                        for h in range(R_HEADS):
                            j, rows = head(h)
                            at, hc = j * P, slice(h * DH, (h + 1) * DH)
                            nc.tensor.matmul(c.ps[rows, 5 + half, at:at + DH], X[tk, h, DH:P], tok[tk, QB, hc],
                                             start=True, stop=True)
                            o = c.ps[rows, 5 + half, at + DH:at + P]
                            nc.tensor.matmul(o, tok[tk, QB, hc], X[tk, h, 0:DH], start=True, stop=False)
                            m = nc.tensor.matmul(o, tok[tk, QK, hc], tok[tk, QV, hc], start=False, stop=True)
                        m.then_inc(local_done, 1)
                pe.wait_ge(local_copied, 3 * NT)
                for n in range(NCH):
                    pe.wait_ge(state_ready, n + 1)
                    for h in range(R_HEADS):
                        j, rows = head(h)
                        m = nc.tensor.matmul(c.ps[rows, 6 + n % 2, j * DH:(j + 1) * DH], GH[rows, n, j, 0:DH],
                                             state[rows, n, j, :], start=True, stop=True)
                    m.then_inc(state_done, 1)
                pe.wait_ge(r_copied, NT)
                for j in range(2):
                    for n in range(NCH):
                        for half in range(2):
                            rows = slice(half * DH, half * DH + DH)
                            m = nc.tensor.matmul(c.ps[rows, j, n * CHUNK:(n + 1) * CHUNK], state[rows, n, j, :],
                                                 r_prime[rows, j, n * CHUNK:(n + 1) * CHUNK], start=True, stop=True)
                    m.then_inc(y_state, 1)
                for j in range(2):
                    pe.wait_ge(y_ready, j + 1)
                    nc.tensor.matmul(c.ps[:, 2 + j, :], c.mat["halves"], y[:, j, :], start=True,
                                     stop=True).then_inc(mean_done, 1)
                for j in range(2):
                    pe.wait_ge(c_squared, j + 1)
                    nc.tensor.matmul(c.ps[:, 4 + j, :], c.mat["halves"], sq[:, j, :], start=True,
                                     stop=True).then_inc(var_done, 1)

            @block.scalar
            def _(act):
                act.wait_ge(mixed, 1)
                nc.scalar.activation(lora[0:DH, 0, :], mix[0:DH, WA_T, :], ACT.Tanh).then_inc(lora_in, 1)
                act.wait_ge(mixed, 2)
                nc.scalar.activation(lora[:, 1, :], mix[:, G_T, :], ACT.Sigmoid).then_inc(lora_in, 1)
                for j in range(2):
                    act.wait_ge(lora_done, j + 1)
                    nc.scalar.activation(sig_w[:, j, :], c.ps[:, j, :], ACT.Sigmoid, bias=vcol("w0", j)).then_inc(lora_out, 1)
                for j in range(2):
                    act.wait_ge(lora_done, 2 + j + 1)
                    nc.scalar.activation(rate[:, j, :], c.ps[:, 2 + j, :], ACT.Sigmoid, bias=vcol("a0", j)).then_inc(lora_out, 1)
                for j in range(2):
                    act.wait_ge(lora_done, 4 + j + 1)
                    nc.scalar.copy(gate[:, j, :], c.ps[:, 4 + j, :]).then_inc(lora_out, 1)
                for j in range(2):
                    act.wait_ge(kk_raw, j + 1)
                    nc.scalar.activation(sq[:, j, :], kk[:, j, :], ACT.Square).then_inc(kk_squared, 1)
                for j in range(2):
                    act.wait_ge(cum_ready, 2 * (j + 1))
                    nc.scalar.activation(decay[:, j, :], cum[:, j, :], ACT.Exp, scale=-DECAY).then_inc(decayed, 1)
                    nc.scalar.activation(grow[:, j, :], cum[:, j, :], ACT.Exp, scale=DECAY).then_inc(decayed, 1)
                    nc.scalar.activation(decay_prev[:, j, :], cum_prev[:, j, :], ACT.Exp, scale=-DECAY).then_inc(decayed, 1)
                for j in range(2):
                    act.wait_ge(kk_floor, j + 1)
                    nc.scalar.activation(cum_prev[:, j, :], cum[:, j, :], ACT.Sqrt).then_inc(kk_root, 1)
                for t in range(NT):
                    act.wait_ge(turned, t + 1)
                    if t:
                        act.wait_ge(local_done, 4 * t)
                    for b in range(2):
                        nc.scalar.copy(tok[:, 2 * b:2 * b + 2, :], c.ps[:, b, :]).then_inc(tok_ready, 1)
                    act.wait_ge(tok_ready, 2 * (t + 1))
                    nc.scalar.copy(X[:, :, DH:P], tok[:, QA, :].rearrange("p (h d) -> p h d", h=R_HEADS)).then_inc(a_copied, 1)
                    for i in range(STEPS - 1):
                        act.wait_ge(step_done, STEPS * t + i + 1)
                        nc.scalar.copy(N[:, :, :], c.ps[:, 1, :]).then_inc(powers_copied, 1)
                        nc.scalar.copy(NT_[:, :, :], c.ps[:, 2, :]).then_inc(powers_copied, 1)
                    act.wait_ge(local_done, 4 * t + 2)
                    nc.scalar.copy(y[:, :, t * P:(t + 1) * P],
                                   c.ps[:, 4, 0:2 * P].rearrange("p (j n) -> p j n", j=2)).then_inc(local_copied, 1)
                    for half in range(2):
                        act.wait_ge(local_done, 4 * t + 3 + half)
                        nc.scalar.copy(GH[:, 2 * t + half, :, :], c.ps[:, 5 + half, 0:2 * P]).then_inc(local_copied, 1)
                for j in range(2):
                    act.wait_ge(centred, j + 1)
                    nc.scalar.activation(sq[:, j, :], y[:, j, :], ACT.Square).then_inc(c_squared, 1)
                for j in range(2):
                    act.wait_ge(var_done, j + 1)
                    nc.scalar.activation(cum[:, j, :], c.ps[:, 4 + j, :], ACT.Sqrt, bias=c.eps[:, 1:2],
                                         scale=1.0 / DH).then_inc(var_root, 1)

            @block.vector
            def _(dve):
                ch = Chain(dve, chain_s)
                ORDER = (WA_T, G_T, 2, 3, 0, 1, 4, 5)
                for t in ORDER:
                    u = c.proj[:, R_T + t, :]
                    ch.mark(nc.vector.tensor_tensor(mix[:, t, 1:S], u[:, 0:S - 1], u[:, 1:S], ALU.subtract))
                    ch.mark(nc.vector.tensor_scalar(mix[:, t, 0:1], u[:, 0:1], -1.0, None, ALU.mult))
                ch.wait()
                for t in ORDER:
                    nc.vector.scalar_tensor_tensor(out=mix[:, t, :], in0=mix[:, t, :], scalar=vcol("mu", t),
                                                   in1=c.proj[:, R_T + t, :], op0=ALU.mult, op1=ALU.add).then_inc(mixed, 1)
                ch.mark(nc.vector.memset(state[:, 0, :, :], 0.0))
                dve.wait_ge(mixed, 8)
                for j in range(2):
                    nc.vector.tensor_scalar(kk[:, j, :], mix[:, K_T + j, :], vcol("k_k", j), None, ALU.mult).then_inc(kk_raw, 1)
                dve.wait_ge(loaded, 64)
                for j in range(2):
                    dve.wait_ge(lora_out, j + 1)
                    nc.vector.tensor_tensor_scan(cum[:, j, :], reset_t[:, :], sig_w[:, j, :], 0.0, ALU.mult,
                                                 ALU.add).then_inc(cum_ready, 1)
                    dve.wait_ge(cum_ready, 2 * j + 1)
                    nc.vector.tensor_tensor(cum_prev[:, j, :], cum[:, j, :], sig_w[:, j, :], ALU.subtract).then_inc(cum_ready, 1)
                dve.wait_ge(decayed, 6)
                for j in range(2):
                    dve.wait_ge(kk_summed, j + 1)
                    nc.vector.tensor_scalar(cum[:, j, :], c.ps[:, 6 + j, :], 1e-24, None, ALU.max).then_inc(kk_floor, 1)
                dve.wait_ge(lora_out, 6)
                for j in range(2):
                    ch.link(nc.vector.tensor_scalar(sig_w[:, j, :], rate[:, j, :], 1.0, vcol("k_a", j),
                                                    ALU.subtract, ALU.mult))
                    ch.link(nc.vector.scalar_tensor_tensor(out=sig_w[:, j, :], in0=sig_w[:, j, :], scalar=1.0,
                                                           in1=mix[:, K_T + j, :], op0=ALU.add, op1=ALU.mult))
                    nc.vector.tensor_tensor(f_k[:, j, :], sig_w[:, j, :], grow[:, j, :], ALU.mult).then_inc(factors, 1)
                    nc.vector.tensor_tensor(f_r[:, j, :], mix[:, R_T + j, :], decay[:, j, :], ALU.mult).then_inc(factors, 1)
                    dve.wait_ge(kk_summed, j + 1)
                    nc.vector.scalar_tensor_tensor(out=sq[:, j, :], in0=mix[:, R_T + j, :], scalar=vcol("r_k", j),
                                                   in1=sig_w[:, j, :], op0=ALU.mult, op1=ALU.mult).then_inc(bonus_in, 1)
                for j in range(2):
                    dve.wait_ge(kk_root, j + 1)
                    ch.link(nc.vector.reciprocal(cum_prev[:, j, :], cum_prev[:, j, :]))
                    ch.link(nc.vector.tensor_tensor(kk[:, j, :], kk[:, j, :], cum_prev[:, j, :], ALU.mult))
                    nc.vector.scalar_tensor_tensor(out=f_a[:, j, :], in0=kk[:, j, :], scalar=-1.0,
                                                   in1=decay_prev[:, j, :], op0=ALU.mult, op1=ALU.mult).then_inc(factors, 1)
                    ch.link(nc.vector.tensor_tensor(rate[:, j, :], rate[:, j, :], kk[:, j, :], ALU.mult))
                    nc.vector.tensor_tensor(f_b[:, j, :], rate[:, j, :], grow[:, j, :], ALU.mult).then_inc(factors, 1)
                for j in range(2):
                    dve.wait_ge(bonus_sum, j + 1)
                    dve.wait_ge(factors, 8)
                    nc.vector.tensor_tensor(kk[:, j, :], c.ps[:, j, :], mix[:, V_T + j, :], ALU.mult).then_inc(bonus_ready, 1)
                for t in range(NT):
                    for b, (dst, mask) in enumerate(((N, 0), (NT_, 1), (akT, 1), (rbT, 2), (rkT, 2))):
                        for q in range(2):
                            dve.wait_ge(pairs, 10 * t + 2 * min(b | 1, 4) + q + 1)
                            at = (b % 2) * 2 * P
                            nc.vector.tensor_tensor(
                                dst[:, q::2, :],
                                c.ps[:, 2 + 3 * q + b // 2, at:at + 2 * P].rearrange("p (j n) -> p j n", j=2),
                                masks[:, mask, 0:2 * P].rearrange("p (j n) -> p j n", j=2),
                                ALU.mult).then_inc(pairs_masked, 1)
                    dve.wait_ge(av_done, t + 1)
                    nc.vector.tensor_copy(X[:, :, 0:DH], c.ps[:, 1, 0:R_HEADS * DH].rearrange(
                        "p (h d) -> p h d", h=R_HEADS)).then_inc(x_ready, 1)
                    dve.wait_ge(a_copied, t + 1)
                    dve.wait_ge(x_ready, (STEPS + 1) * t + 1)
                    for i in range(STEPS):
                        dve.wait_ge(step_done, STEPS * t + i + 1)
                        nc.vector.tensor_tensor(X[:, :, :].rearrange("p h n -> p (h n)"),
                                                X[:, :, :].rearrange("p h n -> p (h n)"), c.ps[:, 0, :],
                                                ALU.add).then_inc(x_ready, 1)
                        dve.wait_ge(x_ready, (STEPS + 1) * t + i + 2)
                    dve.wait_ge(local_done, 4 * t + 1)
                    nc.vector.tensor_tensor(r_prime[:, :, t * P:(t + 1) * P],
                                            c.ps[:, 3, 0:2 * P].rearrange("p (j n) -> p j n", j=2),
                                            f_r[:, :, t * P:(t + 1) * P], ALU.add).then_inc(r_copied, 1)
                    dve.wait_ge(local_done, 4 * t + 4)
                dve.wait_ge(local_copied, 3 * NT)
                ch.wait()
                dve.sem_inc(state_ready, 1)
                for n in range(NCH):
                    if n:
                        dve.wait_ge(state_ready, n + 1)
                    ch.link(nc.vector.tensor_tensor(carried[:, :, :], state[:, n, :, :], GH[:, n, :, DH:P], ALU.add))
                    dve.wait_ge(state_done, n + 1)
                    ch.link(nc.vector.tensor_tensor(carried[:, :, :], carried[:, :, :],
                                                    c.ps[:, 6 + n % 2, 0:P].rearrange("p (j d) -> p j d", j=2), ALU.add))
                    end = (n + 1) * CHUNK
                    ch.mark(nc.vector.tensor_scalar(state[:, n + 1, 0, :], carried[:, 0, :], decay[:, 0, end - 1:end],
                                                    None, ALU.mult))
                    ch.link(nc.vector.tensor_scalar(state[:, n + 1, 1, :], carried[:, 1, :], decay[:, 1, end - 1:end],
                                                    None, ALU.mult))
                    dve.sem_inc(state_ready, 1)
                for j in range(2):
                    dve.wait_ge(y_state, j + 1)
                    nc.vector.tensor_tensor(y[:, j, :], y[:, j, :], c.ps[:, j, :], ALU.add).then_inc(y_ready, 1)
                dve.wait_ge(y_ready, 2)
                for j in range(2):
                    dve.wait_ge(mean_done, j + 1)
                    nc.vector.scalar_tensor_tensor(out=y[:, j, :], in0=c.ps[:, 2 + j, :], scalar=-1.0 / DH,
                                                   in1=y[:, j, :], op0=ALU.mult, op1=ALU.add).then_inc(centred, 1)
                dve.wait_ge(centred, 2)
                dve.wait_ge(c_squared, 2)
                for j in range(2):
                    dve.wait_ge(var_root, j + 1)
                    ch.link(nc.vector.reciprocal(cum[:, j, :], cum[:, j, :]))
                    ch.link(nc.vector.scalar_tensor_tensor(out=y[:, j, :], in0=y[:, j, :], scalar=vcol("ln_w", j),
                                                           in1=cum[:, j, :], op0=ALU.mult, op1=ALU.mult))
                    ch.link(nc.vector.scalar_tensor_tensor(out=y[:, j, :], in0=y[:, j, :], scalar=vcol("ln_b", j),
                                                           in1=kk[:, j, :], op0=ALU.add, op1=ALU.add))
                    ch.link(nc.vector.tensor_tensor(c.y[:, 6 + j, :], y[:, j, :], gate[:, j, :], ALU.mult))


SECOND_TILES = 18
A_Q, A_K, A_V, B_Q, B_K, B_V = 0, 4, 5, 6, 10, 14
SPAN = 2 * S - P


def head_norm_stage(nc, c):
    TILES = [(A_Q + t, "qa") for t in range(4)] + [(A_K, "ka")] + [(B_Q + t, "qb") for t in range(4)] + \
            [(B_K + t, "kb") for t in range(4)]
    with Stage(nc, "headnorm") as st:
        sq, root = st.sb("sq", [P, 2, S]), st.sb("root", [P, 2, S])
        turned_sin = st.sb("turned_sin", [P, 5, S])
        squared, summed, rooted, normed = st.sem("squared"), st.sem("summed"), st.sem("rooted"), st.sem("normed")
        turned, roped, swapped = st.sem("turned"), st.sem("roped"), st.sem("swapped")
        v_turned, v_copied, k_copied = st.sem("v_turned"), st.sem("v_copied"), st.sem("k_copied")
        chain_s = st.sem("dve_chain")
        with nc.Block() as block:
            @block.tensor
            def _(pe):
                for i in range(len(TILES)):
                    pe.wait_ge(squared, i + 1)
                    if i >= 2:
                        pe.wait_ge(rooted, i - 1)
                    nc.tensor.matmul(c.ps[:, i % 2, :], c.mat["halves"], sq[:, i % 2, :], start=True,
                                     stop=True).then_inc(summed, 1)
                for j in range(5):
                    if j >= 2:
                        pe.wait_ge(v_copied, j - 1)
                    for n in range(NT):
                        m = nc.tensor.transpose(c.ps[:, 2 + j % 2, n * P:(n + 1) * P],
                                                c.proj[:, A_V if j == 4 else B_V + j, n * P:(n + 1) * P], c.mat["ident"])
                    m.then_inc(v_turned, 1)
                for t in range(5):
                    pe.wait_ge(normed, t + 1)
                    if t == 4:
                        pe.wait_ge(rooted, len(TILES))
                    nc.tensor.matmul(c.ps[:, (4 + t) % 8, :], c.mat["axial_turn"], c.proj[:, t, :], start=True,
                                     stop=True).then_inc(turned, 1)
                pe.wait_ge(roped, 5)
                nc.tensor.matmul(c.ps[:, 1, :], c.mat["swap"], c.proj[:, A_K, :], start=True,
                                 stop=True).then_inc(swapped, 1)

            @block.scalar
            def _(act):
                def square(i):
                    if i >= 2:
                        act.wait_ge(summed, i - 1)
                    nc.scalar.activation(sq[:, i % 2, :], c.proj[:, TILES[i][0], :], ACT.Square).then_inc(squared, 1)

                square(0)
                for i in range(len(TILES)):
                    if i + 1 < len(TILES):
                        square(i + 1)
                    act.wait_ge(summed, i + 1)
                    if i >= 2:
                        act.wait_ge(normed, i - 1)
                    nc.scalar.activation(root[:, i % 2, :], c.ps[:, i % 2, :], ACT.Sqrt, bias=c.eps[:, 0:1],
                                         scale=1.0 / DH).then_inc(rooted, 1)
                for j in range(5):
                    act.wait_ge(v_turned, j + 1)
                    dst = c.va_tok[:, :, :] if j == 4 else c.vb_tok[:, :, j * P:(j + 1) * P]
                    nc.scalar.copy(dst, c.ps[:, 2 + j % 2, :].rearrange("p (n d) -> p n d", n=NT)).then_inc(v_copied, 1)
                act.wait_ge(swapped, 1)
                nc.scalar.copy(c.k_swap[:, :], c.ps[:, 1, :]).then_inc(k_copied, 1)

            @block.vector
            def _(dve):
                ch = Chain(dve, chain_s)
                for i, (t, gain) in enumerate(TILES):
                    dve.wait_ge(rooted, i + 1)
                    ch.link(nc.vector.reciprocal(root[:, i % 2, :], root[:, i % 2, :]))
                    nc.vector.scalar_tensor_tensor(out=c.proj[:, t, :], in0=c.proj[:, t, :],
                                                   scalar=c.vec[:, VEC2[gain]:VEC2[gain] + 1], in1=root[:, i % 2, :],
                                                   op0=ALU.mult, op1=ALU.mult).then_inc(normed, 1)
                for t in range(5):
                    dve.wait_ge(turned, t + 1)
                    ch.mark(nc.vector.tensor_tensor(turned_sin[:, t, :], c.ps[:, (4 + t) % 8, :], c.rope[:, 1, :], ALU.mult))
                    ch.link(nc.vector.tensor_tensor(c.proj[:, t, :], c.proj[:, t, :], c.rope[:, 0, :], ALU.mult))
                    nc.vector.tensor_tensor(c.proj[:, t, :], c.proj[:, t, :], turned_sin[:, t, :], ALU.add).then_inc(roped, 1)


def full_attention_stage(nc, c, biases):
    STEPS = 2 * HEADS * NT
    with Stage(nc, "attn2") as st:
        bias = st.sb("bias", [P, 2, SPAN])
        biased = st.sb("biased", [P, 2, S])
        probs, probs_t = st.sb("probs", [P, 2, S]), st.sb("probs_t", [P, 2, NT, S])
        row_max, neg_max, row_sum = (st.sb(n, [P, STEPS]) for n in ("row_max", "neg_max", "row_sum"))
        loaded = [st.sem(f"bias_loaded{b}") for b in range(2)]
        scored, biased_ready, max_ready, exps = st.sem("scored"), st.sem("biased"), st.sem("max_ready"), st.sem("exps")
        normed, transposed, pt_copied = st.sem("normed"), st.sem("transposed"), st.sem("pt_copied")
        pv_done, out_copied = st.sem("pv_done"), st.sem("out_copied")
        chain_s = st.sem("dve_chain")

        def operands(h):
            rows = slice(DH * (h % 2), DH * (h % 2) + DH)
            if h < HEADS:
                k = c.proj[rows, A_K, :] if h // GROUP == h % 2 else c.k_swap[rows, :]
                return rows, c.proj[rows, A_Q + h // 2, :], k, c.va_tok[:, :, DH * (h // GROUP):DH * (h // GROUP) + DH]
            h -= HEADS
            return rows, c.proj[rows, B_Q + h // 2, :], c.proj[rows, B_K + h // 2, :], c.vb_tok[:, :, DH * h:DH * h + DH]

        with nc.Block() as block:
            @block.sync
            def _(sp):
                for h in range(HEADS):
                    if h >= 2:
                        sp.wait_ge(biased_ready, NT * (h - 1))
                    sp.dma_start(bias[:, h % 2, :], biases[h]).then_inc(loaded[h % 2], 16)

            @block.tensor
            def _(pe):
                def scores(s):
                    h, i = s // NT, s % NT
                    rows, q, k, _ = operands(h)
                    if s >= 2:
                        if (s - 2) // NT < HEADS:
                            pe.wait_ge(exps, s - 1)
                        else:
                            pe.wait_ge(biased_ready, s - 1 - NT * HEADS)
                    nc.tensor.matmul(c.ps[:, s % 2, :], q[:, i * P:(i + 1) * P], k, start=True,
                                     stop=True).then_inc(scored, 1)

                def turn_probs(s):
                    pe.wait_ge(normed, s + 1)
                    if s >= 2:
                        pe.wait_ge(pt_copied, s - 1)
                    for n in range(NT):
                        m = nc.tensor.transpose(c.ps[:, 2 + s % 2, n * P:(n + 1) * P],
                                                probs[:, s % 2, n * P:(n + 1) * P], c.mat["ident"])
                    m.then_inc(transposed, 1)

                def values(h):
                    rows, _, _, v = operands(h)
                    t = h // 2
                    pe.wait_ge(pt_copied, NT * (h + 1))
                    if h % 2 == 0 and t >= 2:
                        pe.wait_ge(out_copied, t - 1)
                    for n in range(NT):
                        m = nc.tensor.matmul(c.ps[rows, 4 + t % 2, :], v[:, n, :], probs_t[:, h % 2, n, :],
                                             start=(n == 0), stop=(n == NT - 1))
                    m.then_inc(pv_done, 1)

                for s in range(STEPS + 2):
                    if s < STEPS:
                        scores(s)
                    if 1 <= s <= STEPS:
                        turn_probs(s - 1)
                    if s >= 2 and (s - 2) % NT == NT - 1:
                        values((s - 2) // NT)

            @block.scalar
            def _(act):
                def exponents(s):
                    act.wait_ge(max_ready, s + 1)
                    if s >= 2:
                        act.wait_ge(transposed, s - 1)
                    first = s // NT < HEADS
                    nc.scalar.activation(probs[:, s % 2, :], c.ps[:, s % 2, :] if first else biased[:, s % 2, :],
                                         ACT.Exp, bias=neg_max[:, s:s + 1], scale=DH ** -0.5 if first else 1.0,
                                         accum_out=row_sum[:, s:s + 1]).then_inc(exps, 1)

                def copy_turned(s):
                    h, i = s // NT, s % NT
                    act.wait_ge(transposed, s + 1)
                    if h >= 2:
                        act.wait_ge(pv_done, h - 1)
                    nc.scalar.copy(probs_t[:, h % 2, :, i * P:(i + 1) * P],
                                   c.ps[:, 2 + s % 2, :].rearrange("p (n q) -> p n q", n=NT)).then_inc(pt_copied, 1)

                for s in range(STEPS + 1):
                    if s < STEPS:
                        exponents(s)
                    if s >= 1:
                        copy_turned(s - 1)

            @block.vector
            def _(dve):
                ch = Chain(dve, chain_s)

                def maxima(s):
                    h, i = s // NT, s % NT
                    dve.wait_ge(scored, s + 1)
                    src, scale = c.ps[:, s % 2, :], -DH ** -0.5
                    if h >= HEADS:
                        b = h - HEADS
                        dve.wait_ge(loaded[b % 2], 16 * (b // 2 + 1))
                        dve.wait_ge(exps, s - 1)
                        start = (NT - 1 - i) * P
                        nc.vector.scalar_tensor_tensor(out=biased[:, s % 2, :], in0=src, scalar=DH ** -0.5,
                                                       in1=bias[:, b % 2, start:start + S], op0=ALU.mult,
                                                       op1=ALU.add).then_inc(biased_ready, 1)
                        dve.wait_ge(biased_ready, s + 1 - NT * HEADS)
                        src, scale = biased[:, s % 2, :], -1.0
                    ch.link(nc.vector.tensor_reduce(row_max[:, s:s + 1], src, AX, ALU.max))
                    nc.vector.tensor_scalar(neg_max[:, s:s + 1], row_max[:, s:s + 1], scale, None,
                                            ALU.mult).then_inc(max_ready, 1)

                def normalise(s):
                    dve.wait_ge(exps, s + 1)
                    ch.link(nc.vector.reciprocal(row_sum[:, s:s + 1], row_sum[:, s:s + 1]))
                    nc.vector.tensor_scalar(probs[:, s % 2, :], probs[:, s % 2, :], row_sum[:, s:s + 1], None,
                                            ALU.mult).then_inc(normed, 1)

                def copy_out(t):
                    dve.wait_ge(pv_done, 2 * (t + 1))
                    nc.vector.tensor_copy(c.y[:, t, :], c.ps[:, 4 + t % 2, :]).then_inc(out_copied, 1)

                for s in range(STEPS + 1):
                    if s < STEPS:
                        maxima(s)
                    if s >= 1:
                        normalise(s - 1)
                    if s >= 2 * NT + 4 and (s - 4) % (2 * NT) == 0:
                        copy_out((s - 4) // (2 * NT) - 1)
                copy_out(HEADS - 1)


def second_out_stage(nc, c, w_out):
    HT = KD // 2
    with Stage(nc, "out2") as st:
        entry = Entry(st, c, c.y, c.vec[:, VEC2["outa"]:], [tuple(range(HT)), tuple(range(HT, KD))], False)
        W = Weights(st)
        scaled = st.sb("scaled", [P, 2, 2, S])
        scaled_ready, freed, x_ready = st.sem("scaled"), st.sem("banks_read"), st.sem("x_ready")
        with nc.Block() as block:
            @block.sync
            def _(sp):
                for n in range(KD):
                    W.load(sp, 0, n, w_out[n])

            @block.tensor
            def _(pe):
                half = lambda n: lambda k: (c.ps[:, 2 * n + k // HT, :], k % HT == 0, k % HT == HT - 1)
                first_products(pe, nc, c, W, entry, [half(n) for n in range(2)])
                entry.tensor_factor(pe, nc)
                for n in range(2, KD):
                    pe.wait_ge(W.lo_ready, n + 1)
                    pe.wait_ge(freed, 2 * (n - 1))
                    for k in range(KD):
                        for i, (w, h) in enumerate(W.terms(n, k, entry.hi[:, k, :], entry.lo[:, k, :])):
                            m = nc.tensor.matmul(c.ps[:, 2 * (n % 2) + k // HT, :], w, h, start=(k % HT == 0 and i == 0),
                                                 stop=(k % HT == HT - 1 and i == 2))
                    m.then_inc(W.done, 1)

            @block.scalar
            def _(act):
                first_scalar(act, nc, W, entry)
                for n in range(SLOTS, KD):
                    W.split_hi(act, nc, 0, n)

            @block.vector
            def _(dve):
                first_vector(dve, nc, W, entry)
                for j in range(KD):
                    dve.wait_ge(W.done, j + 1)
                    if j >= 2:
                        dve.wait_ge(x_ready, j - 1)
                    for g in range(2):
                        nc.vector.tensor_tensor(scaled[:, j % 2, g, :], c.ps[:, 2 * (j % 2) + g, :], entry.rs[:, g, :],
                                                ALU.mult).then_inc(freed, 1)
                    if SLOTS <= j + 3 < KD:
                        W.split_lo(dve, nc, 0, j + 3)
                    dve.wait_ge(freed, 2 * (j + 1))
                    nc.vector.tensor_tensor(scaled[:, j % 2, 0, :], scaled[:, j % 2, 0, :], scaled[:, j % 2, 1, :], ALU.add).then_inc(scaled_ready, 1)
                    dve.wait_ge(scaled_ready, j + 1)
                    nc.vector.tensor_tensor(c.x[:, j, :], c.x[:, j, :], scaled[:, j % 2, 0, :], ALU.add).then_inc(x_ready, 1)


def conv_ffn_stage(nc, c, w_up, w_down, out):
    with Stage(nc, "convffn") as st:
        entry = Entry(st, c, c.x, c.vec[:, VEC2["norm2"]:], ALL, False)
        W = Weights(st)
        a_hi, a_lo = st.sb("a_hi", [P, KF, S], F32R), st.sb("a_lo", [P, KF, S], F32R)
        conv, u = c.y[:, 0:4, :], c.y[:, 4:6, :]
        freed, middle, side, conv_ready = st.sem("banks_read"), st.sem("middle_tap"), st.sem("side_tap"), st.sem("conv_ready")
        gelu_ready = st.sem("gelu_ready")
        product, act_hi, act_ready = st.sem("product"), st.sem("act_hi_ready"), st.sem("act_ready")
        stored = st.sem("stored")
        tap = lambda it, n, i: c.vec[:, bass.ds(it * 4 + (VEC2["conv"] + 4 * n + i), 1)]
        with nc.Block() as block:
            @block.sync
            def _(sp):
                load_ffn(sp, W, lambda n: w_up[n], lambda n: w_down[n])
                with sp.Fori(0, KD) as j:
                    sp.wait_ge(freed, j + (UP + 1))
                    sp.dma_start(out[:, j, :], c.x[:, j, :]).then_inc(stored, 16)
                sp.wait_ge(stored, 16 * KD)

            @block.tensor
            def _(pe):
                ffn_tensor(pe, nc, c, W, entry, a_hi, a_lo, act_ready, freed)

            @block.scalar
            def _(act):
                first_scalar(act, nc, W, entry)

                def middle_tap(it, n):
                    act.wait_ge(freed, it + (n + 1))
                    nc.scalar.activation(conv[:, n % 4, :], u[:, n % 2, :], ACT.Identity, bias=tap(it, n, 3),
                                         scale=tap(it, n, 1)).then_inc(middle, 1)

                def gelu(it, q):
                    act.wait_ge(conv_ready, it * 2 + (2 * q + 1))
                    nc.scalar.activation(conv[:, 2 * q % 4, :], conv[:, 2 * q % 4, :],
                                         ACT.Gelu_apprx_tanh).then_inc(gelu_ready, 1)

                def first_part(it, q):
                    act.wait_ge(product, it + (q + 1))
                    nc.scalar.copy(a_hi[:, it + q, :], conv[:, 2 * q % 4, :]).then_inc(act_hi, 1)

                middle_tap(0, 0)
                middle_tap(0, 1)
                gelu(0, 0)
                W.split_hi(act, nc, 0, SLOTS)
                middle_tap(0, 2)
                first_part(0, 0)
                with act.Fori(0, LOOPS) as it:
                    for q in (1, 2):
                        W.split_hi(act, nc, it * SLOTS, 2 * q + 3)
                        middle_tap(it * SLOTS, 2 * q + 1)
                        gelu(it * 2, q)
                        W.split_hi(act, nc, it * SLOTS, 2 * q + 4)
                        middle_tap(it * SLOTS, 2 * q + 2)
                        first_part(it * 2, q)
                middle_tap(0, UP - 1)
                gelu(0, KF - 1)
                first_part(0, KF - 1)
                down_splits(act, lambda it, n, w: W.split_hi(act, nc, it, n, w), lambda it, j, products: None)

            @block.vector
            def _(dve):
                first_vector(dve, nc, W, entry)

                def scale(it, n):
                    dve.wait_ge(W.done, it + (n + 1))
                    nc.vector.tensor_tensor(u[:, n % 2, :], c.ps[:, n % SLOTS, :], entry.rs[:, 0, :],
                                            ALU.mult).then_inc(freed, 1)

                def side_taps(it, n):
                    d, s = conv[:, n % 4, :], u[:, n % 2, :]
                    dve.wait_ge(middle, it + (n + 1))
                    nc.vector.scalar_tensor_tensor(out=d[:, 1:S], in0=s[:, 0:S - 1], scalar=tap(it, n, 0), in1=d[:, 1:S],
                                                   op0=ALU.mult, op1=ALU.add).then_inc(side, 1)
                    dve.wait_ge(side, it + (n + 1))
                    nc.vector.scalar_tensor_tensor(out=d[:, 0:S - 1], in0=s[:, 1:S], scalar=tap(it, n, 2),
                                                   in1=d[:, 0:S - 1], op0=ALU.mult, op1=ALU.add).then_inc(conv_ready, 1)

                def multiply(it, q):
                    gate, value = conv[:, 2 * q % 4, :], conv[:, (2 * q + 1) % 4, :]
                    dve.wait_ge(gelu_ready, it + (q + 1))
                    dve.wait_ge(conv_ready, it * 2 + (2 * q + 2))
                    nc.vector.tensor_tensor(gate, gate, value, ALU.mult).then_inc(product, 1)

                def rest(it, q):
                    dve.wait_ge(act_hi, it + (q + 1))
                    nc.vector.tensor_tensor(a_lo[:, it + q, :], conv[:, 2 * q % 4, :], a_hi[:, it + q, :].bitcast(F32),
                                            ALU.subtract).then_inc(act_ready, 1)

                scale(0, 0)
                scale(0, 1)
                side_taps(0, 0)
                side_taps(0, 1)
                W.split_lo(dve, nc, 0, SLOTS)
                scale(0, 2)
                multiply(0, 0)
                side_taps(0, 2)
                with dve.Fori(0, LOOPS) as it:
                    for q in (1, 2):
                        W.split_lo(dve, nc, it * SLOTS, 2 * q + 3)
                        scale(it * SLOTS, 2 * q + 1)
                        rest(it * 2, q - 1)
                        side_taps(it * SLOTS, 2 * q + 1)
                        W.split_lo(dve, nc, it * SLOTS, 2 * q + 4)
                        scale(it * SLOTS, 2 * q + 2)
                        multiply(it * 2, q)
                        side_taps(it * SLOTS, 2 * q + 2)
                scale(0, UP - 1)
                rest(0, KF - 2)
                side_taps(0, UP - 1)
                multiply(0, KF - 1)
                rest(0, KF - 1)

                def outputs(it, j, products):
                    dve.wait_ge(W.done, it * SLOTS + products)
                    nc.vector.tensor_tensor(c.x[:, it + j, :], c.x[:, it + j, :], c.ps[:, j % 2, :],
                                            ALU.add).then_inc(freed, 1)

                down_splits(dve, lambda it, n, w: W.split_lo(dve, nc, it, n, w), outputs)


def load_stage(nc, c, x_t, mats):
    with Stage(nc, "load") as st:
        loaded, made = st.sem("loaded"), st.sem("made")
        with nc.Block() as block:
            @block.sync
            def _(sp):
                sp.dma_start(c.x[:, :, :], x_t).then_inc(loaded, 16)
                sp.dma_start(c.mats[:, :, :], mats).then_inc(loaded, 16)
                sp.wait_ge(loaded, 32)

            @block.vector
            def _(dve):
                nc.vector.memset(c.eps[:, 0:1], NORM_EPS).then_inc(made, 1)
                nc.vector.memset(c.eps[:, 1:2], GN_EPS).then_inc(made, 1)
                nc.vector.memset(c.y[:, :, :], 0.0).then_inc(made, 1)
                nc.vector.memset(c.ps[:, POST_BANK, 0:NT], 0.0).then_inc(made, 1)
                dve.wait_ge(made, 4)


def vec_stage(nc, c, l, vecs, rope=None):
    with Stage(nc, "vec") as st:
        loaded = st.sem("loaded")
        with nc.Block() as block:
            @block.sync
            def _(sp):
                sp.dma_start(c.vec[:, 0:vecs.shape[-1]], vecs[l] if l is not None else vecs).then_inc(loaded, 16)
                if rope is not None:
                    sp.dma_start(c.rope[:, :, :], rope).then_inc(loaded, 16)
                sp.wait_ge(loaded, 16 if rope is None else 32)


def build(nc, a, out):
    c = Chip()
    with ExitStack() as ctx:
        def sb(name, shape, dt=F32):
            return ctx.enter_context(nc.sbuf_tensor(name, shape, dt))

        c.ps = ctx.enter_context(nc.psum_tensor("ps", [P, 8, S], F32))
        c.x, c.y = sb("x", [P, KD, S]), sb("y", [P, KD, S])
        c.mats = sb("mats", [P, len(MATS), P])
        c.mat = {m: c.mats[:, i, :] for i, m in enumerate(MATS)}
        c.vec = sb("vec", [P, max(NVEC, NVEC2)])
        c.eps = sb("eps", [P, 2])
        c.rope = sb("rope", [P, 2, S])
        load_stage(nc, c, a["x"], a["mats"])
        rope_stage(nc, c, a["positions"], a["inv_freq"])
        with nc.Fori(0, DEPTH) as l:
            vec_stage(nc, c, l, a["vecs"])
            ffn_stage(nc, c, "ffn1", l, a["w_ffn1_in"], a["w_ffn1_out"], c.vec[:, VEC["ffn1_pre"]:],
                      VEC["ffn1_post"], True)
            with ExitStack() as mix:
                c.proj = mix.enter_context(nc.sbuf_tensor("proj", [P, MIX_TILES, S], F32))
                c.gates = mix.enter_context(nc.sbuf_tensor("gates", [4, 2, S], F32))
                proj_stage(nc, c, "mixproj", lambda n: a["w_in"][l, n], MIX_TILES,
                           c.vec[:, VEC["mix_pre"]:], True)
                window_attention_stage(nc, c, a["window_mask"])
                mlstm_stage(nc, c, a["selectors"])
                rwkv_stage(nc, c, l, a["loras"], a["chunk_masks"], a["reset"])
            mix_out_stage(nc, c, l, a["w_out"])
            ffn_stage(nc, c, "ffn2", l, a["w_ffn2_in"], a["w_ffn2_out"], c.vec[:, VEC["ffn2_pre"]:],
                      VEC["ffn2_post"], True)
            ple_stage(nc, c, l, a["w_ple_gate"], a["w_ple_proj"], a["p"])
        vec_stage(nc, c, None, a["vecs_2"], a["axial"])
        with ExitStack() as second:
            def sb2(name, shape):
                return second.enter_context(nc.sbuf_tensor(name, shape, F32))

            c.proj = sb2("proj_2", [P, SECOND_TILES, S])
            c.va_tok, c.vb_tok, c.k_swap = sb2("va_tok", [P, NT, P]), sb2("vb_tok", [P, NT, 4 * P]), sb2("k_swap", [P, S])
            proj_stage(nc, c, "proj2", lambda n: a["w_in_2"][n], SECOND_TILES, c.vec[:, VEC2["norm1"]:], False)
            head_norm_stage(nc, c)
            full_attention_stage(nc, c, a["biases"])
        second_out_stage(nc, c, a["w_out_2"])
        conv_ffn_stage(nc, c, a["w_up_2"], a["w_down_2"], out)


def columns(w):
    k, n = w.shape
    return np.ascontiguousarray(w.reshape(k // P, P, n // P, P).transpose(2, 1, 0, 3)).reshape(n // P, P, -1)


def pieces(w):
    t = columns(w)
    out = np.zeros((t.shape[0], len(PIECES), P, PIECE), np.float32)
    for i, (k0, ks) in enumerate(PIECES):
        out[:, i, :, :ks * P] = t[:, :, k0 * P:(k0 + ks) * P]
    return out.reshape(-1, P, PIECE)


def gate_up(w):
    t = columns(w)
    n = t.shape[0] // 2
    return np.ascontiguousarray(np.stack([t[:n], t[n:]], 1)).reshape(2 * n, P, -1)


def per_partition(v):
    return v.reshape(-1, P).T


def shape_matrices():
    i = np.arange(P)
    row, col = i[:, None], i[None, :]
    same_half, same_chunk = row // DH == col // DH, row // CHUNK == col // CHUNK
    turn = np.zeros((P, P), np.float32)
    axial = np.zeros((P, P), np.float32)
    for m in range(P):
        d = m % DH
        if d < ROPE_DIM // 2:
            turn[m + ROPE_DIM // 2, m] = -1.0
        elif d < ROPE_DIM:
            turn[m - ROPE_DIM // 2, m] = 1.0
        if d % 32 < 16:
            axial[m + 16, m] = -1.0
        else:
            axial[m - 16, m] = 1.0
    m = {"ident": row == col, "ones": (row >= 0) & (col >= 0), "halves": same_half, "rope_turn": turn,
         "swap": (row + DH) % P == col, "axial_turn": axial, "strict_low": same_chunk & (row > col),
         "strict_up": same_chunk & (row < col), "incl_up": same_chunk & (row <= col), "causal": row <= col}
    return np.ascontiguousarray(np.stack([np.asarray(m[n], np.float32) for n in MATS], 1))


def layouts(inputs):
    f = {n: np.asarray(v) for n, v in inputs.items()}
    a = {}
    feature_tiles = lambda t: np.ascontiguousarray(t.T.reshape(-1, P, S).transpose(1, 0, 2))
    each = lambda fn, w: np.stack([fn(w[l]) for l in range(DEPTH)])
    a["x"] = feature_tiles(f["x"][0])
    a["p"] = np.stack([feature_tiles(f["p"][l, 0]) for l in range(DEPTH)])
    a["mats"] = shape_matrices()
    for n in ("ffn1", "ffn2"):
        a[f"w_{n}_in"] = each(gate_up, f[f"w_{n}_in"])
        a[f"w_{n}_out"] = each(pieces, f[f"w_{n}_out"])
    a["w_ple_gate"] = each(columns, f["w_ple_gate"])
    a["w_ple_proj"] = each(lambda w: np.ascontiguousarray(columns(w).transpose(1, 0, 2)), f["w_ple_proj"])
    vecs = np.zeros((DEPTH, P, NVEC), np.float32)
    for l in range(DEPTH):
        def put(name, cols):
            vecs[l, :cols.shape[0], VEC[name]:VEC[name] + cols.shape[1]] = cols
        for n in ("ffn1", "mix", "ffn2", "ple"):
            put(n + "_pre", per_partition(f[f"ln_{n}_pre"][l]))
            put(n + "_post", per_partition(f[f"ln_{n}_post"][l]))
        for t in range(4):
            put_at = f["mlstm_conv"][l][t]
            vecs[l, :, VEC["conv"] + 4 * t:VEC["conv"] + 4 * t + 4] = per_partition(put_at)
        put("m_norm", per_partition(f["mlstm_norm"][l]))
        for n in ("mu", "w0", "a0", "k_k", "k_a", "ln_w", "ln_b"):
            put(n, per_partition(f["rwkv_" + n][l]))
        put("r_k", per_partition(f["rwkv_r_k"][l].reshape(-1)))
        put("sinks", np.broadcast_to(f["attn_sinks"][l], (P, 8)))
        put("i_bias", f["mlstm_i_bias"][l][:, None])
        put("f_bias", f["mlstm_f_bias"][l][:, None])
    a["vecs"] = vecs
    attn_cols, rwkv_at = 768, 768 + 1032
    pick = np.r_[rwkv_at:rwkv_at + 1024, 0:attn_cols + 1024]

    def gate_tile(w):
        t = np.zeros((D, P), np.float32)
        t[:, 0:4], t[:, 32:36] = w[:, rwkv_at - 8:rwkv_at - 4], w[:, rwkv_at - 4:rwkv_at]
        return t

    a["w_in"] = each(lambda w: columns(np.concatenate([w[:, pick], gate_tile(w)], 1)), f["w_in"])
    a["w_out"] = each(columns, f["w_out"])
    a["loras"] = np.stack([np.stack([np.concatenate([f["rwkv_w_up"][l], f["rwkv_a_up"][l]]), f["rwkv_g_up"][l]])
                           for l in range(DEPTH)])
    a["positions"] = np.broadcast_to(f["positions"].astype(np.int32, copy=False), (P, S))
    d = np.arange(P) % DH
    inv = 500000.0 ** (-2.0 * (d % (ROPE_DIM // 2)) / ROPE_DIM)
    a["inv_freq"] = np.where(d < ROPE_DIM, inv, 0.0).astype(np.float32)[:, None]
    lag = np.arange(P)[:, None] + WIN - np.arange(2 * WIN)[None, :]
    band = (lag >= 0) & (lag < WIN)
    blocks = np.stack([band & ((n > 0) | (np.arange(2 * WIN) >= WIN)) for n in range(NT)], 1)
    a["window_mask"] = np.where(blocks, 0.0, NEG).astype(np.float32).reshape(P, 2, S)
    sel = np.zeros((4, 6, P), np.float32)
    for h in range(4):
        sel[h, h] = 1.0
        sel[h, 4 + h // 2, DH * (h % 2):DH * (h % 2) + DH] = 1.0
    a["selectors"] = sel
    m = a["mats"]
    a["chunk_masks"] = np.stack([np.tile(m[:, MATS.index(n)], 4) for n in ("strict_low", "strict_up", "incl_up")], 1)
    a["reset"] = np.broadcast_to((np.arange(S) % CHUNK != 0).astype(np.float32), (P, S))
    a["w_in_2"], a["w_out_2"] = columns(f["w_in_2"]), columns(f["w_out_2"])
    a["w_up_2"], a["w_down_2"] = gate_up(f["w_up_2"]), pieces(f["w_down_2"])
    v2 = np.zeros((P, NVEC2), np.float32)
    for name, n in (("norm1", "norm1_g_2"), ("outa", "outa_norm_g_2"), ("outb", "outb_norm_g_2"), ("norm2", "norm2_g_2")):
        cols = per_partition(f[n])
        v2[:, VEC2[name]:VEC2[name] + cols.shape[1]] = cols
    for name in ("qa", "ka", "qb", "kb"):
        v2[:, VEC2[name]] = np.concatenate([f[f"{name}_norm_g_2"]] * 2)
    taps = np.concatenate([f["conv_w_2"], f["conv_b_2"][None]])
    v2[:, VEC2["conv"]:] = taps.reshape(4, 2, KF, P).transpose(3, 2, 1, 0).reshape(P, -1)
    a["vecs_2"] = v2
    token, d = np.arange(S), np.arange(P) % DH
    place = np.where(d[:, None] < 32, token[None] // 64, token[None] % 64)
    angle = place * (10000.0 ** (-2.0 * (d % 16) / 32))[:, None]
    a["axial"] = np.stack([np.cos(angle), np.sin(angle)], 1).astype(np.float32)
    apart = np.abs(np.arange(P)[:, None] + (NT - 1) * P - np.arange(SPAN)[None, :])
    count = sum((apart % step == 0) & (apart <= window // 2) for window, step in ((128, 1), (512, 4), (2048, 16)))
    held = np.where(count > 0, np.log(np.maximum(count, 1)), NEG)
    a["biases"] = np.stack([held - 2.0 ** -(h + 1) * apart for h in range(8)]).astype(np.float32)
    return a


def kernel(**inputs):
    import concourse.bacc as bacc
    from concourse.bass_utils import run_bass_kernel_spmd

    nc = bacc.Bacc("TRN2", target_bir_lowering=False, num_devices=1)
    arrays = {f"in_{n}": np.ascontiguousarray(v) for n, v in layouts(inputs).items()}
    aps = {n[3:]: nc.dram_tensor(n, v.shape, mybir.dt.from_np(v.dtype), kind="ExternalInput").ap()
           for n, v in arrays.items()}
    out = nc.dram_tensor("out", (P, KD, S), F32, kind="ExternalOutput").ap()
    build(nc, aps, out)
    run = run_bass_kernel_spmd(nc, [arrays], core_ids=[0])
    y = run.results[0]["out"]
    return np.ascontiguousarray(np.asarray(y).transpose(1, 0, 2).reshape(D, S).T).reshape(1, S, D)
```

```python
from contextlib import ExitStack

import numpy as np

import concourse.bass as bass
from concourse import mybir

F32 = mybir.dt.float32
I32 = mybir.dt.int32
F32R = mybir.dt.float32r
ACT = mybir.ActivationFunctionType
ALU = mybir.AluOpType
AX = mybir.AxisListType.X

P = 128
S = 512
D = 1024
KD = D // P
FF = 2816
KF = FF // P
DEPTH = 2
DH = 64
NT = S // P
SLOTS = 4
NORM_EPS = 1e-6
GN_EPS = 64e-5
NEG = -1e30
CHUNK = 64
NCH = S // CHUNK
DECAY = float(np.exp(-0.5))
ROPE_DIM = DH // 4
TWO_PI = 2.0 * np.pi
MIX_TILES = 22
PLE = 256

VEC = {}
_at = 0
for _name, _n in (("ffn1_pre", 8), ("ffn1_post", 8), ("mix_pre", 8), ("mix_post", 8), ("ffn2_pre", 8),
                  ("ffn2_post", 8), ("ple_pre", 8), ("ple_post", 8), ("conv", 16), ("m_norm", 2), ("mu", 8),
                  ("w0", 2), ("a0", 2), ("k_k", 2), ("k_a", 2), ("r_k", 2), ("ln_w", 2), ("ln_b", 2),
                  ("sinks", 8), ("i_bias", 1), ("f_bias", 1)):
    VEC[_name] = _at
    _at += _n
NVEC = _at
VEC2 = {}
_at = 0
for _name, _n in (("norm1", 8), ("qa", 1), ("ka", 1), ("qb", 1), ("kb", 1), ("outa", 4), ("outb", 4), ("norm2", 8),
                  ("conv", 2 * 4 * KF)):
    VEC2[_name] = _at
    _at += _n
NVEC2 = _at

MATS = ("ident", "ones", "halves", "rope_turn", "swap", "axial_turn", "strict_low", "strict_up", "incl_up", "causal")


class Stage:

    def __init__(self, nc, c, name):
        self.nc, self.c, self.name = nc, c, name
        self.ctx, self.sem_ctx, self.sems = ExitStack(), ExitStack(), []

    def __enter__(self):
        self.ctx.__enter__()
        return self

    def sb(self, name, shape, dt=F32):
        return self.ctx.enter_context(self.nc.sbuf_tensor(f"{self.name}_{name}", shape, dt))

    def sem(self, name):
        s = self.sem_ctx.enter_context(self.nc.semaphore(f"{self.name}_{name}"))
        self.sems.append(s)
        return s

    def zero_stale(self):
        for stage in self.c.stale:
            for s in stage.sems:
                self.nc.gpsimd.sem_clear(s)

    def __exit__(self, *e):
        if e[0] is None:
            self.nc.all_engine_barrier()
            for stage in self.c.stale:
                stage.sem_ctx.close()
            self.c.stale = [self]
        return self.ctx.__exit__(*e)


def settle(nc, c):
    for stage in c.stale:
        for s in stage.sems:
            nc.gpsimd.sem_clear(s)
        stage.sem_ctx.close()
    c.stale = []
    nc.all_engine_barrier()


class Chain:

    def __init__(self, eng, sem):
        self.eng, self.sem, self.n = eng, sem, 0

    def mark(self, ins):
        self.n += 1
        ins.then_inc(self.sem, 1)

    def wait(self):
        if self.n:
            self.eng.wait_ge(self.sem, self.n)

    def link(self, ins):
        self.mark(ins)
        self.wait()


class Chip:
    stale = []


POST_BANK = 7


class Spread:

    def __init__(self, st, c, name, sums, features, banks, diag=None):
        self.c, self.sums, self.features, self.banks = c, sums, features, banks
        G = len(banks)
        self.root, self.inv = st.sb(f"{name}_root", [P, NT, G]), st.sb(f"{name}_inv", [P, NT, G])
        self.diag = diag if diag is not None else st.sb(f"{name}_diag", [P, NT, P])
        self.rooted, self.inverted = st.sem(f"{name}_rooted"), st.sem(f"{name}_inverted")
        self.diag_ready, self.spread = st.sem(f"{name}_diag_ready"), st.sem(f"{name}_spread")

    def scalar(self, act, nc):
        nc.scalar.activation(self.root[:, :, :], self.sums, ACT.Sqrt, bias=self.c.eps[:, 0:1],
                             scale=1.0 / self.features).then_inc(self.rooted, 1)

    def vector(self, dve, nc):
        dve.wait_ge(self.rooted, 1)
        nc.vector.reciprocal(self.inv[:, :, :], self.root[:, :, :]).then_inc(self.inverted, 1)
        dve.wait_ge(self.inverted, 1)
        for g in range(len(self.banks)):
            if g:
                dve.wait_ge(self.spread, g)
            nc.vector.tensor_tensor(self.diag[:, :, :], self.c.mat["ident"].unsqueeze(1).to_broadcast([P, NT, P]),
                                    self.inv[:, :, g:g + 1].to_broadcast([P, NT, P]), ALU.mult).then_inc(self.diag_ready, 1)

    def tensor(self, pe, nc):
        for g, bank in enumerate(self.banks):
            pe.wait_ge(self.diag_ready, g + 1)
            nc.tensor.matmul(self.c.ps[:, bank, :], self.c.mat["ones"], self.diag[:, :, :], start=True,
                             stop=True).then_inc(self.spread, 1)


class Entry:

    def __init__(self, st, c, src, gain, groups, post, fetch=None):
        self.st, self.c, self.src, self.gain, self.groups, self.post, self.fetch = st, c, src, gain, groups, post, fetch
        self.hi, self.lo = st.sb("h_hi", [P, KD, S], F32R), st.sb("h_lo", [P, KD, S], F32R)
        self.hi_ready, self.lo_ready = st.sem("h_hi_ready"), st.sem("h_lo_ready")
        if fetch:
            self.fetched = st.sem("vectors_fetched")
        if post:
            self.post_factor = Spread(st, c, "post", c.ps[:, POST_BANK, 0:NT].unsqueeze(2), D, [POST_BANK])
            self.scaled, self.x_ready = st.sem("post_scaled"), st.sem("x_ready")
        G = len(groups)
        if groups:
            self.sq = c.y if src is c.x else st.sb("sq", [P, KD, S])
            self.squared, self.summed, self.rs_ready = st.sem("squared"), st.sem("summed"), st.sem("rs_ready")
            self.folded = st.sem("folded")
            self.pre = Spread(st, c, "pre", c.ps[:, 6, 0:G * NT].rearrange("p (g n) -> p n g", g=G), P * (KD // G),
                              range(6, 6 + G), self.post_factor.diag if post else None)
            self.rs = st.sb("rs", [P, len(groups), S])

    def scalar_start(self, act, nc):
        if self.post:
            self.post_factor.scalar(act, nc)
        if self.fetch:
            self.fetch().then_inc(self.fetched, 1)

    def scalar_tiles(self, act, nc):
        if self.fetch:
            act.wait_ge(self.fetched, 1)
        for k in range(KD):
            if self.post:
                act.wait_ge(self.x_ready, k + 1)
            if self.gain is None:
                nc.scalar.copy(self.hi[:, k, :], self.src[:, k, :]).then_inc(self.hi_ready, 1)
            else:
                nc.scalar.activation(self.hi[:, k, :], self.src[:, k, :], ACT.Copy,
                                     scale=self.gain[:, k:k + 1]).then_inc(self.hi_ready, 1)
            if self.groups:
                nc.scalar.activation(self.sq[:, k, :], self.src[:, k, :], ACT.Square).then_inc(self.squared, 1)

    def scalar_root(self, act, nc):
        if self.groups:
            act.wait_ge(self.summed, 1)
            self.pre.scalar(act, nc)

    def scalar_factor(self, act, nc):
        for g in range(len(self.groups)):
            act.wait_ge(self.pre.spread, g + 1)
            nc.scalar.copy(self.rs[:, g, :], self.c.ps[:, self.pre.banks[g], :]).then_inc(self.rs_ready, 1)

    def gpsimd(self, pool, nc):
        self.st.zero_stale()
        if self.post:
            for k in range(KD):
                pool.wait_ge(self.scaled, k + 1)
                nc.gpsimd.tensor_tensor(self.c.x[:, k, :], self.c.x[:, k, :], self.c.y[:, k, :], ALU.add).then_inc(self.x_ready, 1)

    def vector_start(self, dve, nc):
        if self.post:
            self.post_factor.vector(dve, nc)
            dve.wait_ge(self.post_factor.spread, 1)
        if self.fetch:
            dve.wait_ge(self.fetched, 1)

    def vector_step(self, dve, nc, i):
        c = self.c
        if self.post and i < KD:
            nc.vector.tensor_tensor(c.y[:, i, :], c.y[:, i, :], c.ps[:, POST_BANK, :], ALU.mult).then_inc(self.scaled, 1)
        k = i - 2
        if 0 <= k < KD:
            dve.wait_ge(self.hi_ready, k + 1)
            if self.gain is None:
                m = nc.vector.tensor_tensor(self.lo[:, k, :], self.src[:, k, :], self.hi[:, k, :].bitcast(F32), ALU.subtract)
            else:
                m = nc.vector.scalar_tensor_tensor(out=self.lo[:, k, :], in0=self.src[:, k, :], scalar=self.gain[:, k:k + 1],
                                                   in1=self.hi[:, k, :].bitcast(F32), op0=ALU.mult, op1=ALU.subtract)
            m.then_inc(self.lo_ready, 1)

    def vector_fold(self, dve, nc):
        G, width = len(self.groups), KD // max(len(self.groups), 1)
        if self.groups:
            dve.wait_ge(self.squared, KD)
        folds = 0
        while self.groups and width > 1:
            width //= 2
            v = self.sq[:, :, :].rearrange("p (g k) n -> p g k n", g=G)
            if folds:
                dve.wait_ge(self.folded, folds)
            nc.vector.tensor_tensor(v[:, :, 0:width, :], v[:, :, 0:width, :], v[:, :, width:2 * width, :],
                                    ALU.add).then_inc(self.folded, 1)
            folds += 1

    def vector_factor(self, dve, nc):
        if self.groups:
            self.pre.vector(dve, nc)

    def tensor_post(self, pe, nc):
        if self.post:
            self.post_factor.tensor(pe, nc)

    def tensor_sums(self, pe, nc):
        G, folds = len(self.groups), (KD // max(len(self.groups), 1)).bit_length() - 1
        if self.groups:
            pe.wait_ge(self.folded, folds)
            for g in range(G):
                for n in range(NT):
                    m = nc.tensor.matmul(self.c.ps[:, 6, g * NT + n:g * NT + n + 1],
                                         self.sq[:, g * (KD // G), n * P:(n + 1) * P],
                                         self.c.mats[:, MATS.index("ones"), 0:1], start=True, stop=True)
            m.then_inc(self.summed, 1)

    def tensor_factor(self, pe, nc):
        if self.groups:
            self.pre.tensor(pe, nc)


class Exit:

    def __init__(self, st, c, gain, factor):
        self.c, self.gain, self.factor = c, gain, factor
        self.sq, self.total, self.warm = st.sb("y_sq", [P, 2, S]), st.sb("y_total", [P, S]), st.sb("warm", [P, 1])
        self.y_squared, self.y_ready, self.added = st.sem("y_squared"), st.sem("y_ready"), st.sem("y_added")
        self.warmed = st.sem("warmed")

    def scalar(self, act, nc, y, it, j):
        act.wait_ge(self.added, it + (j + 1))
        nc.scalar.activation(self.sq[:, j % 2, :], y, ACT.Square).then_inc(self.y_squared, 1)

    def scalar_end(self, act, nc):
        nc.scalar.activation(self.warm[:, :], self.c.eps[:, 0:1], ACT.Sqrt).then_inc(self.warmed, 1)

    def vector_start(self, dve, nc):
        dve.sem_inc(self.added, 1)
        nc.vector.memset(self.total[:, :], 0.0).then_inc(self.added, 1)

    def vector(self, dve, nc, y, it, j, freed=None):
        dve.wait_ge(self.y_squared, it + (j + 1))
        dve.wait_ge(self.added, it + (j + 2))
        nc.vector.tensor_tensor(self.total[:, :], self.total[:, :], self.sq[:, j % 2, :], ALU.add).then_inc(self.added, 1)
        m = nc.vector.tensor_scalar(self.c.y[:, it + j, :], y, self.gain(it + j), self.factor, ALU.mult, ALU.mult)
        m.then_inc(freed if freed is not None else self.y_ready, 1)

    def tensor(self, pe, nc):
        pe.wait_ge(self.added, KD + 2)
        for n in range(NT):
            nc.tensor.matmul(self.c.ps[:, POST_BANK, n:n + 1], self.total[:, n * P:(n + 1) * P],
                             self.c.mats[:, MATS.index("ones"), 0:1], start=True, stop=True)


class Weights:

    def __init__(self, st):
        self.raw = st.sb("w_raw", [P, SLOTS, D])
        self.hi, self.lo = st.sb("w_hi", [P, 2, D], F32R), st.sb("w_lo", [P, 2, D], F32R)
        self.raw_ready = [st.sem(f"w_raw_ready{s}") for s in range(SLOTS)]
        self.hi_ready, self.lo_ready, self.done = st.sem("w_hi_ready"), st.sem("w_lo_ready"), st.sem("mm_done")

    def load(self, sp, it, n, src, width=D):
        s = n % SLOTS
        if n >= SLOTS:
            sp.wait_ge(self.lo_ready, it + (n - SLOTS + 1))
        sp.dma_start(self.raw[:, s, 0:width], src).then_inc(self.raw_ready[s], 16)

    def split_hi(self, act, nc, it, n, width=D):
        s = n % SLOTS
        act.wait_ge(self.raw_ready[s], it * (16 // SLOTS) + 16 * (n // SLOTS + 1))
        if n >= 2:
            act.wait_ge(self.done, it + (n - 1))
        nc.scalar.copy(self.hi[:, n % 2, 0:width], self.raw[:, s, 0:width]).then_inc(self.hi_ready, 1)

    def split_lo(self, dve, nc, it, n, width=D):
        s = n % SLOTS
        dve.wait_ge(self.hi_ready, it + (n + 1))
        nc.vector.tensor_tensor(self.lo[:, n % 2, 0:width], self.raw[:, s, 0:width],
                                self.hi[:, n % 2, 0:width].bitcast(F32), ALU.subtract).then_inc(self.lo_ready, 1)

    def terms(self, n, k, hi, lo):
        w = slice(k * P, (k + 1) * P)
        return ((self.hi[:, n % 2, w], hi), (self.hi[:, n % 2, w], lo), (self.lo[:, n % 2, w], hi))

    def multiply(self, nc, out, n, ks, hi, lo, k0=0, start=True, stop=True):
        for k in range(ks):
            for i, (w, h) in enumerate(self.terms(n, k, hi[:, k0 + k, :], lo[:, k0 + k, :])):
                m = nc.tensor.matmul(out, w, h, start=(start and k == 0 and i == 0), stop=(stop and k == ks - 1 and i == 2))
        return m


def first_products(pe, nc, c, W, entry, outs):
    entry.tensor_post(pe, nc)
    pe.wait_ge(W.lo_ready, 2)
    for k in range(KD):
        pe.wait_ge(entry.lo_ready, k + 1)
        for n in range(2):
            out, start, stop = outs[n](k)
            for i, (w, h) in enumerate(W.terms(n, k, entry.hi[:, k, :], entry.lo[:, k, :])):
                m = nc.tensor.matmul(out, w, h, start=(start and i == 0), stop=(stop and i == 2))
            if k == KD - 1:
                m.then_inc(W.done, 1)
    entry.tensor_sums(pe, nc)


def whole(c, bank):
    return lambda k: (c.ps[:, bank, :], k == 0, k == KD - 1)


def first_scalar(act, nc, W, entry):
    entry.scalar_start(act, nc)
    W.split_hi(act, nc, 0, 0)
    W.split_hi(act, nc, 0, 1)
    entry.scalar_tiles(act, nc)
    W.split_hi(act, nc, 0, 2)
    entry.scalar_root(act, nc)
    W.split_hi(act, nc, 0, 3)
    entry.scalar_factor(act, nc)


def first_vector(dve, nc, W, entry):
    entry.vector_start(dve, nc)
    for i in range(KD + 2):
        entry.vector_step(dve, nc, i)
        if i in (1, 2):
            W.split_lo(dve, nc, 0, i - 1)
    entry.vector_fold(dve, nc)
    W.split_lo(dve, nc, 0, 2)
    entry.vector_factor(dve, nc)
    W.split_lo(dve, nc, 0, 3)
    if entry.groups:
        dve.wait_ge(entry.rs_ready, len(entry.groups))


ALL = [tuple(range(KD))]

PIECES = ((0, 6), (6, 6), (12, 5), (17, 5))
PIECE = 6 * P
UP = 2 * KF
LOOPS = (UP - SLOTS) // SLOTS


def load_ffn(sp, W, w_in, w_out):
    for n in range(SLOTS):
        W.load(sp, 0, n, w_in(n))
    with sp.Fori(0, LOOPS) as it:
        for n in range(SLOTS, 2 * SLOTS):
            W.load(sp, it * SLOTS, n, w_in(it * SLOTS + n))
    with sp.Fori(0, KD) as j:
        for i, (_, ks) in enumerate(PIECES):
            W.load(sp, j * SLOTS, UP + i, w_out(j * SLOTS + i)[:, 0:ks * P], ks * P)


def ffn_tensor(pe, nc, c, W, entry, a_hi, a_lo, act_ready, freed):
    first_products(pe, nc, c, W, entry, [whole(c, n) for n in range(2)])

    def tile(it, n):
        pe.wait_ge(W.lo_ready, it + (n + 1))
        if n >= SLOTS:
            pe.wait_ge(freed, it + (n - SLOTS + 1))
        W.multiply(nc, c.ps[:, n % SLOTS, :], n, KD, entry.hi, entry.lo).then_inc(W.done, 1)

    tile(0, 2)
    entry.tensor_factor(pe, nc)
    tile(0, 3)
    with pe.Fori(0, LOOPS) as it:
        for n in range(SLOTS, 2 * SLOTS):
            tile(it * SLOTS, n)
    with pe.Fori(0, KD // 2) as it:
        for b in range(2):
            pe.wait_ge(freed, it * 2 + (UP - 1 + b))
            for i, (k0, ks) in enumerate(PIECES):
                n = UP + SLOTS * b + i
                pe.wait_ge(W.lo_ready, it * (2 * SLOTS) + (n + 1))
                pe.wait_ge(act_ready, k0 + ks)
                W.multiply(nc, c.ps[:, b, :], n, ks, a_hi, a_lo, k0, start=(i == 0),
                           stop=(i == len(PIECES) - 1)).then_inc(W.done, 1)


def down_splits(eng, split, evacuate):
    def output(it, b, last):
        for i in range(1, SLOTS):
            split(it * SLOTS, UP + SLOTS * b + i, PIECES[i][1] * P)
        if not last:
            split(it * SLOTS, UP + SLOTS * (b + 1), PIECES[0][1] * P)
        evacuate(it, b, UP + SLOTS * b + SLOTS)

    with eng.Fori(0, KD // 2 - 1) as it:
        for b in range(2):
            output(it * 2, b, False)
    output(0, KD - 2, False)
    output(0, KD - 1, True)


def ffn_stage(nc, c, name, l, w_in, w_out, pre, post_at, fetch=None):
    with Stage(nc, c, name) as st:
        entry = Entry(st, c, c.x, pre, ALL, True, fetch)
        leave = Exit(st, c, lambda j: c.vec[:, bass.ds(j + post_at, 1)], 0.5)
        W = Weights(st)
        a_hi, a_lo = st.sb("a_hi", [P, KF, S], F32R), st.sb("a_lo", [P, KF, S], F32R)
        gate, up = c.y[:, 0:2, :], c.y[:, 2, :]
        freed = st.sem("banks_read")
        silu_ready = st.sem("silu_ready")
        product, act_hi, act_ready = st.sem("product"), st.sem("act_hi_ready"), st.sem("act_ready")
        with nc.Block() as block:
            @block.sync
            def _(sp):
                load_ffn(sp, W, lambda n: w_in[l, n], lambda n: w_out[l, n])

            @block.tensor
            def _(pe):
                ffn_tensor(pe, nc, c, W, entry, a_hi, a_lo, act_ready, freed)
                leave.tensor(pe, nc)

            @block.scalar
            def _(act):
                first_scalar(act, nc, W, entry)

                def silu(it, q):
                    act.wait_ge(freed, it * 2 + (2 * q + 1))
                    nc.scalar.activation(gate[:, q % 2, :], gate[:, q % 2, :], ACT.Silu).then_inc(silu_ready, 1)

                def first_part(it, q):
                    act.wait_ge(product, it + (q + 1))
                    nc.scalar.copy(a_hi[:, it + q, :], gate[:, q % 2, :]).then_inc(act_hi, 1)

                silu(0, 0)
                first_part(0, 0)
                W.split_hi(act, nc, 0, SLOTS)
                silu(0, 1)
                with act.Fori(0, LOOPS) as it:
                    for q in (1, 2):
                        W.split_hi(act, nc, it * SLOTS, 2 * q + 3)
                        first_part(it * 2, q)
                        W.split_hi(act, nc, it * SLOTS, 2 * q + 4)
                        silu(it * 2, q + 1)
                first_part(0, KF - 1)

                def squares(it, j, products):
                    act.wait_ge(W.done, it * SLOTS + products)
                    leave.scalar(act, nc, c.ps[:, j % 2, :], it, j)

                down_splits(act, lambda it, n, w: W.split_hi(act, nc, it, n, w), squares)
                leave.scalar_end(act, nc)

            @block.gpsimd
            def _(pool):
                entry.gpsimd(pool, nc)

            @block.vector
            def _(dve):
                leave.vector_start(dve, nc)
                first_vector(dve, nc, W, entry)

                def scale_gate(it, q):
                    dve.wait_ge(W.done, it * 2 + (2 * q + 1))
                    nc.vector.tensor_tensor(gate[:, q % 2, :], c.ps[:, 2 * q % SLOTS, :], entry.rs[:, 0, :],
                                            ALU.mult).then_inc(freed, 1)

                def multiply(it, q):
                    dve.wait_ge(W.done, it * 2 + (2 * q + 2))
                    nc.vector.tensor_tensor(up, c.ps[:, (2 * q + 1) % SLOTS, :], entry.rs[:, 0, :],
                                            ALU.mult).then_inc(freed, 1)
                    dve.wait_ge(silu_ready, it + (q + 1))
                    dve.wait_ge(freed, it * 2 + (2 * q + 2))
                    nc.vector.tensor_tensor(gate[:, q % 2, :], gate[:, q % 2, :], up, ALU.mult).then_inc(product, 1)

                def rest(it, q):
                    dve.wait_ge(act_hi, it + (q + 1))
                    nc.vector.tensor_tensor(a_lo[:, it + q, :], gate[:, q % 2, :], a_hi[:, it + q, :].bitcast(F32),
                                            ALU.subtract).then_inc(act_ready, 1)

                scale_gate(0, 0)
                multiply(0, 0)
                W.split_lo(dve, nc, 0, SLOTS)
                scale_gate(0, 1)
                rest(0, 0)
                with dve.Fori(0, LOOPS) as it:
                    for q in (1, 2):
                        W.split_lo(dve, nc, it * SLOTS, 2 * q + 3)
                        multiply(it * 2, q)
                        W.split_lo(dve, nc, it * SLOTS, 2 * q + 4)
                        scale_gate(it * 2, q + 1)
                        rest(it * 2, q)
                multiply(0, KF - 1)
                rest(0, KF - 1)

                def outputs(it, j, products):
                    leave.vector(dve, nc, c.ps[:, j % 2, :], it, j, freed)

                down_splits(dve, lambda it, n, w: W.split_lo(dve, nc, it, n, w), outputs)


def eight_products(pe, nc, c, W, entry, freed):
    for n in range(2, KD):
        pe.wait_ge(W.lo_ready, n + 1)
        if n >= SLOTS:
            pe.wait_ge(freed, n - SLOTS + 1)
        W.multiply(nc, c.ps[:, n % SLOTS, :], n, KD, entry.hi, entry.lo).then_inc(W.done, 1)
        if n == 2:
            entry.tensor_factor(pe, nc)


def mix_out_stage(nc, c, l, w_out):
    with Stage(nc, c, "mixout") as st:
        entry = Entry(st, c, c.y, None, (), False)
        leave = Exit(st, c, lambda j: c.vec[:, VEC["mix_post"] + j:VEC["mix_post"] + j + 1], 1.0)
        W = Weights(st)
        freed = st.sem("banks_read")
        with nc.Block() as block:
            @block.sync
            def _(sp):
                for n in range(KD):
                    W.load(sp, 0, n, w_out[l, n])

            @block.tensor
            def _(pe):
                first_products(pe, nc, c, W, entry, [whole(c, n) for n in range(2)])
                eight_products(pe, nc, c, W, entry, freed)
                leave.tensor(pe, nc)

            @block.scalar
            def _(act):
                first_scalar(act, nc, W, entry)
                for j in range(KD):
                    if SLOTS <= j + 3 < KD:
                        W.split_hi(act, nc, 0, j + 3)
                    act.wait_ge(W.done, j + 1)
                    leave.scalar(act, nc, c.ps[:, j % SLOTS, :], 0, j)
                leave.scalar_end(act, nc)

            @block.gpsimd
            def _(pool):
                entry.gpsimd(pool, nc)

            @block.vector
            def _(dve):
                leave.vector_start(dve, nc)
                first_vector(dve, nc, W, entry)
                for j in range(KD):
                    if SLOTS <= j + 3 < KD:
                        W.split_lo(dve, nc, 0, j + 3)
                    leave.vector(dve, nc, c.ps[:, j % SLOTS, :], 0, j, freed)


def ple_stage(nc, c, l, w_gate, w_proj, p_t):
    KP = PLE // P
    with Stage(nc, c, "ple") as st:
        entry = Entry(st, c, c.x, c.vec[:, VEC["ple_pre"]:], ALL, True)
        leave = Exit(st, c, lambda j: c.vec[:, VEC["ple_post"] + j:VEC["ple_post"] + j + 1], 1.0)
        W = Weights(st)
        proj_w, pt = st.sb("proj_w", [P, KD, KP * P]), st.sb("pt", [P, KP, S])
        wp_hi, wp_lo = st.sb("proj_w_hi", [P, KD, KP * P], F32R), st.sb("proj_w_lo", [P, KD, KP * P], F32R)
        p_hi, p_lo = st.sb("p_hi", [P, KP, S], F32R), st.sb("p_lo", [P, KP, S], F32R)
        gate, y = st.sb("gate", [P, 2, S]), st.sb("y", [P, 2, S])
        p_loaded, p_hi_ready, p_ready = st.sem("p_loaded"), st.sem("p_hi_ready"), st.sem("p_ready")
        freed, p_done, gate_ready, gated = st.sem("banks_read"), st.sem("p_done"), st.sem("gate_ready"), st.sem("gated")
        with nc.Block() as block:
            @block.sync
            def _(sp):
                W.load(sp, 0, 0, w_gate[l, 0])
                W.load(sp, 0, 1, w_gate[l, 1])
                sp.dma_start(proj_w[:, :, :], w_proj[l]).then_inc(p_loaded, 16)
                sp.dma_start(pt[:, :, :], p_t[l]).then_inc(p_loaded, 16)
                for n in range(2, KD):
                    W.load(sp, 0, n, w_gate[l, n])

            @block.tensor
            def _(pe):
                first_products(pe, nc, c, W, entry, [whole(c, n) for n in range(2)])

                def from_p(j):
                    if j >= 2:
                        pe.wait_ge(gated, j - 1)
                    for k in range(KP):
                        w = slice(k * P, (k + 1) * P)
                        for i, (a, b) in enumerate(((wp_hi, p_hi), (wp_hi, p_lo), (wp_lo, p_hi))):
                            m = nc.tensor.matmul(c.ps[:, 4 + j % 2, :], a[:, j, w], b[:, k, :], start=(k == 0 and i == 0),
                                                 stop=(k == KP - 1 and i == 2))
                    m.then_inc(p_done, 1)

                for n in range(2, KD):
                    pe.wait_ge(W.lo_ready, n + 1)
                    if n >= SLOTS:
                        pe.wait_ge(freed, n - SLOTS + 1)
                    W.multiply(nc, c.ps[:, n % SLOTS, :], n, KD, entry.hi, entry.lo).then_inc(W.done, 1)
                    if n == 2:
                        entry.tensor_factor(pe, nc)
                    if n == 3:
                        pe.wait_ge(p_ready, 2)
                        from_p(0)
                        from_p(1)
                    if n >= 4:
                        from_p(n - 2)
                from_p(KD - 2)
                from_p(KD - 1)
                leave.tensor(pe, nc)

            @block.scalar
            def _(act):
                entry.scalar_start(act, nc)
                W.split_hi(act, nc, 0, 0)
                W.split_hi(act, nc, 0, 1)
                entry.scalar_tiles(act, nc)
                W.split_hi(act, nc, 0, 2)
                entry.scalar_root(act, nc)
                act.wait_ge(p_loaded, 32)
                nc.scalar.copy(wp_hi[:, :, :], proj_w[:, :, :]).then_inc(p_hi_ready, 1)
                nc.scalar.copy(p_hi[:, :, :], pt[:, :, :]).then_inc(p_hi_ready, 1)
                W.split_hi(act, nc, 0, 3)
                entry.scalar_factor(act, nc)

                def squares(j):
                    act.wait_ge(gated, j + 1)
                    leave.scalar(act, nc, y[:, j % 2, :], 0, j)

                for j in range(KD):
                    if SLOTS <= j + 3 < KD:
                        W.split_hi(act, nc, 0, j + 3)
                    act.wait_ge(freed, j + 1)
                    nc.scalar.activation(gate[:, j % 2, :], gate[:, j % 2, :], ACT.Sigmoid).then_inc(gate_ready, 1)
                    if j:
                        squares(j - 1)
                squares(KD - 1)
                leave.scalar_end(act, nc)

            @block.gpsimd
            def _(pool):
                entry.gpsimd(pool, nc)
                pool.wait_ge(p_hi_ready, 2)
                nc.gpsimd.tensor_tensor(wp_lo[:, :, :], proj_w[:, :, :], wp_hi[:, :, :].bitcast(F32),
                                        ALU.subtract).then_inc(p_ready, 1)
                nc.gpsimd.tensor_tensor(p_lo[:, :, :], pt[:, :, :], p_hi[:, :, :].bitcast(F32),
                                        ALU.subtract).then_inc(p_ready, 1)

            @block.vector
            def _(dve):
                leave.vector_start(dve, nc)
                entry.vector_start(dve, nc)
                for i in range(KD + 2):
                    entry.vector_step(dve, nc, i)
                    if i in (1, 2):
                        W.split_lo(dve, nc, 0, i - 1)
                entry.vector_fold(dve, nc)
                W.split_lo(dve, nc, 0, 2)
                entry.vector_factor(dve, nc)
                W.split_lo(dve, nc, 0, 3)
                dve.wait_ge(entry.rs_ready, 1)

                def gated_product(j):
                    dve.wait_ge(gate_ready, j + 1)
                    dve.wait_ge(p_done, j + 1)
                    nc.vector.tensor_tensor(y[:, j % 2, :], gate[:, j % 2, :], c.ps[:, 4 + j % 2, :],
                                            ALU.mult).then_inc(gated, 1)
                    leave.vector(dve, nc, y[:, j % 2, :], 0, j)

                for j in range(KD):
                    if SLOTS <= j + 3 < KD:
                        W.split_lo(dve, nc, 0, j + 3)
                    dve.wait_ge(W.done, j + 1)
                    nc.vector.tensor_tensor(gate[:, j % 2, :], c.ps[:, j % SLOTS, :], entry.rs[:, 0, :],
                                            ALU.mult).then_inc(freed, 1)
                    if j:
                        gated_product(j - 1)
                gated_product(KD - 1)


def start_stage(nc, c, a):
    MAGIC = 1.5 * 2.0 ** 23
    C1 = 6.28125
    C2 = round((TWO_PI - C1) * 2 ** 20) / 2 ** 20
    C3 = float(TWO_PI - C1 - C2)
    EDGE = 3.1415925
    with Stage(nc, c, "start") as st:
        pos_i, pos = st.sb("pos_i", [P, S], I32), st.sb("pos", [P, S])
        ang, turns, freq = st.sb("ang", [P, S]), st.sb("turns", [P, S]), st.sb("freq", [P, 1])
        half_pi = st.sb("half_pi", [P, 1])
        positions_loaded, loaded, made = st.sem("positions_loaded"), st.sem("loaded"), st.sem("made")
        reduced, sines = st.sem("reduced"), st.sem("sines")
        chain_s = st.sem("dve_chain")
        with nc.Block() as block:
            @block.sync
            def _(sp):
                sp.dma_start(pos_i[:, :], a["positions"]).then_inc(positions_loaded, 16)
                sp.dma_start(freq[:, :], a["inv_freq"]).then_inc(positions_loaded, 16)
                for k in range(KD):
                    sp.dma_start(c.x[:, k, :], a["x"][:, k, :]).then_inc(loaded, 16)
                sp.dma_start(c.mats[:, :, :], a["mats"]).then_inc(loaded, 16)
                sp.dma_start(c.vecs[:, :, :], a["vecs"]).then_inc(loaded, 16)
                sp.dma_start(c.vec2[:, :], a["vecs_2"]).then_inc(loaded, 16)
                sp.wait_ge(loaded, 16 * (KD + 3))

            @block.gpsimd
            def _(pool):
                nc.gpsimd.memset(c.eps[:, 0:1], NORM_EPS).then_inc(made, 1)
                nc.gpsimd.memset(c.eps[:, 1:2], GN_EPS).then_inc(made, 1)
                nc.gpsimd.memset(c.y[:, :, :], 0.0).then_inc(made, 1)
                pool.wait_ge(made, 3)

            @block.vector
            def _(dve):
                ch = Chain(dve, chain_s)
                ch.mark(nc.vector.memset(half_pi[:, :], float(np.pi / 2)))
                ch.mark(nc.vector.memset(c.ps[:, POST_BANK, 0:NT], 0.0))
                dve.wait_ge(positions_loaded, 32)
                ch.link(nc.vector.tensor_copy(pos[:, :], pos_i[:, :]))
                ch.link(nc.vector.tensor_scalar(ang[:, :], pos[:, :], freq[:, 0:1], None, ALU.mult))
                ch.link(nc.vector.tensor_scalar(turns[:, :], ang[:, :], 1.0 / TWO_PI, MAGIC, ALU.mult, ALU.add))
                ch.link(nc.vector.tensor_scalar(turns[:, :], turns[:, :], MAGIC, None, ALU.subtract))
                for part in (C1, C2, C3):
                    ch.link(nc.vector.scalar_tensor_tensor(out=ang[:, :], in0=turns[:, :], scalar=-part,
                                                           in1=ang[:, :], op0=ALU.mult, op1=ALU.add))
                nc.vector.tensor_scalar(ang[:, :], ang[:, :], EDGE, -EDGE, ALU.min, ALU.max).then_inc(reduced, 1)

            @block.scalar
            def _(act):
                act.wait_ge(reduced, 1)
                nc.scalar.activation(c.rope[:, 1, :], ang[:, :], ACT.Sin).then_inc(sines, 1)
                nc.scalar.activation(pos[:, :], ang[:, :], ACT.Abs).then_inc(sines, 1)
                act.wait_ge(sines, 2)
                nc.scalar.activation(c.rope[:, 0, :], pos[:, :], ACT.Sin, bias=half_pi[:, 0:1],
                                     scale=-1.0).then_inc(sines, 1)


M_QK = 4
R_T, K_T, V_T, WA_T, G_T, AQ_T, AK_T, AV_T, MQ_T, MV_T, MO_T = 0, 2, 4, 6, 7, 8, 12, 13, 14, 18, 20


def proj_stage(nc, c, name, w_in, tiles, gain, gates, table=None):
    total = tiles + (1 if gates else 0)
    loops = (total - SLOTS) // SLOTS
    tail = range(SLOTS * (loops + 1), total)
    with Stage(nc, c, name) as st:
        entry = Entry(st, c, c.x, gain, ALL, True)
        W = Weights(st)
        freed, table_loaded = st.sem("banks_read"), st.sem("table_loaded")
        with nc.Block() as block:
            @block.sync
            def _(sp):
                for n in range(SLOTS):
                    W.load(sp, 0, n, w_in(n))
                with sp.Fori(0, loops) as it:
                    for n in range(SLOTS, 2 * SLOTS):
                        W.load(sp, it * SLOTS, n, w_in(it * SLOTS + n))
                for n in tail:
                    W.load(sp, 0, n, w_in(n))
                if table is not None:
                    sp.dma_start(c.rope[:, :, :], table).then_inc(table_loaded, 16)
                    sp.wait_ge(table_loaded, 16)

            @block.gpsimd
            def _(pool):
                entry.gpsimd(pool, nc)

            @block.tensor
            def _(pe):
                first_products(pe, nc, c, W, entry, [whole(c, n) for n in range(2)])

                def tile(it, n):
                    pe.wait_ge(W.lo_ready, it + (n + 1))
                    if n >= SLOTS:
                        pe.wait_ge(freed, it + (n - SLOTS + 1))
                    W.multiply(nc, c.ps[:, n % SLOTS, :], n, KD, entry.hi, entry.lo).then_inc(W.done, 1)

                tile(0, 2)
                entry.tensor_factor(pe, nc)
                tile(0, 3)
                with pe.Fori(0, loops) as it:
                    for n in range(SLOTS, 2 * SLOTS):
                        tile(it * SLOTS, n)
                for n in tail:
                    tile(0, n)

            @block.scalar
            def _(act):
                first_scalar(act, nc, W, entry)
                with act.Fori(0, loops) as it:
                    for n in range(SLOTS, 2 * SLOTS):
                        W.split_hi(act, nc, it * SLOTS, n)
                for n in tail:
                    W.split_hi(act, nc, 0, n)

            @block.vector
            def _(dve):
                first_vector(dve, nc, W, entry)

                def store(it, n):
                    dve.wait_ge(W.done, it + (n + 1))
                    b = n % SLOTS
                    if gates and isinstance(it, int) and it + n == tiles:
                        for g in range(2):
                            rows = slice(32 * g, 32 * g + 4)
                            nc.vector.tensor_tensor(c.gates[0:4, g, :], c.ps[rows, b, :], entry.rs[rows, 0, :],
                                                    ALU.mult).then_inc(freed, 1)
                    else:
                        nc.vector.tensor_tensor(c.proj[:, it + n, :], c.ps[:, b, :], entry.rs[:, 0, :],
                                                ALU.mult).then_inc(freed, 1)

                for n in range(2):
                    store(0, n)
                with dve.Fori(0, loops) as it:
                    for n in range(SLOTS, 2 * SLOTS):
                        W.split_lo(dve, nc, it * SLOTS, n)
                        store(it * SLOTS, n - 2)
                for n in tail:
                    W.split_lo(dve, nc, 0, n)
                    store(0, n - 2)
                for n in (total - 2, total - 1):
                    store(0, n)


HEADS, GROUP, WIN = 8, 4, 128


def window_attention_stage(nc, c, window_masks):
    SCALE = DH ** -0.5
    half_of = lambda i: slice(DH * (i % 2), DH * (i % 2) + DH)
    with Stage(nc, c, "attn") as st:
        tapped, conv_s = st.sb("tapped", [P, S]), st.sem("conv_chain")
        ident_r, ones_r = st.sb("ident_r", [P, P], F32R), st.sb("ones_r", [P, P], F32R)
        masks, masks_r = st.sb("masks", [P, 3, S]), st.sb("masks_r", [P, 3, S], F32R)
        turned_sin, rotated = st.sb("turned_sin", [P, 2, S]), st.sb("rotated", [P, 2, S])
        k_hi, k_lo = st.sb("k_hi", [P, 2, S], F32R), st.sb("k_lo", [P, 2, S], F32R)
        q_both = st.sb("q_both", [P, 3, S], F32R)
        v_tok = st.sb("v_tok", [P, NT, 2, DH + 1])
        sinks = st.sb("sinks", [P, HEADS])
        top, neg_top = st.sb("top", [P, 2, NT]), st.sb("neg_top", [P, 2, NT], F32R)
        diag = st.sb("diag", [P, 2, NT, P], F32R)
        sink_exp, share = st.sb("sink_exp", [P, 2, NT, 1]), st.sb("share", [P, 2, NT, 1])
        probs = st.sb("probs", [P, 2, NT, 2 * WIN])
        o_tok = st.sb("o_tok", [P, 2, NT, 2, DH])
        loaded, consts, ones_set, sinks_ready = st.sem("loaded"), st.sem("consts"), st.sem("ones_set"), st.sem("sinks_ready")
        turned, cos_done, sin_done, roped = st.sem("turned"), st.sem("cos_done"), st.sem("sin_done"), st.sem("roped")
        v_turned, v_copied = st.sem("v_turned"), st.sem("v_copied")
        k_firsts, k_ready, q_firsts, q_ready = st.sem("k_firsts"), st.sem("k_ready"), st.sem("q_firsts"), st.sem("q_ready")
        rough, rough_read, tops, diag_ready = st.sem("rough"), st.sem("rough_read"), st.sem("tops"), st.sem("diag_ready")
        scored, exps, sink_exps, pv_done = st.sem("scored"), st.sem("exps"), st.sem("sink_exps"), st.sem("pv_done")
        summed, inverted, normed = st.sem("summed"), st.sem("inverted"), st.sem("normed")
        transposed, out_copied = st.sem("transposed"), st.sem("out_copied")
        ROPED = (4, 0, 1, 2, 3)
        PARTNER_BANK = (0, 1, 6, 7, 7)
        with nc.Block() as block:
            @block.sync
            def _(sp):
                sp.dma_start(masks[:, :, :], window_masks).then_inc(loaded, 16)

            @block.gpsimd
            def _(pool):
                st.zero_stale()
                nc.gpsimd.memset(v_tok[:, :, :, DH:DH + 1], 1.0).then_inc(ones_set, 1)
                pool.wait_ge(ones_set, 1)
                conv = Chain(pool, conv_s)
                tap = lambda n, t: c.vec[:, VEC["conv"] + 4 * n + t:VEC["conv"] + 4 * n + t + 1]
                for t in range(4):
                    u, out = c.proj[:, MQ_T + t, :], c.y[:, M_QK + t, :]
                    conv.link(nc.gpsimd.tensor_scalar(out, u, tap(3, t), None, ALU.mult))
                    for back in range(1, 4):
                        conv.link(nc.gpsimd.tensor_scalar(tapped[:, 0:S - back], u[:, 0:S - back], tap(3 - back, t), None, ALU.mult))
                        conv.link(nc.gpsimd.tensor_tensor(out[:, back:S], out[:, back:S], tapped[:, 0:S - back], ALU.add))

            @block.tensor
            def _(pe):
                def partner(i):
                    nc.tensor.matmul(c.ps[:, PARTNER_BANK[i], :], c.mat["rope_turn"], c.proj[:, AQ_T + ROPED[i], :],
                                     start=True, stop=True).then_inc(turned, 1)

                for i in range(3):
                    partner(i)
                for n in range(NT):
                    m = nc.tensor.transpose(c.ps[:, 5, n * P:(n + 1) * P], c.proj[:, AV_T, n * P:(n + 1) * P],
                                            c.mat["ident"])
                m.then_inc(v_turned, 1)
                partner(3)
                pe.wait_ge(consts, 3)

                def rough_scores(h):
                    pe.wait_ge(q_ready, h + 1)
                    if h % GROUP == 0:
                        pe.wait_ge(k_ready, 2 * (h // GROUP + 1))
                    if h:
                        pe.wait_ge(rough_read, h)
                    for b in range(2):
                        nc.tensor.matmul(c.ps[:, b, :], ident_r[:, :], masks_r[:, b, :], start=True, stop=False)
                        for n in (2 * b, 2 * b + 1):
                            at, first = (n % 2) * 2 * WIN, max(n - 1, 0)
                            m = nc.tensor.matmul(c.ps[:, b, at + (first - n + 1) * P:at + 2 * P], q_both[:, h % 3, n * P:(n + 1) * P],
                                                 k_hi[:, h // GROUP, first * P:(n + 1) * P], start=False, stop=(n % 2 == 1))
                    m.then_inc(rough, 1)

                def scores(h):
                    if h >= 2:
                        pe.wait_ge(exps, 2 * (h - 1))
                    for b in range(2):
                        bank = 2 + 2 * (h % 2) + b
                        nc.tensor.matmul(c.ps[:, bank, 0:S - b * P], ident_r[:, :], masks_r[:, 2, 0:S - b * P], start=True,
                                         stop=False)
                        for j in (2 * b, 2 * b + 1):
                            last = min(j + 2, NT)
                            o = c.ps[:, bank, (j % 2) * 2 * P:(j % 2) * 2 * P + (last - j) * P]
                            for k in (k_hi, k_lo):
                                nc.tensor.matmul(o, k[:, h // GROUP, j * P:(j + 1) * P], q_both[:, h % 3, j * P:last * P],
                                                 start=False, stop=False)
                            if j == 0:
                                pe.wait_ge(diag_ready, h + 1)
                            m = nc.tensor.matmul(o, ones_r[:, :], diag[:, h % 2, j:last, :], start=False, stop=(j % 2 == 1))
                        m.then_inc(scored, 1)

                def values(h):
                    g = h // GROUP
                    pe.wait_ge(exps, 2 * (h + 1))
                    if h == 0:
                        pe.wait_ge(v_copied, 1)
                        pe.wait_ge(ones_set, 1)
                    if h:
                        pe.wait_ge(normed, h)
                    for n in range(NT):
                        o = c.ps[:, 6, n * (DH + 1):(n + 1) * (DH + 1)]
                        if n:
                            nc.tensor.matmul(o, probs[:, h % 2, n - 1, WIN:2 * WIN], v_tok[:, n - 1, g, :], start=True, stop=False)
                        m = nc.tensor.matmul(o, probs[:, h % 2, n, 0:WIN], v_tok[:, n, g, :], start=(n == 0), stop=True)
                    m.then_inc(pv_done, 1)

                def turn_back(t):
                    pe.wait_ge(normed, 2 * t + 2)
                    if t:
                        pe.wait_ge(out_copied, t)
                    for n in range(NT):
                        m = nc.tensor.transpose(c.ps[:, 7, n * P:(n + 1) * P], o_tok[:, t % 2, n, :, :], c.mat["ident"])
                    m.then_inc(transposed, 1)

                pe.wait_ge(roped, 2)
                rough_scores(0)
                for h in range(HEADS):
                    if h + 1 < HEADS:
                        rough_scores(h + 1)
                    if h == 1:
                        pe.wait_ge(roped, 4)
                        partner(4)
                        pe.wait_ge(v_copied, 1)
                    scores(h)
                    if h == 3:
                        pe.wait_ge(roped, 5)
                    if h >= 3 and h % 2:
                        turn_back((h - 3) // 2)
                    if h:
                        if h == 1:
                            pe.wait_ge(roped, 3)
                        values(h - 1)
                values(HEADS - 1)
                turn_back(HEADS // 2 - 1)

            @block.scalar
            def _(act):
                nc.scalar.copy(ident_r[:, :], c.mat["ident"]).then_inc(consts, 1)
                nc.scalar.copy(ones_r[:, :], c.mat["ones"]).then_inc(consts, 1)
                act.wait_ge(loaded, 16)
                nc.scalar.copy(masks_r[:, :, :], masks[:, :, :]).then_inc(consts, 1)

                def first_of_q(h):
                    act.wait_ge(roped, h // 2 + 2)
                    if h >= 3:
                        act.wait_ge(scored, 2 * (h - 2))
                    nc.scalar.copy(q_both[half_of(h), h % 3, :], c.proj[half_of(h), AQ_T + h // 2, :]).then_inc(q_firsts, 1)

                act.wait_ge(roped, 1)
                for g in range(2):
                    for half in range(2):
                        nc.scalar.copy(k_hi[half_of(half), g, :], c.proj[half_of(g), AK_T, :]).then_inc(k_firsts, 1)
                    if g == 0:
                        first_of_q(0)
                        first_of_q(1)
                act.wait_ge(v_turned, 1)
                nc.scalar.copy(v_tok[:, :, :, 0:DH], c.ps[:, 5, :].rearrange("p (n g d) -> p n g d", n=NT, g=2)).then_inc(v_copied, 1)

                def exponents(h):
                    act.wait_ge(tops, h + 1)
                    if h >= 2:
                        act.wait_ge(summed, h - 1)
                    nc.scalar.activation(sink_exp[:, h % 2, :, 0], neg_top[:, h % 2, :].bitcast(F32), ACT.Exp, scale=SCALE,
                                         bias=c.vec[:, VEC["sinks"] + h:VEC["sinks"] + h + 1]).then_inc(sink_exps, 1)
                    for b in range(2):
                        act.wait_ge(scored, 2 * h + b + 1)
                        if h >= 2:
                            act.wait_ge(pv_done, h - 1)
                        bank, w = 2 + 2 * (h % 2) + b, S - b * P
                        nc.scalar.activation(probs[:, h % 2, 2 * b:2 * b + 2, :].rearrange("p j q -> p (j q)")[:, 0:w],
                                             c.ps[:, bank, 0:w], ACT.Exp, scale=SCALE).then_inc(exps, 1)

                def copy_out(t):
                    act.wait_ge(transposed, t + 1)
                    nc.scalar.copy(c.y[:, t, :], c.ps[:, 7, :]).then_inc(out_copied, 1)

                for h in range(HEADS):
                    if h + 2 < HEADS:
                        first_of_q(h + 2)
                    exponents(h)
                    if h >= 3 and h % 2:
                        copy_out((h - 3) // 2)
                copy_out(HEADS // 2 - 1)

            @block.vector
            def _(dve):
                def rotate(i):
                    u, b = c.proj[:, AQ_T + ROPED[i], :], i % 2
                    if i >= 2:
                        dve.wait_ge(roped, i - 1)
                    nc.vector.tensor_tensor(rotated[:, b, :], u, c.rope[:, 0, :], ALU.mult).then_inc(cos_done, 1)
                    dve.wait_ge(turned, i + 1)
                    nc.vector.tensor_tensor(turned_sin[:, b, :], c.ps[:, PARTNER_BANK[i], :], c.rope[:, 1, :],
                                            ALU.mult).then_inc(sin_done, 1)
                    dve.wait_ge(sin_done, i + 1)
                    nc.vector.tensor_tensor(u, rotated[:, b, :], turned_sin[:, b, :], ALU.add).then_inc(roped, 1)

                def rest_of_k(g):
                    for half in range(2):
                        dve.wait_ge(k_firsts, 2 * (g + 1))
                        nc.vector.tensor_tensor(k_lo[half_of(half), g, :], c.proj[half_of(g), AK_T, :],
                                                k_hi[half_of(g), g, :].bitcast(F32), ALU.subtract).then_inc(k_ready, 1)

                def rest_of_q(h):
                    dve.wait_ge(q_firsts, h + 1)
                    nc.vector.tensor_tensor(q_both[half_of(h + 1), h % 3, :], c.proj[half_of(h), AQ_T + h // 2, :],
                                            q_both[half_of(h), h % 3, :].bitcast(F32), ALU.subtract).then_inc(q_ready, 1)

                def maxima(h):
                    dve.wait_ge(rough, h + 1)
                    nc.vector.tensor_reduce(top[:, h % 2, :], c.ps[:, 0:2, :].rearrange("p b (n k) -> p (b n) k", n=2), AX,
                                            ALU.max).then_inc(rough_read, 1)
                    dve.wait_ge(rough_read, h + 1)
                    if h >= 2:
                        dve.wait_ge(sink_exps, h - 1)
                    nc.vector.tensor_scalar(neg_top[:, h % 2, :], top[:, h % 2, :], sinks[:, h:h + 1], -1.0, ALU.max,
                                            ALU.mult).then_inc(tops, 1)
                    dve.wait_ge(tops, h + 1)
                    if h >= 2:
                        dve.wait_ge(scored, 2 * (h - 1))
                    nc.vector.tensor_tensor(diag[:, h % 2, :, :], c.mat["ident"].unsqueeze(1).to_broadcast([P, NT, P]),
                                            neg_top[:, h % 2, :].bitcast(F32).unsqueeze(2).to_broadcast([P, NT, P]),
                                            ALU.mult).then_inc(diag_ready, 1)

                def normalise(h):
                    t = h // 2
                    dve.wait_ge(pv_done, h + 1)
                    dve.wait_ge(sink_exps, h + 1)
                    o = c.ps[:, 6, 0:NT * (DH + 1)].rearrange("p (n d) -> p n d", n=NT)
                    nc.vector.tensor_tensor(share[:, h % 2, :, :], o[:, :, DH:DH + 1], sink_exp[:, h % 2, :, :],
                                            ALU.add).then_inc(summed, 1)
                    dve.wait_ge(summed, h + 1)
                    nc.vector.reciprocal(share[:, h % 2, :, :], share[:, h % 2, :, :]).then_inc(inverted, 1)
                    dve.wait_ge(inverted, h + 1)
                    if t >= 2:
                        dve.wait_ge(transposed, t - 1)
                    nc.vector.tensor_tensor(o_tok[:, t % 2, :, h % 2, :], o[:, :, 0:DH],
                                            share[:, h % 2, :, :].to_broadcast([P, NT, DH]), ALU.mult).then_inc(normed, 1)

                nc.vector.tensor_scalar(sinks[:, :], c.vec[:, VEC["sinks"]:VEC["sinks"] + HEADS], 1.0 / SCALE, None,
                                        ALU.mult).then_inc(sinks_ready, 1)
                rotate(0)
                rotate(1)
                rest_of_k(0)
                rest_of_q(0)
                rest_of_q(1)
                dve.wait_ge(sinks_ready, 1)
                maxima(0)
                rotate(2)
                for h in range(HEADS):
                    if h + 1 < HEADS:
                        maxima(h + 1)
                    if h in (0, 2):
                        rotate(h // 2 + 3)
                    if h >= 2:
                        normalise(h - 2)
                    if h == 1:
                        rest_of_k(1)
                    if h + 2 < HEADS:
                        rest_of_q(h + 2)
                normalise(HEADS - 2)
                normalise(HEADS - 1)


M_HEADS, CAP = 4, 15.0


def mlstm_stage(nc, c, selectors):
    with Stage(nc, c, "mlstm") as st:
        qk = c.y[:, M_QK:M_QK + 4, :]
        g_tanh, soft = st.sb("g_tanh", [4, 2, S]), st.sb("soft", [4, S])
        neg_g, u, run_max = st.sb("neg_g", [4, S]), st.sb("u", [4, S]), st.sb("run_max", [4, S])
        low, zeros = st.sb("low", [4, S]), st.sb("zeros", [4, S])
        select = st.sb("select", [4, 6, P])
        u_col, floor_col = st.sb("u_col", [P, NT, M_HEADS]), st.sb("floor_col", [P, NT, M_HEADS])
        v_tok = st.sb("v_tok", [P, NT, M_HEADS, DH + 1])
        below, weight = st.sb("below", [P, 2, S]), st.sb("weight", [P, 2, S])
        weighted_s = st.sb("weighted", [P, 2, NT, S])
        den = st.sb("den", [P, NT, M_HEADS])
        hid, sq = st.sb("hid", [P, NT, M_HEADS, DH]), st.sb("sq", [P, 2, NT, DH])
        squares, root, inv = (st.sb(n, [P, NT, M_HEADS]) for n in ("squares", "root", "inv"))
        warm = st.sb("warm", [P, 1])
        o_gate, shifted = st.sb("o_gate", [P, 2, S]), st.sb("shifted", [P, 2, S])
        shift_done, share_done, mixed = st.sem("shift_done"), st.sem("share_done"), st.sem("mixed")
        loaded, qk_ready = st.sem("loaded"), st.sem("qk_ready")
        zeros_set, ones_set = st.sem("zeros_set"), st.sem("ones_set")
        biased, tanhed, exped, softened = st.sem("biased"), st.sem("tanhed"), st.sem("exped"), st.sem("softened")
        u_ready, max_ready, low_ready = st.sem("u_ready"), st.sem("max_ready"), st.sem("low_ready")
        v_turned, u_turned, low_turned, max_spread = st.sem("v_turned"), st.sem("u_turned"), st.sem("low_turned"), st.sem("max_spread")
        v_copied, u_copied, floored = st.sem("v_copied"), st.sem("u_copied"), st.sem("floored")
        s_done, below_ready, w_ready = st.sem("s_done"), st.sem("below_ready"), st.sem("w_ready")
        weighted, nd_done = st.sem("weighted_ready"), st.sem("nd_done")
        hid_ready, squared, summed = st.sem("hid_ready"), st.sem("squared"), st.sem("summed")
        warmed, rooted, o_ready = st.sem("warmed"), st.sem("rooted"), st.sem("o_ready")
        normed, turned_back = st.sem("normed"), st.sem("turned_back")
        chain_s = st.sem("dve_chain")
        ITEMS = [(h, s) for h in range(M_HEADS) for s in range(NT)]
        MAX_BANK, OUT_BANK = 4, 2
        QK_ORDER = (0, 2, 1, 3)
        with nc.Block() as block:
            @block.sync
            def _(sp):
                sp.dma_start(select[:, :, :], selectors).then_inc(loaded, 16)

            @block.gpsimd
            def _(pool):
                st.zero_stale()
                nc.gpsimd.memset(zeros[:, :], 0.0).then_inc(zeros_set, 1)
                nc.gpsimd.memset(v_tok[:, :, :, DH:DH + 1], 1.0).then_inc(ones_set, 1)
                pool.wait_ge(ones_set, 1)
                for t in range(KD):
                    u_t, d = c.proj[:, R_T + t, :], shifted[:, t % 2, :]
                    if t >= 2:
                        pool.wait_ge(mixed, t - 1)
                    nc.gpsimd.tensor_tensor(d[:, 1:S], u_t[:, 0:S - 1], u_t[:, 1:S], ALU.subtract).then_inc(shift_done, 1)
                    nc.gpsimd.tensor_scalar(d[:, 0:1], u_t[:, 0:1], -1.0, None, ALU.mult).then_inc(shift_done, 1)
                    pool.wait_ge(shift_done, 2 * (t + 1))
                    nc.gpsimd.tensor_scalar(d, d, c.vec[:, VEC["mu"] + t:VEC["mu"] + t + 1], None, ALU.mult).then_inc(share_done, 1)
                    pool.wait_ge(share_done, t + 1)
                    nc.gpsimd.tensor_tensor(u_t, u_t, d, ALU.add).then_inc(mixed, 1)

            @block.tensor
            def _(pe):
                for half in range(2):
                    for n in range(2):
                        for j in range(2):
                            m = nc.tensor.transpose(c.ps[:, 2 + half, (2 * n + j) * P:(2 * n + j + 1) * P],
                                                    c.proj[:, MV_T + j, (2 * half + n) * P:(2 * half + n + 1) * P],
                                                    c.mat["ident"])
                    m.then_inc(v_turned, 1)

                def columns_of(bank, rows, done):
                    for n in range(NT):
                        m = nc.tensor.matmul(c.ps[:, bank, n * M_HEADS:(n + 1) * M_HEADS], rows[:, n * P:(n + 1) * P],
                                             c.mats[0:4, MATS.index("ident"), 0:4], start=True, stop=True)
                    m.then_inc(done, 1)

                def spread_max(h):
                    nc.tensor.matmul(c.ps[:, MAX_BANK + h, :], select[:, h, :], run_max[:, :],
                                     start=True, stop=True).then_inc(max_spread, 1)

                pe.wait_ge(u_ready, 1)
                columns_of(0, u, u_turned)
                pe.wait_ge(loaded, 16)
                pe.wait_ge(max_ready, 1)
                spread_max(0)
                pe.wait_ge(low_ready, 1)
                pe.wait_ge(v_copied, 2)
                columns_of(3, low, low_turned)
                for h in range(1, M_HEADS):
                    spread_max(h)

                def scores(i):
                    h, s = ITEMS[i]
                    p0 = DH * (h % 2)
                    if i == 0:
                        pe.wait_ge(u_copied, 1)
                    if s == 0:
                        pe.wait_ge(qk_ready, 2 * (h // 2 + 1))
                    if i >= 2:
                        pe.wait_ge(weighted, i - 1)
                    nc.tensor.matmul(c.ps[:, i % 2, 0:S - s * P], qk[p0:p0 + DH, 2 + h // 2, s * P:(s + 1) * P],
                                     qk[p0:p0 + DH, h // 2, s * P:S], start=True, stop=True).then_inc(s_done, 1)

                def sums(h):
                    pe.wait_ge(weighted, NT * (h + 1))
                    if h == 0:
                        pe.wait_ge(ones_set, 1)
                    if h == 1:
                        pe.wait_ge(floored, 1)
                    if h >= OUT_BANK:
                        pe.wait_ge(below_ready, NT * (h - 1))
                    for n in range(NT):
                        for s in range(n + 1):
                            m = nc.tensor.matmul(c.ps[:, OUT_BANK + h, n * (DH + 1):(n + 1) * (DH + 1)],
                                                 weighted_s[:, h % 2, s, n * P:(n + 1) * P], v_tok[:, s, h, :],
                                                 start=(s == 0), stop=(s == n))
                    m.then_inc(nd_done, 1)

                for h in range(M_HEADS):
                    for s in range(NT):
                        if s == 2 and h:
                            sums(h - 1)
                        scores(NT * h + s)
                sums(M_HEADS - 1)
                for j in range(2):
                    pe.wait_ge(normed, j + 1)
                    pe.wait_ge(below_ready, NT * M_HEADS)
                    for n in range(NT):
                        m = nc.tensor.transpose(c.ps[:, 6 + j, n * P:(n + 1) * P], hid[:, n, 2 * j:2 * j + 2, :], c.mat["ident"])
                    m.then_inc(turned_back, 1)

            @block.scalar
            def _(act):
                act.wait_ge(biased, 2)
                nc.scalar.activation(g_tanh[:, :, :], c.gates[0:4, :, :], ACT.Tanh, scale=1.0 / CAP).then_inc(tanhed, 1)
                act.wait_ge(tanhed, 1)
                nc.scalar.activation(soft[:, :], g_tanh[:, 1, :], ACT.Exp, scale=-CAP).then_inc(exped, 1)
                act.wait_ge(exped, 1)
                nc.scalar.activation(soft[:, :], soft[:, :], ACT.Ln, bias=1.0).then_inc(softened, 1)
                for half in range(2):
                    act.wait_ge(v_turned, half + 1)
                    nc.scalar.copy(v_tok[:, 2 * half:2 * half + 2, :, 0:DH],
                                   c.ps[:, 2 + half, :].rearrange("p (n h d) -> p n h d", n=2, h=M_HEADS)).then_inc(v_copied, 1)
                for j in range(2):
                    nc.scalar.activation(o_gate[:, j, :], c.proj[:, MO_T + j, :], ACT.Sigmoid).then_inc(o_ready, 1)
                act.wait_ge(u_turned, 1)
                nc.scalar.copy(u_col[:, :, :], c.ps[:, 0, 0:NT * M_HEADS]).then_inc(u_copied, 1)
                for t in QK_ORDER:
                    nc.scalar.activation(qk[:, t, :], qk[:, t, :], ACT.Silu).then_inc(qk_ready, 1)
                act.wait_ge(low_turned, 1)
                nc.scalar.activation(floor_col[:, :, :], c.ps[:, 3, 0:NT * M_HEADS], ACT.Exp).then_inc(floored, 1)

                def square(h):
                    act.wait_ge(hid_ready, h + 1)
                    if h >= 2:
                        act.wait_ge(summed, h - 1)
                    nc.scalar.activation(sq[:, h % 2, :, :], hid[:, :, h, :], ACT.Square).then_inc(squared, 1)

                for i, (h, s) in enumerate(ITEMS):
                    act.wait_ge(below_ready, i + 1)
                    if i >= 2:
                        act.wait_ge(weighted, i - 1)
                    nc.scalar.activation(weight[:, i % 2, 0:S - s * P], below[:, i % 2, 0:S - s * P], ACT.Exp,
                                         scale=-1.0).then_inc(w_ready, 1)
                    if h and s == NT - 1:
                        square(h - 1)
                nc.scalar.activation(warm[:, :], c.eps[:, 0:1], ACT.Sqrt).then_inc(warmed, 1)
                square(M_HEADS - 1)
                act.wait_ge(summed, M_HEADS)
                nc.scalar.activation(root[:, :, :], squares[:, :, :], ACT.Sqrt, bias=c.eps[:, 0:1],
                                     scale=1.0 / DH).then_inc(rooted, 1)

            @block.vector
            def _(dve):
                ch = Chain(dve, chain_s)
                for g, name in ((0, "i_bias"), (1, "f_bias")):
                    nc.vector.tensor_scalar(c.gates[0:4, g, :], c.gates[0:4, g, :], c.vec[0:4, VEC[name]:VEC[name] + 1],
                                            None, ALU.add).then_inc(biased, 1)
                dve.wait_ge(zeros_set, 1)
                dve.wait_ge(softened, 1)
                ch.link(nc.vector.tensor_tensor_scan(neg_g[:, :], soft[:, :], zeros[:, :], 0.0, ALU.add, ALU.add))
                nc.vector.scalar_tensor_tensor(out=u[:, :], in0=g_tanh[:, 0, :], scalar=CAP, in1=neg_g[:, :],
                                               op0=ALU.mult, op1=ALU.add).then_inc(u_ready, 1)
                dve.wait_ge(u_ready, 1)
                nc.vector.tensor_tensor_scan(run_max[:, :], u[:, :], u[:, :], NEG, ALU.max,
                                             ALU.max).then_inc(max_ready, 1)
                dve.wait_ge(max_ready, 1)
                nc.vector.tensor_tensor(low[:, :], neg_g[:, :], run_max[:, :], ALU.subtract).then_inc(low_ready, 1)
                dve.wait_ge(u_copied, 1)

                def exponent(i):
                    h, s = ITEMS[i]
                    dve.wait_ge(max_spread, h + 1)
                    if i >= 2:
                        dve.wait_ge(w_ready, i - 1)
                    col = u_col[:, s, h:h + 1]
                    nc.vector.tensor_scalar(below[:, i % 2, 0:S - s * P], c.ps[:, MAX_BANK + h, s * P:S], col, col,
                                            ALU.max, ALU.subtract).then_inc(below_ready, 1)

                def normalise(h):
                    dve.wait_ge(nd_done, h + 1)
                    dve.wait_ge(floored, 1)
                    o = c.ps[:, OUT_BANK + h, 0:NT * (DH + 1)].rearrange("p (n d) -> p n d", n=NT)
                    d = den[:, :, h:h + 1]
                    ch.link(nc.vector.tensor_scalar(d, o[:, :, DH:DH + 1], -1.0, None, ALU.mult))
                    ch.link(nc.vector.tensor_tensor(d, d, o[:, :, DH:DH + 1], ALU.max))
                    ch.link(nc.vector.tensor_tensor(d, d, floor_col[:, :, h:h + 1], ALU.max))
                    ch.link(nc.vector.reciprocal(d, d))
                    nc.vector.tensor_tensor(hid[:, :, h, :], o[:, :, 0:DH], d.to_broadcast([P, NT, DH]),
                                            ALU.mult).then_inc(hid_ready, 1)

                def sum_squares(h):
                    dve.wait_ge(squared, h + 1)
                    nc.vector.tensor_reduce(squares[:, :, h], sq[:, h % 2, :, :], AX, ALU.add).then_inc(summed, 1)

                exponent(0)
                for i, (h, s) in enumerate(ITEMS):
                    if i + 1 < len(ITEMS):
                        exponent(i + 1)
                    dve.wait_ge(w_ready, i + 1)
                    ch.link(nc.vector.tensor_tensor(weight[:, i % 2, 0:P], weight[:, i % 2, 0:P], c.mat["causal"],
                                                    ALU.mult))
                    dve.wait_ge(s_done, i + 1)
                    if h >= 2:
                        dve.wait_ge(nd_done, h - 1)
                    nc.vector.scalar_tensor_tensor(out=weighted_s[:, h % 2, s, s * P:S],
                                                   in0=c.ps[:, i % 2, 0:S - s * P], scalar=DH ** -0.5,
                                                   in1=weight[:, i % 2, 0:S - s * P], op0=ALU.mult,
                                                   op1=ALU.mult).then_inc(weighted, 1)
                    if h and s == 2:
                        normalise(h - 1)
                    if h and s == 3:
                        sum_squares(h - 1)
                normalise(M_HEADS - 1)
                sum_squares(M_HEADS - 1)
                dve.wait_ge(rooted, 1)
                ch.link(nc.vector.reciprocal(inv[:, :, :], root[:, :, :]))
                for j in range(2):
                    v = hid[:, :, 2 * j:2 * j + 2, :]
                    nc.vector.tensor_tensor(v, v, inv[:, :, 2 * j:2 * j + 2].unsqueeze(3).to_broadcast([P, NT, 2, DH]),
                                            ALU.mult).then_inc(normed, 1)
                for j in range(2):
                    dve.wait_ge(turned_back, j + 1)
                    dve.wait_ge(o_ready, j + 1)
                    ch.link(nc.vector.scalar_tensor_tensor(
                        out=c.y[:, 4 + j, :], in0=c.ps[:, 6 + j, :], scalar=c.vec[:, VEC["m_norm"] + j:VEC["m_norm"] + j + 1],
                        in1=o_gate[:, j, :], op0=ALU.mult, op1=ALU.mult))


R_HEADS = 4
QA, QB, QK, QV = range(4)


def rwkv_stage(nc, c, l, loras, chunk_masks, reset):
    with Stage(nc, c, "rwkv") as st:
        mix = c.proj[:, R_T:R_T + KD, :]
        w_up, g_up = st.sb("w_up", [P, 2 * P]), st.sb("g_up", [P, 2 * P])
        masks = st.sb("masks", [P, 3, 2 * P])
        reset_t = st.sb("reset", [P, S])
        cum_prev, decay_prev, f_a, f_b, f_k, f_r, lora = (c.proj[:, AQ_T + 2 * i:AQ_T + 2 * i + 2, :] for i in range(7))
        sig_w, rate, gate = st.sb("sig_w", [P, 2, S]), st.sb("rate", [P, 2, S]), st.sb("gate", [P, 2, S])
        cum, decay, grow = st.sb("cum", [P, 2, S]), st.sb("decay", [P, 2, S]), st.sb("grow", [P, 2, S])
        kk, sq, kk_len = (st.sb(n, [P, 2, S]) for n in ("kk", "sq", "kk_len"))
        warm = st.sb("warm", [P, 1])
        tok_2, X_2 = st.sb("tok", [P, 2, 4, 2 * P]), st.sb("x", [P, 2, R_HEADS, P])
        rbT_2, rkT_2 = st.sb("rb_t", [P, 2, R_HEADS, P]), st.sb("rk_t", [P, 2, R_HEADS, P])
        N, NT_, akT = (st.sb(n, [P, R_HEADS, P]) for n in ("n", "n_t", "ak_t"))
        power, power_t = st.sb("power", [P, 2, R_HEADS, P]), st.sb("power_t", [P, 2, R_HEADS, P])
        tok, X, rbT, rkT = ([b[:, t % 2] for t in range(NT)] for b in (tok_2, X_2, rbT_2, rkT_2))
        r_prime, y = st.sb("r_prime", [P, 2, S]), st.sb("y", [P, 2, S])
        GH = st.sb("gh", [P, NCH, 2, P])
        state, carried = st.sb("state", [P, NCH + 1, 2, DH]), st.sb("carried", [P, 2, DH])
        loaded, lora_in, lora_out, warmed = st.sem("loaded"), st.sem("lora_in"), st.sem("lora_out"), st.sem("warmed")
        lora_done, cum_ready, decayed = st.sem("lora_done"), st.sem("cum_ready"), st.sem("decayed")
        kk_raw, kk_squared, kk_summed = st.sem("kk_raw"), st.sem("kk_squared"), st.sem("kk_summed")
        kk_floor, kk_root, factors = st.sem("kk_floor"), st.sem("kk_root"), st.sem("factors")
        bonus_in, bonus_sum, bonus_ready = st.sem("bonus_in"), st.sem("bonus_sum"), st.sem("bonus_ready")
        turned, tok_ready, pairs, pairs_masked = st.sem("turned"), st.sem("tok_ready"), st.sem("pairs"), st.sem("pairs_masked")
        av_done, x_ready, a_copied = st.sem("av_done"), st.sem("x_ready"), st.sem("a_copied")
        n_done, nt_done, step_done = st.sem("n_done"), st.sem("nt_done"), st.sem("step_done")
        n_copied, nt_copied = st.sem("n_copied"), st.sem("nt_copied")
        local_done, local_copied, r_copied = st.sem("local_done"), st.sem("local_copied"), st.sem("r_copied")
        state_done, state_ready, y_state, y_ready = st.sem("state_done"), st.sem("state_ready"), st.sem("y_state"), st.sem("y_ready")
        mean_done, centred, c_squared = st.sem("mean_done"), st.sem("centred"), st.sem("c_squared")
        var_done, var_root = st.sem("var_done"), st.sem("var_root")
        scaled, chain_s = st.sem("scaled"), st.sem("dve_chain")
        STEPS = 6
        PAIR_BANK = ((5, 6), (5, 6), (7, 3), (7, 3), (4, 5))
        head = lambda h: (h // 2, slice(DH * (h % 2), DH * (h % 2) + DH))
        vcol = lambda name, j: c.vec[:, VEC[name] + j:VEC[name] + j + 1]
        with nc.Block() as block:
            @block.sync
            def _(sp):
                sp.dma_start(w_up[:, :], loras[l, 0]).then_inc(loaded, 16)
                sp.dma_start(g_up[:, :], loras[l, 1]).then_inc(loaded, 16)
                sp.dma_start(reset_t[:, :], reset).then_inc(loaded, 16)
                sp.dma_start(masks[:, :, :], chunk_masks).then_inc(loaded, 16)

            @block.gpsimd
            def _(pool):
                st.zero_stale()
                for j in range(2):
                    pool.wait_ge(decayed, 3 * j + 2)
                    nc.gpsimd.tensor_tensor(f_r[:, j, :], mix[:, R_T + j, :], decay[:, j, :], ALU.mult).then_inc(scaled, 1)
                    pool.wait_ge(bonus_in, j + 1)
                    nc.gpsimd.tensor_tensor(f_k[:, j, :], sig_w[:, j, :], grow[:, j, :], ALU.mult).then_inc(scaled, 1)

            @block.tensor
            def _(pe):
                for j in range(2):
                    pe.wait_ge(kk_squared, j + 1)
                    nc.tensor.matmul(c.ps[:, 6 + j, :], c.mat["halves"], sq[:, j, :], start=True,
                                     stop=True).then_inc(kk_summed, 1)
                pe.wait_ge(loaded, 64)
                pe.wait_ge(lora_in, 1)
                for j in range(2):
                    nc.tensor.matmul(c.ps[:, j, :], w_up[0:DH, j * P:(j + 1) * P], lora[0:DH, 0, :],
                                     start=True, stop=True).then_inc(lora_done, 1)
                for j in range(2):
                    nc.tensor.matmul(c.ps[:, 2 + j, :], w_up[DH:P, j * P:(j + 1) * P], mix[DH:P, WA_T, :],
                                     start=True, stop=True).then_inc(lora_done, 1)
                pe.wait_ge(lora_in, 2)
                for j in range(2):
                    nc.tensor.matmul(c.ps[:, 4 + j, :], g_up[:, j * P:(j + 1) * P], lora[:, 1, :],
                                     start=True, stop=True).then_inc(lora_done, 1)
                pe.wait_ge(lora_out, 2)
                for j in range(2):
                    pe.wait_ge(bonus_in, j + 1)
                    nc.tensor.matmul(c.ps[:, j, :], c.mat["halves"], sq[:, j, :], start=True,
                                     stop=True).then_inc(bonus_sum, 1)
                pe.wait_ge(lora_out, 6)
                pe.wait_ge(kk_floor, 2)
                pe.wait_ge(factors, 4)
                pe.wait_ge(scaled, 4)
                def turn(t):
                    cols = slice(t * P, (t + 1) * P)
                    if t >= 2:
                        pe.wait_ge(local_copied, 3 * (t - 1))
                        pe.wait_ge(r_copied, t - 1)
                    for q, src in ((QA, f_a), (QB, f_b), (QK, f_k), (QV, None)):
                        for j in range(2):
                            i = 2 * q + j
                            m = nc.tensor.transpose(c.ps[:, 3 + i // 4, (i % 4) * P:(i % 4 + 1) * P],
                                                    src[:, j, cols] if src is not None else mix[:, V_T + j, cols],
                                                    c.mat["ident"])
                    m.then_inc(turned, 1)

                def pair(t, b):
                    cols = slice(t * P, (t + 1) * P)
                    left, right = ((f_a, f_b), (f_b, f_a), (f_k, f_a), (f_b, f_r), (f_k, f_r))[b]
                    for q in range(2):
                        rows = slice(DH * q, DH * q + DH)
                        for j in range(2):
                            at = (b % 2) * 2 * P + j * P
                            m = nc.tensor.matmul(c.ps[:, PAIR_BANK[b][q], at:at + P], left[rows, j, cols],
                                                 right[rows, j, cols], start=True, stop=True)
                        m.then_inc(pairs, 1)

                def prepare(t, part):
                    if part == 0:
                        turn(t)
                    elif part == 1:
                        pair(t, 0)
                        pair(t, 1)
                    elif part == 2:
                        pe.wait_ge(tok_ready, 2 * (t + 1))
                        pair(t, 2)
                        pair(t, 3)
                    elif part == 3:
                        pe.wait_ge(pairs_masked, 10 * t + 4)
                        pair(t, 4)

                def a_values(t):
                    pe.wait_ge(tok_ready, 2 * (t + 1))
                    pe.wait_ge(pairs_masked, 10 * (t + 1))
                    for h in range(R_HEADS):
                        m = nc.tensor.matmul(c.ps[:, 1, h * DH:(h + 1) * DH], akT[:, h, :],
                                             tok[t][:, QV, h * DH:(h + 1) * DH], start=True, stop=True)
                    m.then_inc(av_done, 1)

                for part in range(4):
                    prepare(0, part)
                pe.wait_ge(bonus_ready, 2)
                a_values(0)
                for t in range(NT):
                    pe.wait_ge(a_copied, t + 1)
                    for i in range(STEPS):
                        n, n_t = (power[:, (i - 1) % 2], power_t[:, (i - 1) % 2]) if i else (N, NT_)
                        if i:
                            pe.wait_ge(n_copied, (STEPS - 1) * t + i)
                            pe.wait_ge(nt_copied, (STEPS - 1) * t + i)
                        else:
                            pe.wait_ge(x_ready, (STEPS + 1) * t + 1)
                        if i < STEPS - 1:
                            for h in range(R_HEADS):
                                m = nc.tensor.matmul(c.ps[:, 1, h * P:(h + 1) * P], n_t[:, h, :], n[:, h, :],
                                                     start=True, stop=True)
                            m.then_inc(n_done, 1)
                            for h in range(R_HEADS):
                                m = nc.tensor.matmul(c.ps[:, 2, h * P:(h + 1) * P], n[:, h, :], n_t[:, h, :],
                                                     start=True, stop=True)
                            m.then_inc(nt_done, 1)
                        pe.wait_ge(x_ready, (STEPS + 1) * t + i + 1)
                        for h in range(R_HEADS):
                            m = nc.tensor.matmul(c.ps[:, 0, h * P:(h + 1) * P], n_t[:, h, :], X[t][:, h, :],
                                                 start=True, stop=True)
                        m.then_inc(step_done, 1)
                        if t + 1 < NT:
                            prepare(t + 1, i)
                    if t + 1 < NT:
                        a_values(t + 1)
                    pe.wait_ge(x_ready, (STEPS + 1) * t + STEPS + 1)
                    for h in range(R_HEADS):
                        j, rows = head(h)
                        m = nc.tensor.matmul(c.ps[rows, 6, j * P:(j + 1) * P], X[t][:, h, DH:P], rbT[t][:, h, :],
                                             start=True, stop=True)
                    m.then_inc(local_done, 1)
                    for h in range(R_HEADS):
                        j, rows = head(h)
                        o = c.ps[rows, 7, j * P:(j + 1) * P]
                        nc.tensor.matmul(o, X[t][:, h, 0:DH], rbT[t][:, h, :], start=True, stop=False)
                        m = nc.tensor.matmul(o, tok[t][:, QV, h * DH:(h + 1) * DH], rkT[t][:, h, :], start=False, stop=True)
                    m.then_inc(local_done, 1)
                    for half in range(2):
                        tk = slice(half * CHUNK, (half + 1) * CHUNK)
                        for h in range(R_HEADS):
                            j, rows = head(h)
                            at, hc = j * P, slice(h * DH, (h + 1) * DH)
                            nc.tensor.matmul(c.ps[rows, 3 + half, at:at + DH], X[t][tk, h, DH:P], tok[t][tk, QB, hc],
                                             start=True, stop=True)
                            o = c.ps[rows, 3 + half, at + DH:at + P]
                            nc.tensor.matmul(o, tok[t][tk, QB, hc], X[t][tk, h, 0:DH], start=True, stop=False)
                            m = nc.tensor.matmul(o, tok[t][tk, QK, hc], tok[t][tk, QV, hc], start=False, stop=True)
                        m.then_inc(local_done, 1)
                pe.wait_ge(r_copied, NT)
                pe.wait_ge(local_copied, 3 * NT)
                for n in range(NCH):
                    pe.wait_ge(state_ready, n + 1)
                    for h in range(R_HEADS):
                        j, rows = head(h)
                        m = nc.tensor.matmul(c.ps[rows, 6 + n % 2, j * DH:(j + 1) * DH], GH[rows, n, j, 0:DH],
                                             state[rows, n, j, :], start=True, stop=True)
                    m.then_inc(state_done, 1)
                    for j in range(2):
                        for half in range(2):
                            rows = slice(half * DH, half * DH + DH)
                            m = nc.tensor.matmul(c.ps[rows, j, n * CHUNK:(n + 1) * CHUNK], state[rows, n, j, :],
                                                 r_prime[rows, j, n * CHUNK:(n + 1) * CHUNK], start=True, stop=True)
                        m.then_inc(y_state, 1)
                for j in range(2):
                    pe.wait_ge(y_ready, j + 1)
                    nc.tensor.matmul(c.ps[:, 2 + j, :], c.mat["halves"], y[:, j, :], start=True,
                                     stop=True).then_inc(mean_done, 1)
                for j in range(2):
                    pe.wait_ge(c_squared, j + 1)
                    nc.tensor.matmul(c.ps[:, 4 + j, :], c.mat["halves"], sq[:, j, :], start=True,
                                     stop=True).then_inc(var_done, 1)

            @block.scalar
            def _(act):
                for j in range(2):
                    act.wait_ge(kk_raw, j + 1)
                    nc.scalar.activation(sq[:, j, :], kk[:, j, :], ACT.Square).then_inc(kk_squared, 1)
                nc.scalar.activation(lora[0:DH, 0, :], mix[0:DH, WA_T, :], ACT.Tanh).then_inc(lora_in, 1)
                for j in range(2):
                    act.wait_ge(kk_floor, j + 1)
                    nc.scalar.activation(kk_len[:, j, :], kk_len[:, j, :], ACT.Sqrt).then_inc(kk_root, 1)
                nc.scalar.activation(lora[:, 1, :], mix[:, G_T, :], ACT.Sigmoid).then_inc(lora_in, 1)
                for j in range(2):
                    act.wait_ge(lora_done, j + 1)
                    nc.scalar.activation(sig_w[:, j, :], c.ps[:, j, :], ACT.Sigmoid, bias=vcol("w0", j)).then_inc(lora_out, 1)
                for j in range(2):
                    act.wait_ge(lora_done, 2 + j + 1)
                    nc.scalar.activation(rate[:, j, :], c.ps[:, 2 + j, :], ACT.Sigmoid, bias=vcol("a0", j)).then_inc(lora_out, 1)
                for j in range(2):
                    act.wait_ge(cum_ready, 2 * (j + 1))
                    nc.scalar.activation(decay[:, j, :], cum[:, j, :], ACT.Exp, scale=-DECAY).then_inc(decayed, 1)
                    nc.scalar.activation(grow[:, j, :], cum[:, j, :], ACT.Exp, scale=DECAY).then_inc(decayed, 1)
                    nc.scalar.activation(decay_prev[:, j, :], cum_prev[:, j, :], ACT.Exp, scale=-DECAY).then_inc(decayed, 1)
                for j in range(2):
                    act.wait_ge(lora_done, 4 + j + 1)
                    nc.scalar.copy(gate[:, j, :], c.ps[:, 4 + j, :]).then_inc(lora_out, 1)
                nc.scalar.activation(warm[:, :], c.eps[:, 0:1], ACT.Sqrt).then_inc(warmed, 1)

                def rows_of(t):
                    act.wait_ge(turned, t + 1)
                    if t >= 2:
                        act.wait_ge(local_done, 4 * (t - 1))
                    for b in range(2):
                        nc.scalar.copy(tok[t][:, 2 * b:2 * b + 2, :], c.ps[:, 3 + b, :]).then_inc(tok_ready, 1)
                    act.wait_ge(tok_ready, 2 * (t + 1))
                    nc.scalar.copy(X[t][:, :, DH:P], tok[t][:, QA, :].rearrange("p (h d) -> p h d", h=R_HEADS)).then_inc(a_copied, 1)

                rows_of(0)
                for t in range(NT):
                    for i in range(STEPS - 1):
                        act.wait_ge(n_done, (STEPS - 1) * t + i + 1)
                        nc.scalar.copy(power[:, i % 2], c.ps[:, 1, :].rearrange("p (h n) -> p h n", h=R_HEADS)).then_inc(n_copied, 1)
                        if i == 1 and t + 1 < NT:
                            rows_of(t + 1)
                    act.wait_ge(local_done, 4 * t + 2)
                    nc.scalar.copy(y[:, :, t * P:(t + 1) * P],
                                   c.ps[:, 7, 0:2 * P].rearrange("p (j n) -> p j n", j=2)).then_inc(local_copied, 1)
                    for half in range(2):
                        act.wait_ge(local_done, 4 * t + 3 + half)
                        nc.scalar.copy(GH[:, 2 * t + half, :, :], c.ps[:, 3 + half, 0:2 * P]).then_inc(local_copied, 1)
                for j in range(2):
                    act.wait_ge(centred, j + 1)
                    nc.scalar.activation(sq[:, j, :], y[:, j, :], ACT.Square).then_inc(c_squared, 1)
                for j in range(2):
                    act.wait_ge(var_done, j + 1)
                    nc.scalar.activation(cum[:, j, :], c.ps[:, 4 + j, :], ACT.Sqrt, bias=c.eps[:, 1:2],
                                         scale=1.0 / DH).then_inc(var_root, 1)

            @block.vector
            def _(dve):
                ch = Chain(dve, chain_s)
                for j in range(2):
                    nc.vector.tensor_scalar(kk[:, j, :], mix[:, K_T + j, :], vcol("k_k", j), None, ALU.mult).then_inc(kk_raw, 1)
                ch.mark(nc.vector.memset(state[:, 0, :, :], 0.0))
                for j in range(2):
                    dve.wait_ge(kk_summed, j + 1)
                    nc.vector.tensor_scalar(kk_len[:, j, :], c.ps[:, 6 + j, :], 1e-24, None, ALU.max).then_inc(kk_floor, 1)

                def unit(j):
                    dve.wait_ge(kk_root, j + 1)
                    dve.wait_ge(kk_raw, 2)
                    ch.link(nc.vector.reciprocal(kk_len[:, j, :], kk_len[:, j, :]))
                    ch.link(nc.vector.tensor_tensor(kk[:, j, :], kk[:, j, :], kk_len[:, j, :], ALU.mult))

                unit(0)
                dve.wait_ge(loaded, 64)
                for j in range(2):
                    dve.wait_ge(lora_out, j + 1)
                    nc.vector.tensor_tensor_scan(cum[:, j, :], reset_t[:, :], sig_w[:, j, :], 0.0, ALU.mult,
                                                 ALU.add).then_inc(cum_ready, 1)
                    dve.wait_ge(cum_ready, 2 * j + 1)
                    nc.vector.tensor_tensor(cum_prev[:, j, :], cum[:, j, :], sig_w[:, j, :], ALU.subtract).then_inc(cum_ready, 1)
                unit(1)
                dve.wait_ge(cum_ready, 4)
                dve.wait_ge(lora_out, 4)
                for j in range(2):
                    ch.link(nc.vector.tensor_scalar(sig_w[:, j, :], rate[:, j, :], 1.0, vcol("k_a", j),
                                                    ALU.subtract, ALU.mult))
                    ch.link(nc.vector.scalar_tensor_tensor(out=sig_w[:, j, :], in0=sig_w[:, j, :], scalar=1.0,
                                                           in1=mix[:, K_T + j, :], op0=ALU.add, op1=ALU.mult))
                    nc.vector.scalar_tensor_tensor(out=sq[:, j, :], in0=mix[:, R_T + j, :], scalar=vcol("r_k", j),
                                                   in1=sig_w[:, j, :], op0=ALU.mult, op1=ALU.mult).then_inc(bonus_in, 1)
                    ch.link(nc.vector.tensor_tensor(rate[:, j, :], rate[:, j, :], kk[:, j, :], ALU.mult))
                for j in range(2):
                    dve.wait_ge(decayed, 3 * (j + 1))
                    nc.vector.scalar_tensor_tensor(out=f_a[:, j, :], in0=kk[:, j, :], scalar=-1.0,
                                                   in1=decay_prev[:, j, :], op0=ALU.mult, op1=ALU.mult).then_inc(factors, 1)
                    nc.vector.tensor_tensor(f_b[:, j, :], rate[:, j, :], grow[:, j, :], ALU.mult).then_inc(factors, 1)
                for j in range(2):
                    dve.wait_ge(bonus_sum, j + 1)
                    dve.wait_ge(factors, 4)
                    nc.vector.tensor_tensor(kk[:, j, :], c.ps[:, j, :], mix[:, V_T + j, :], ALU.mult).then_inc(bonus_ready, 1)
                def mask_pairs(t, b):
                    dst, mask = ((N, 0), (NT_, 1), (akT, 1), (rbT[t], 2), (rkT[t], 2))[b]
                    if t >= 2 and b == 3:
                        dve.wait_ge(local_done, 4 * (t - 1))
                    for q in range(2):
                        dve.wait_ge(pairs, 10 * t + 2 * min(b | 1, 4) + q + 1)
                        at = (b % 2) * 2 * P
                        nc.vector.tensor_tensor(
                            dst[:, q::2, :], c.ps[:, PAIR_BANK[b][q], at:at + 2 * P].rearrange("p (j n) -> p j n", j=2),
                            masks[:, mask, :].rearrange("p (j n) -> p j n", j=2), ALU.mult).then_inc(pairs_masked, 1)

                def a_values(t):
                    dve.wait_ge(av_done, t + 1)
                    nc.vector.tensor_copy(X[t][:, :, 0:DH], c.ps[:, 1, 0:R_HEADS * DH].rearrange(
                        "p (h d) -> p h d", h=R_HEADS)).then_inc(x_ready, 1)

                for b in range(5):
                    mask_pairs(0, b)
                a_values(0)
                for t in range(NT):
                    dve.wait_ge(a_copied, t + 1)
                    dve.wait_ge(x_ready, (STEPS + 1) * t + 1)
                    for i in range(STEPS):
                        if i < STEPS - 1:
                            dve.wait_ge(nt_done, (STEPS - 1) * t + i + 1)
                            nc.vector.tensor_copy(power_t[:, i % 2], c.ps[:, 2, :].rearrange(
                                "p (h n) -> p h n", h=R_HEADS)).then_inc(nt_copied, 1)
                        dve.wait_ge(step_done, STEPS * t + i + 1)
                        x = X[t].rearrange("p h n -> p (h n)")
                        nc.vector.tensor_tensor(x, x, c.ps[:, 0, :], ALU.add).then_inc(x_ready, 1)
                        if t + 1 < NT:
                            for b in {2: (0, 1), 3: (2, 3), 4: (4,)}.get(i, ()):
                                mask_pairs(t + 1, b)
                        dve.wait_ge(x_ready, (STEPS + 1) * t + i + 2)
                    if t + 1 < NT:
                        a_values(t + 1)
                    dve.wait_ge(local_done, 4 * t + 1)
                    nc.vector.tensor_tensor(r_prime[:, :, t * P:(t + 1) * P],
                                            c.ps[:, 6, 0:2 * P].rearrange("p (j n) -> p j n", j=2),
                                            f_r[:, :, t * P:(t + 1) * P], ALU.add).then_inc(r_copied, 1)
                dve.wait_ge(local_copied, 3 * NT)
                ch.wait()
                dve.sem_inc(state_ready, 1)
                for n in range(NCH):
                    if n:
                        dve.wait_ge(state_ready, n + 1)
                    end = (n + 1) * CHUNK
                    ch.link(nc.vector.tensor_tensor(carried[:, :, :], state[:, n, :, :], GH[:, n, :, DH:P], ALU.add))
                    for j in range(2):
                        ch.mark(nc.vector.tensor_scalar(carried[:, j, :], carried[:, j, :], decay[:, j, end - 1:end], None, ALU.mult))
                    ch.wait()
                    dve.wait_ge(state_done, n + 1)
                    for j in range(2):
                        ch.mark(nc.vector.scalar_tensor_tensor(
                            out=state[:, n + 1, j, :], in0=c.ps[:, 6 + n % 2, j * DH:(j + 1) * DH],
                            scalar=decay[:, j, end - 1:end], in1=carried[:, j, :], op0=ALU.mult, op1=ALU.add))
                    ch.wait()
                    dve.sem_inc(state_ready, 1)
                for j in range(2):
                    dve.wait_ge(y_state, 2 * (NCH - 1) + j + 1)
                    nc.vector.tensor_tensor(y[:, j, :], y[:, j, :], c.ps[:, j, :], ALU.add).then_inc(y_ready, 1)
                dve.wait_ge(y_ready, 2)
                for j in range(2):
                    dve.wait_ge(mean_done, j + 1)
                    nc.vector.scalar_tensor_tensor(out=y[:, j, :], in0=c.ps[:, 2 + j, :], scalar=-1.0 / DH,
                                                   in1=y[:, j, :], op0=ALU.mult, op1=ALU.add).then_inc(centred, 1)
                dve.wait_ge(centred, 2)
                dve.wait_ge(c_squared, 2)
                for j in range(2):
                    dve.wait_ge(var_root, j + 1)
                    ch.link(nc.vector.reciprocal(cum[:, j, :], cum[:, j, :]))
                    ch.link(nc.vector.scalar_tensor_tensor(out=y[:, j, :], in0=y[:, j, :], scalar=vcol("ln_w", j),
                                                           in1=cum[:, j, :], op0=ALU.mult, op1=ALU.mult))
                    ch.link(nc.vector.scalar_tensor_tensor(out=y[:, j, :], in0=y[:, j, :], scalar=vcol("ln_b", j),
                                                           in1=kk[:, j, :], op0=ALU.add, op1=ALU.add))
                    ch.link(nc.vector.tensor_tensor(c.y[:, 6 + j, :], y[:, j, :], gate[:, j, :], ALU.mult))


SECOND_TILES = 18
A_Q, A_K, A_V, B_Q, B_K, B_V = 0, 4, 5, 6, 10, 14
SPAN = 2 * S - P


def operands_of(h):
    half = lambda i: slice(DH * (i % 2), DH * (i % 2) + DH)
    if h < HEADS:
        g = h // GROUP
        return A_Q + h // 2, half(h), A_K, half(g), g, g
    b = h - HEADS
    return B_Q + b // 2, half(h), B_K + b // 2, half(h), HEADS // GROUP + b, HEADS // GROUP + b


NORM_A = [(A_Q + t, "qa") for t in range(4)] + [(A_K, "ka")]
NORM_B = [tile for t in range(4) for tile in ((B_Q + t, "qb"), (B_K + t, "kb"))]


def widen_head_factors(nc, c, wide, i):
    return nc.scalar.copy(wide[:, i % 2, :, :, :], c.head_inv[:, i, :, :].unsqueeze(3).to_broadcast([P, NT, 2, DH]))


def spread_head_factors(nc, c, bank, wide, i):
    for n in range(NT):
        m = nc.tensor.transpose(c.ps[:, bank, n * P:(n + 1) * P], wide[:, i % 2, n, :, :], c.mat["ident"])
    return m


def head_norm_stage(nc, c):
    tiles = NORM_A + NORM_B
    NA = len(NORM_A)
    with Stage(nc, c, "headnorm") as st:
        sq, root = st.sb("sq", [P, 2, S]), st.sb("root", [P, len(tiles), NT, 2])
        turned_sin, rotated = st.sb("turned_sin", [P, 2, S]), st.sb("rotated", [P, 2, S])
        wide = st.sb("wide", [P, 2, NT, 2, DH])
        squared, summed, rooted, inverted = st.sem("squared"), st.sem("summed"), st.sem("rooted"), st.sem("inverted")
        widened = st.sem("widened")
        spread, normed, turned, roped = st.sem("spread"), st.sem("normed"), st.sem("turned"), st.sem("roped")
        cos_done, sin_done = st.sem("cos_done"), st.sem("sin_done")
        v_turned, v_copied, ones_set = st.sem("v_turned"), st.sem("v_copied"), st.sem("ones_set")
        with nc.Block() as block:
            @block.gpsimd
            def _(pool):
                st.zero_stale()
                nc.gpsimd.memset(c.v_tok[:, :, :, DH:DH + 1], 1.0).then_inc(ones_set, 1)
                pool.wait_ge(ones_set, 1)

            @block.tensor
            def _(pe):
                def sums(i):
                    pe.wait_ge(squared, i + 1)
                    for n in range(NT):
                        at = (i * NT + n) * 2
                        m = nc.tensor.matmul(c.ps[:, 0, at:at + 2], sq[:, i % 2, n * P:(n + 1) * P],
                                             c.mats[:, MATS.index("halves"), 0:P:DH], start=True, stop=True)
                    m.then_inc(summed, 1)

                def values(j):
                    if j >= 2:
                        pe.wait_ge(v_copied, j - 1)
                    for n in range(NT):
                        m = nc.tensor.transpose(c.ps[:, 6 + j % 2, n * P:(n + 1) * P],
                                                c.proj[:, A_V if j == 0 else B_V + j - 1, n * P:(n + 1) * P],
                                                c.mat["ident"])
                    m.then_inc(v_turned, 1)

                def factors(t):
                    pe.wait_ge(widened, t + 1)
                    if t >= 2:
                        pe.wait_ge(normed, t - 1)
                    spread_head_factors(nc, c, 1 + t % 2, wide, t).then_inc(spread, 1)

                def partner(t):
                    pe.wait_ge(normed, t + 1)
                    if t >= 2:
                        pe.wait_ge(sin_done, t - 1)
                    nc.tensor.matmul(c.ps[:, 3 + t % 2, :], c.mat["axial_turn"], c.proj[:, t, :], start=True,
                                     stop=True).then_inc(turned, 1)

                for i in range(NA):
                    sums(i)
                for j in range(2):
                    values(j)
                pe.wait_ge(rooted, 1)
                for i in range(NA, len(tiles)):
                    sums(i)
                    t = i - NA
                    if t < NA:
                        factors(t)
                    if 1 <= t <= NA:
                        partner(t - 1)
                for j in range(2, 5):
                    values(j)

            @block.scalar
            def _(act):
                def square(i):
                    if i >= 2:
                        act.wait_ge(summed, i - 1)
                    nc.scalar.activation(sq[:, i % 2, :], c.proj[:, tiles[i][0], :], ACT.Square).then_inc(squared, 1)

                def roots(first, last):
                    act.wait_ge(summed, last)
                    nc.scalar.activation(root[:, first:last, :, :], c.ps[:, 0, first * 2 * NT:last * 2 * NT], ACT.Sqrt,
                                         bias=c.eps[:, 0:1], scale=1.0 / DH).then_inc(rooted, 1)

                def values(j):
                    act.wait_ge(v_turned, j + 1)
                    dst = c.v_tok[:, :, 2 * j:2 * j + 2, 0:DH]
                    nc.scalar.copy(dst, c.ps[:, 6 + j % 2, :].rearrange("p (n h d) -> p n h d", n=NT, h=2)).then_inc(v_copied, 1)

                for i in range(NA):
                    square(i)
                roots(0, NA)
                values(0)
                for i in range(NA, len(tiles)):
                    square(i)
                    t = i - NA
                    if t < NA:
                        if t == 0:
                            act.wait_ge(inverted, 1)
                        if t >= 2:
                            act.wait_ge(spread, t - 1)
                        widen_head_factors(nc, c, wide, t).then_inc(widened, 1)
                values(1)
                roots(NA, len(tiles))
                for j in range(2, 5):
                    values(j)

            @block.vector
            def _(dve):
                dve.wait_ge(rooted, 1)
                nc.vector.reciprocal(c.head_inv[:, 0:NA, :, :], root[:, 0:NA, :, :]).then_inc(inverted, 1)

                def norm(t):
                    tile, gain = tiles[t]
                    dve.wait_ge(spread, t + 1)
                    nc.vector.scalar_tensor_tensor(out=c.proj[:, tile, :], in0=c.proj[:, tile, :],
                                                   scalar=c.vec2[:, VEC2[gain]:VEC2[gain] + 1], in1=c.ps[:, 1 + t % 2, :],
                                                   op0=ALU.mult, op1=ALU.mult).then_inc(normed, 1)

                norm(0)
                for t in range(NA):
                    if t + 1 < NA:
                        norm(t + 1)
                    dve.wait_ge(normed, t + 1)
                    if t >= 2:
                        dve.wait_ge(roped, t - 1)
                    nc.vector.tensor_tensor(rotated[:, t % 2, :], c.proj[:, t, :], c.rope[:, 0, :],
                                            ALU.mult).then_inc(cos_done, 1)
                    dve.wait_ge(turned, t + 1)
                    nc.vector.tensor_tensor(turned_sin[:, t % 2, :], c.ps[:, 3 + t % 2, :], c.rope[:, 1, :],
                                            ALU.mult).then_inc(sin_done, 1)
                    dve.wait_ge(sin_done, t + 1)
                    nc.vector.tensor_tensor(c.proj[:, t, :], rotated[:, t % 2, :], turned_sin[:, t % 2, :],
                                            ALU.add).then_inc(roped, 1)
                dve.wait_ge(rooted, 2)
                nc.vector.reciprocal(c.head_inv[:, NA:, :, :], root[:, NA:, :, :]).then_inc(inverted, 1)


def full_attention_stage(nc, c, biases):
    TOTAL = 2 * HEADS
    with Stage(nc, c, "attn2") as st:
        ident_r, ones_r = st.sb("ident_r", [P, P], F32R), st.sb("ones_r", [P, P], F32R)
        bias = st.sb("bias", [P, 2, SPAN])
        bias_hi, bias_lo = st.sb("bias_hi", [P, 3, SPAN], F32R), st.sb("bias_lo", [P, 3, SPAN], F32R)
        probs = st.sb("probs", [P, 2, NT, S])
        diag = st.sb("diag", [P, 2, NT, P], F32R)
        top, neg_top = st.sb("top", [P, 2, NT]), st.sb("neg_top", [P, 2, NT], F32R)
        share = st.sb("share", [P, 2, NT, 1])
        o_tok = st.sb("o_tok", [P, 2, NT, 2, DH])
        wide = st.sb("wide", [P, 2, NT, 2, DH])
        loaded = [st.sem(f"bias_loaded{b}") for b in range(2)]
        consts, bias_hi_ready, bias_ready = st.sem("consts"), st.sem("bias_hi_ready"), st.sem("bias_ready")
        rough, rough_read, tops, diag_ready = st.sem("rough"), st.sem("rough_read"), st.sem("tops"), st.sem("diag_ready")
        scored, exps, pv_done, inverted, normed = st.sem("scored"), st.sem("exps"), st.sem("pv_done"), st.sem("inverted"), st.sem("normed")
        transposed, out_copied = st.sem("transposed"), st.sem("out_copied")
        widened, spread, b_normed = st.sem("widened"), st.sem("spread"), st.sem("b_normed")
        q_hi, q_lo, k_both = (st.sb(n, [P, 3, S], F32R) for n in ("q_hi", "q_lo", "k_both"))
        firsts, operands = st.sem("first_parts"), st.sem("operands")

        def new_keys(h):
            return operands_of(h)[4] if h == 0 or operands_of(h)[4] != operands_of(h - 1)[4] else None

        def parts_by(h):
            return 2 * (h + 1) + operands_of(h)[4] + 1

        def last_with_keys(g):
            return max(h for h in range(TOTAL) if operands_of(h)[4] == g)

        def bias_of(parts, h, i):
            return parts[:, (h - HEADS) % 3, (NT - 1 - i) * P:(NT - 1 - i) * P + S]

        with nc.Block() as block:
            @block.sync
            def _(sp):
                for b in range(HEADS):
                    if b >= 2:
                        sp.wait_ge(bias_ready, b - 1)
                    sp.dma_start(bias[:, b % 2, :], biases[b]).then_inc(loaded[b % 2], 16)

            @block.gpsimd
            def _(pool):
                st.zero_stale()

            @block.tensor
            def _(pe):
                def rough_scores(h, i):
                    u, keys = NT * h + i, operands_of(h)[4] % 3
                    if i == 0:
                        pe.wait_ge(operands, parts_by(h))
                        if h >= HEADS:
                            pe.wait_ge(bias_hi_ready, h - HEADS + 1)
                    if u >= 2:
                        pe.wait_ge(rough_read, u - 1)
                    m = nc.tensor.matmul(c.ps[:, u % 2, :], q_hi[:, h % 3, i * P:(i + 1) * P], k_both[:, keys, :],
                                         start=True, stop=(h < HEADS))
                    if h >= HEADS:
                        m = nc.tensor.matmul(c.ps[:, u % 2, :], ident_r[:, :], bias_of(bias_hi, h, i), start=False, stop=True)
                    m.then_inc(rough, 1)

                def scores(h, j):
                    v = NT * h + j
                    o, k = c.ps[:, 2 + v % 3, :], k_both[:, operands_of(h)[4] % 3, j * P:(j + 1) * P]
                    if v >= 3:
                        pe.wait_ge(exps, v - 2)
                    nc.tensor.matmul(o, k, q_hi[:, h % 3, :], start=True, stop=False)
                    nc.tensor.matmul(o, k, q_lo[:, h % 3, :], start=False, stop=False)
                    if h >= HEADS:
                        if j == 0:
                            pe.wait_ge(bias_ready, h - HEADS + 1)
                        nc.tensor.matmul(o, ident_r[:, :], bias_of(bias_hi, h, j), start=False, stop=False)
                        nc.tensor.matmul(o, ident_r[:, :], bias_of(bias_lo, h, j), start=False, stop=False)
                    if j == 0:
                        pe.wait_ge(diag_ready, h + 1)
                    nc.tensor.matmul(o, ones_r[:, :], diag[:, h % 2, :, :], start=False, stop=True).then_inc(scored, 1)

                def values(h):
                    v = operands_of(h)[5]
                    pe.wait_ge(exps, NT * (h + 1))
                    if h >= 2:
                        pe.wait_ge(normed, h - 1)
                    for n in range(NT):
                        at = n * (DH + 1)
                        for j in range(NT):
                            m = nc.tensor.matmul(c.ps[:, 5 + h % 2, at:at + DH + 1], probs[:, h % 2, j, n * P:(n + 1) * P],
                                                 c.v_tok[:, j, v, :], start=(j == 0), stop=(j == NT - 1))
                    m.then_inc(pv_done, 1)

                def turn_back(t):
                    pe.wait_ge(normed, 2 * t + 2)
                    if t:
                        pe.wait_ge(out_copied, t)
                    pe.wait_ge(b_normed, min(2 * t + 4, HEADS))
                    for n in range(NT):
                        m = nc.tensor.transpose(c.ps[:, 7, n * P:(n + 1) * P], o_tok[:, t % 2, n, :, :], c.mat["ident"])
                    m.then_inc(transposed, 1)

                pe.wait_ge(consts, 2)
                for i in range(NT):
                    rough_scores(0, i)
                for h in range(TOTAL):
                    if h < HEADS:
                        if h >= 4:
                            pe.wait_ge(out_copied, (h - 2) // 2)
                        if h:
                            pe.wait_ge(b_normed, h)
                        pe.wait_ge(widened, h + 1)
                        spread_head_factors(nc, c, 7, wide, len(NORM_A) + h).then_inc(spread, 1)
                    for i in range(NT):
                        if h + 1 < TOTAL:
                            rough_scores(h + 1, i)
                        scores(h, i)
                        if i == 1 and h >= 3 and h % 2:
                            turn_back((h - 3) // 2)
                    if h:
                        values(h - 1)
                values(TOTAL - 1)
                turn_back(HEADS - 1)

            @block.scalar
            def _(act):
                nc.scalar.copy(ident_r[:, :], c.mat["ident"]).then_inc(consts, 1)
                nc.scalar.copy(ones_r[:, :], c.mat["ones"]).then_inc(consts, 1)

                def widen(b):
                    if b >= 2:
                        act.wait_ge(spread, b - 1)
                    widen_head_factors(nc, c, wide, len(NORM_A) + b).then_inc(widened, 1)

                def copy_out(t):
                    act.wait_ge(transposed, t + 1)
                    nc.scalar.copy(c.y[:, t, :], c.ps[:, 7, :]).then_inc(out_copied, 1)

                def first_parts(h):
                    q, q_rows, k, k_rows, g, _ = operands_of(h)
                    if h >= HEADS:
                        act.wait_ge(b_normed, 2 * ((h - HEADS) // 2) + 2)
                    if h >= 3:
                        act.wait_ge(scored, NT * (h - 2))
                    for half in (slice(0, DH), slice(DH, P)):
                        nc.scalar.copy(q_hi[half, h % 3, :], c.proj[q_rows, q, :]).then_inc(firsts, 1)
                    if new_keys(h) is not None:
                        if g >= 3:
                            act.wait_ge(scored, NT * (last_with_keys(g - 3) + 1))
                        nc.scalar.copy(k_both[k_rows, g % 3, :], c.proj[k_rows, k, :]).then_inc(firsts, 1)

                first_parts(0)
                first_parts(1)
                widen(0)
                for h in range(TOTAL):
                    if h + 1 < HEADS:
                        widen(h + 1)
                    if h + 2 < TOTAL:
                        first_parts(h + 2)
                    b = h + 2 - HEADS
                    if 0 <= b < HEADS:
                        act.wait_ge(loaded[b % 2], 16 * (b // 2 + 1))
                        if b >= 3:
                            act.wait_ge(scored, NT * (HEADS + b - 2))
                        nc.scalar.copy(bias_hi[:, b % 3, :], bias[:, b % 2, :]).then_inc(bias_hi_ready, 1)
                    for j in range(NT):
                        act.wait_ge(scored, NT * h + j + 1)
                        if h >= 2:
                            act.wait_ge(pv_done, h - 1)
                        nc.scalar.activation(probs[:, h % 2, j, :], c.ps[:, 2 + (NT * h + j) % 3, :], ACT.Exp,
                                             scale=DH ** -0.5).then_inc(exps, 1)
                        if j == 2 and h >= 3 and h % 2:
                            copy_out((h - 3) // 2)
                copy_out(HEADS - 1)

            @block.vector
            def _(dve):
                def maximum(h, i):
                    u = NT * h + i
                    dve.wait_ge(rough, u + 1)
                    nc.vector.tensor_reduce(top[:, h % 2, i:i + 1], c.ps[:, u % 2, :], AX, ALU.max).then_inc(rough_read, 1)

                def diagonal(h):
                    dve.wait_ge(rough_read, NT * (h + 1))
                    nc.vector.tensor_scalar(neg_top[:, h % 2, :], top[:, h % 2, :], -1.0, None, ALU.mult).then_inc(tops, 1)
                    dve.wait_ge(tops, h + 1)
                    if h >= 2:
                        dve.wait_ge(scored, NT * (h - 1))
                    nc.vector.tensor_tensor(diag[:, h % 2, :, :], c.mat["ident"].unsqueeze(1).to_broadcast([P, NT, P]),
                                            neg_top[:, h % 2, :].bitcast(F32).unsqueeze(2).to_broadcast([P, NT, P]),
                                            ALU.mult).then_inc(diag_ready, 1)

                def normalise(h):
                    t = h // 2
                    dve.wait_ge(pv_done, h + 1)
                    o = c.ps[:, 5 + h % 2, 0:NT * (DH + 1)].rearrange("p (n d) -> p n d", n=NT)
                    nc.vector.reciprocal(share[:, h % 2, :, :], o[:, :, DH:DH + 1]).then_inc(inverted, 1)
                    dve.wait_ge(inverted, h + 1)
                    if t >= 2:
                        dve.wait_ge(transposed, t - 1)
                    nc.vector.tensor_tensor(o_tok[:, t % 2, :, h % 2, :], o[:, :, 0:DH],
                                            share[:, h % 2, :, :].to_broadcast([P, NT, DH]), ALU.mult).then_inc(normed, 1)

                def rests(h):
                    q, q_rows, k, k_rows, g, _ = operands_of(h)
                    dve.wait_ge(firsts, parts_by(h))
                    for half in (slice(0, DH), slice(DH, P)):
                        nc.vector.tensor_tensor(q_lo[half, h % 3, :], c.proj[q_rows, q, :], q_hi[q_rows, h % 3, :].bitcast(F32),
                                                ALU.subtract).then_inc(operands, 1)
                    if new_keys(h) is not None:
                        other = slice(DH - k_rows.start, P - k_rows.start)
                        nc.vector.tensor_tensor(k_both[other, g % 3, :], c.proj[k_rows, k, :],
                                                k_both[k_rows, g % 3, :].bitcast(F32), ALU.subtract).then_inc(operands, 1)

                rests(0)
                rests(1)
                for i in range(NT):
                    maximum(0, i)
                diagonal(0)
                for h in range(TOTAL):
                    if h < HEADS:
                        tile, gain = NORM_B[h]
                        dve.wait_ge(spread, h + 1)
                        nc.vector.scalar_tensor_tensor(out=c.proj[:, tile, :], in0=c.proj[:, tile, :],
                                                       scalar=c.vec2[:, VEC2[gain]:VEC2[gain] + 1], in1=c.ps[:, 7, :],
                                                       op0=ALU.mult, op1=ALU.mult).then_inc(b_normed, 1)
                    for i in range(NT):
                        if h + 1 < TOTAL:
                            maximum(h + 1, i)
                        if i == 1:
                            if h >= 2:
                                normalise(h - 2)
                            if h + 2 < TOTAL:
                                rests(h + 2)
                    if h + 1 < TOTAL:
                        diagonal(h + 1)
                    b = h + 2 - HEADS
                    if 0 <= b < HEADS:
                        dve.wait_ge(bias_hi_ready, b + 1)
                        nc.vector.tensor_tensor(bias_lo[:, b % 3, :], bias[:, b % 2, :], bias_hi[:, b % 3, :].bitcast(F32),
                                                ALU.subtract).then_inc(bias_ready, 1)
                normalise(TOTAL - 2)
                normalise(TOTAL - 1)


def second_out_stage(nc, c, w_out):
    HT = KD // 2
    with Stage(nc, c, "out2") as st:
        entry = Entry(st, c, c.y, c.vec2[:, VEC2["outa"]:], [tuple(range(HT)), tuple(range(HT, KD))], False)
        W = Weights(st)
        scaled = st.sb("scaled", [P, 2, 2, S])
        scaled_ready, freed, x_ready = st.sem("scaled"), st.sem("banks_read"), st.sem("x_ready")
        with nc.Block() as block:
            @block.sync
            def _(sp):
                for n in range(KD):
                    W.load(sp, 0, n, w_out[n])

            @block.gpsimd
            def _(pool):
                entry.gpsimd(pool, nc)

            @block.tensor
            def _(pe):
                half = lambda n: lambda k: (c.ps[:, 2 * n + k // HT, :], k % HT == 0, k % HT == HT - 1)
                first_products(pe, nc, c, W, entry, [half(n) for n in range(2)])
                entry.tensor_factor(pe, nc)
                for n in range(2, KD):
                    pe.wait_ge(W.lo_ready, n + 1)
                    pe.wait_ge(freed, 2 * (n - 1))
                    for k in range(KD):
                        for i, (w, h) in enumerate(W.terms(n, k, entry.hi[:, k, :], entry.lo[:, k, :])):
                            m = nc.tensor.matmul(c.ps[:, 2 * (n % 2) + k // HT, :], w, h, start=(k % HT == 0 and i == 0),
                                                 stop=(k % HT == HT - 1 and i == 2))
                    m.then_inc(W.done, 1)

            @block.scalar
            def _(act):
                first_scalar(act, nc, W, entry)
                for n in range(SLOTS, KD):
                    W.split_hi(act, nc, 0, n)

            @block.vector
            def _(dve):
                first_vector(dve, nc, W, entry)
                for j in range(KD):
                    dve.wait_ge(W.done, j + 1)
                    if j >= 2:
                        dve.wait_ge(x_ready, j - 1)
                    for g in range(2):
                        nc.vector.tensor_tensor(scaled[:, j % 2, g, :], c.ps[:, 2 * (j % 2) + g, :], entry.rs[:, g, :],
                                                ALU.mult).then_inc(freed, 1)
                    if SLOTS <= j + 3 < KD:
                        W.split_lo(dve, nc, 0, j + 3)
                    dve.wait_ge(freed, 2 * (j + 1))
                    nc.vector.tensor_tensor(scaled[:, j % 2, 0, :], scaled[:, j % 2, 0, :], scaled[:, j % 2, 1, :], ALU.add).then_inc(scaled_ready, 1)
                    dve.wait_ge(scaled_ready, j + 1)
                    nc.vector.tensor_tensor(c.x[:, j, :], c.x[:, j, :], scaled[:, j % 2, 0, :], ALU.add).then_inc(x_ready, 1)


def conv_ffn_stage(nc, c, w_up, w_down, out):
    with Stage(nc, c, "convffn") as st:
        entry = Entry(st, c, c.x, c.vec2[:, VEC2["norm2"]:], ALL, False)
        W = Weights(st)
        a_hi, a_lo = st.sb("a_hi", [P, KF, S], F32R), st.sb("a_lo", [P, KF, S], F32R)
        conv, u = c.y[:, 0:4, :], c.y[:, 4:6, :]
        freed, middle, side, conv_ready = st.sem("banks_read"), st.sem("middle_tap"), st.sem("side_tap"), st.sem("conv_ready")
        gelu_ready = st.sem("gelu_ready")
        product, act_hi, act_ready = st.sem("product"), st.sem("act_hi_ready"), st.sem("act_ready")
        stored = st.sem("stored")
        tap = lambda it, n, i: c.vec2[:, bass.ds(it * 4 + (VEC2["conv"] + 4 * n + i), 1)]
        with nc.Block() as block:
            @block.sync
            def _(sp):
                load_ffn(sp, W, lambda n: w_up[n], lambda n: w_down[n])
                with sp.Fori(0, KD) as j:
                    sp.wait_ge(freed, j + (UP + 1))
                    sp.dma_start(out[:, j, :], c.x[:, j, :]).then_inc(stored, 16)
                sp.wait_ge(stored, 16 * KD)

            @block.gpsimd
            def _(pool):
                entry.gpsimd(pool, nc)

            @block.tensor
            def _(pe):
                ffn_tensor(pe, nc, c, W, entry, a_hi, a_lo, act_ready, freed)

            @block.scalar
            def _(act):
                first_scalar(act, nc, W, entry)

                def middle_tap(it, n):
                    act.wait_ge(freed, it + (n + 1))
                    nc.scalar.activation(conv[:, n % 4, :], u[:, n % 2, :], ACT.Identity, bias=tap(it, n, 3),
                                         scale=tap(it, n, 1)).then_inc(middle, 1)

                def gelu(it, q):
                    act.wait_ge(conv_ready, it * 2 + (2 * q + 1))
                    nc.scalar.activation(conv[:, 2 * q % 4, :], conv[:, 2 * q % 4, :],
                                         ACT.Gelu_apprx_tanh).then_inc(gelu_ready, 1)

                def first_part(it, q):
                    act.wait_ge(product, it + (q + 1))
                    nc.scalar.copy(a_hi[:, it + q, :], conv[:, 2 * q % 4, :]).then_inc(act_hi, 1)

                middle_tap(0, 0)
                middle_tap(0, 1)
                gelu(0, 0)
                W.split_hi(act, nc, 0, SLOTS)
                middle_tap(0, 2)
                first_part(0, 0)
                with act.Fori(0, LOOPS) as it:
                    for q in (1, 2):
                        W.split_hi(act, nc, it * SLOTS, 2 * q + 3)
                        middle_tap(it * SLOTS, 2 * q + 1)
                        gelu(it * 2, q)
                        W.split_hi(act, nc, it * SLOTS, 2 * q + 4)
                        middle_tap(it * SLOTS, 2 * q + 2)
                        first_part(it * 2, q)
                middle_tap(0, UP - 1)
                gelu(0, KF - 1)
                first_part(0, KF - 1)
                down_splits(act, lambda it, n, w: W.split_hi(act, nc, it, n, w), lambda it, j, products: None)

            @block.vector
            def _(dve):
                first_vector(dve, nc, W, entry)

                def scale(it, n):
                    dve.wait_ge(W.done, it + (n + 1))
                    nc.vector.tensor_tensor(u[:, n % 2, :], c.ps[:, n % SLOTS, :], entry.rs[:, 0, :],
                                            ALU.mult).then_inc(freed, 1)

                def side_taps(it, n):
                    d, s = conv[:, n % 4, :], u[:, n % 2, :]
                    dve.wait_ge(middle, it + (n + 1))
                    nc.vector.scalar_tensor_tensor(out=d[:, 1:S], in0=s[:, 0:S - 1], scalar=tap(it, n, 0), in1=d[:, 1:S],
                                                   op0=ALU.mult, op1=ALU.add).then_inc(side, 1)
                    dve.wait_ge(side, it + (n + 1))
                    nc.vector.scalar_tensor_tensor(out=d[:, 0:S - 1], in0=s[:, 1:S], scalar=tap(it, n, 2),
                                                   in1=d[:, 0:S - 1], op0=ALU.mult, op1=ALU.add).then_inc(conv_ready, 1)

                def multiply(it, q):
                    gate, value = conv[:, 2 * q % 4, :], conv[:, (2 * q + 1) % 4, :]
                    dve.wait_ge(gelu_ready, it + (q + 1))
                    dve.wait_ge(conv_ready, it * 2 + (2 * q + 2))
                    nc.vector.tensor_tensor(gate, gate, value, ALU.mult).then_inc(product, 1)

                def rest(it, q):
                    dve.wait_ge(act_hi, it + (q + 1))
                    nc.vector.tensor_tensor(a_lo[:, it + q, :], conv[:, 2 * q % 4, :], a_hi[:, it + q, :].bitcast(F32),
                                            ALU.subtract).then_inc(act_ready, 1)

                scale(0, 0)
                scale(0, 1)
                side_taps(0, 0)
                side_taps(0, 1)
                W.split_lo(dve, nc, 0, SLOTS)
                scale(0, 2)
                multiply(0, 0)
                side_taps(0, 2)
                with dve.Fori(0, LOOPS) as it:
                    for q in (1, 2):
                        W.split_lo(dve, nc, it * SLOTS, 2 * q + 3)
                        scale(it * SLOTS, 2 * q + 1)
                        rest(it * 2, q - 1)
                        side_taps(it * SLOTS, 2 * q + 1)
                        W.split_lo(dve, nc, it * SLOTS, 2 * q + 4)
                        scale(it * SLOTS, 2 * q + 2)
                        multiply(it * 2, q)
                        side_taps(it * SLOTS, 2 * q + 2)
                scale(0, UP - 1)
                rest(0, KF - 2)
                side_taps(0, UP - 1)
                multiply(0, KF - 1)
                rest(0, KF - 1)

                def outputs(it, j, products):
                    dve.wait_ge(W.done, it * SLOTS + products)
                    nc.vector.tensor_tensor(c.x[:, it + j, :], c.x[:, it + j, :], c.ps[:, j % 2, :],
                                            ALU.add).then_inc(freed, 1)

                down_splits(dve, lambda it, n, w: W.split_lo(dve, nc, it, n, w), outputs)


def build(nc, a, out):
    c = Chip()
    with ExitStack() as ctx:
        def sb(name, shape, dt=F32):
            return ctx.enter_context(nc.sbuf_tensor(name, shape, dt))

        c.ps = ctx.enter_context(nc.psum_tensor("ps", [P, 8, S], F32))
        c.x, c.y = sb("x", [P, KD, S]), sb("y", [P, KD, S])
        c.mats = sb("mats", [P, len(MATS), P])
        c.mat = {m: c.mats[:, i, :] for i, m in enumerate(MATS)}
        c.vecs, c.vec, c.vec2 = sb("vecs", [P, DEPTH, NVEC]), sb("vec", [P, NVEC]), sb("vec_2", [P, NVEC2])
        c.eps = sb("eps", [P, 2])
        c.rope = sb("rope", [P, 2, S])
        start_stage(nc, c, a)
        settle(nc, c)
        with nc.Fori(0, DEPTH) as l:
            def this_layers_vectors():
                return nc.scalar.copy(c.vec[:, :], c.vecs[:, bass.ds(l, 1), :].rearrange("p l v -> p (l v)"))

            ffn_stage(nc, c, "ffn1", l, a["w_ffn1_in"], a["w_ffn1_out"], c.vec[:, VEC["ffn1_pre"]:],
                      VEC["ffn1_post"], this_layers_vectors)
            with ExitStack() as mix:
                c.proj = mix.enter_context(nc.sbuf_tensor("proj", [P, MIX_TILES, S], F32))
                c.gates = mix.enter_context(nc.sbuf_tensor("gates", [4, 2, S], F32))
                proj_stage(nc, c, "mixproj", lambda n: a["w_in"][l, n], MIX_TILES,
                           c.vec[:, VEC["mix_pre"]:], True)
                window_attention_stage(nc, c, a["window_masks"])
                mlstm_stage(nc, c, a["selectors"])
                rwkv_stage(nc, c, l, a["loras"], a["chunk_masks"], a["reset"])
            mix_out_stage(nc, c, l, a["w_out"])
            ffn_stage(nc, c, "ffn2", l, a["w_ffn2_in"], a["w_ffn2_out"], c.vec[:, VEC["ffn2_pre"]:],
                      VEC["ffn2_post"])
            ple_stage(nc, c, l, a["w_ple_gate"], a["w_ple_proj"], a["p"])
            settle(nc, c)
        with ExitStack() as second:
            def sb2(name, shape, dt=F32):
                return second.enter_context(nc.sbuf_tensor(name, shape, dt))

            c.proj = sb2("proj_2", [P, SECOND_TILES, S])
            proj_stage(nc, c, "proj2", lambda n: a["w_in_2"][n], SECOND_TILES, c.vec2[:, VEC2["norm1"]:], False,
                       a["axial"])
            c.v_tok = sb2("v_tok", [P, NT, 2 + HEADS, DH + 1])
            c.head_inv = sb2("head_inv", [P, len(NORM_A + NORM_B), NT, 2])
            head_norm_stage(nc, c)
            full_attention_stage(nc, c, a["biases"])
        second_out_stage(nc, c, a["w_out_2"])
        conv_ffn_stage(nc, c, a["w_up_2"], a["w_down_2"], out)
        settle(nc, c)


def columns(w):
    k, n = w.shape
    return np.ascontiguousarray(w.reshape(k // P, P, n // P, P).transpose(2, 1, 0, 3)).reshape(n // P, P, -1)


def pieces(w):
    t = columns(w)
    out = np.zeros((t.shape[0], len(PIECES), P, PIECE), np.float32)
    for i, (k0, ks) in enumerate(PIECES):
        out[:, i, :, :ks * P] = t[:, :, k0 * P:(k0 + ks) * P]
    return out.reshape(-1, P, PIECE)


def gate_up(w):
    t = columns(w)
    n = t.shape[0] // 2
    return np.ascontiguousarray(np.stack([t[:n], t[n:]], 1)).reshape(2 * n, P, -1)


def per_partition(v):
    return v.reshape(-1, P).T


def shape_matrices():
    i = np.arange(P)
    row, col = i[:, None], i[None, :]
    same_half, same_chunk = row // DH == col // DH, row // CHUNK == col // CHUNK
    turn = np.zeros((P, P), np.float32)
    axial = np.zeros((P, P), np.float32)
    for m in range(P):
        d = m % DH
        if d < ROPE_DIM // 2:
            turn[m + ROPE_DIM // 2, m] = -1.0
        elif d < ROPE_DIM:
            turn[m - ROPE_DIM // 2, m] = 1.0
        if d % 32 < 16:
            axial[m + 16, m] = -1.0
        else:
            axial[m - 16, m] = 1.0
    m = {"ident": row == col, "ones": (row >= 0) & (col >= 0), "halves": same_half, "rope_turn": turn,
         "swap": (row + DH) % P == col, "axial_turn": axial, "strict_low": same_chunk & (row > col),
         "strict_up": same_chunk & (row < col), "incl_up": same_chunk & (row <= col), "causal": row <= col}
    return np.ascontiguousarray(np.stack([np.asarray(m[n], np.float32) for n in MATS], 1))


def layouts(inputs):
    f = {n: np.asarray(v) for n, v in inputs.items()}
    a = {}
    feature_tiles = lambda t: np.ascontiguousarray(t.T.reshape(-1, P, S).transpose(1, 0, 2))
    each = lambda fn, w: np.stack([fn(w[l]) for l in range(DEPTH)])
    a["x"] = feature_tiles(f["x"][0])
    a["p"] = np.stack([feature_tiles(f["p"][l, 0]) for l in range(DEPTH)])
    a["mats"] = shape_matrices()
    for n in ("ffn1", "ffn2"):
        a[f"w_{n}_in"] = each(gate_up, f[f"w_{n}_in"])
        a[f"w_{n}_out"] = each(pieces, f[f"w_{n}_out"])
    a["w_ple_gate"] = each(columns, f["w_ple_gate"])
    a["w_ple_proj"] = each(lambda w: np.ascontiguousarray(columns(w).transpose(1, 0, 2)), f["w_ple_proj"])
    vecs = np.zeros((DEPTH, P, NVEC), np.float32)
    for l in range(DEPTH):
        def put(name, cols):
            vecs[l, :cols.shape[0], VEC[name]:VEC[name] + cols.shape[1]] = cols
        for n in ("ffn1", "mix", "ffn2", "ple"):
            put(n + "_pre", per_partition(f[f"ln_{n}_pre"][l]))
            put(n + "_post", per_partition(f[f"ln_{n}_post"][l]))
        for t in range(4):
            put_at = f["mlstm_conv"][l][t]
            vecs[l, :, VEC["conv"] + 4 * t:VEC["conv"] + 4 * t + 4] = per_partition(put_at)
        put("m_norm", per_partition(f["mlstm_norm"][l]))
        for n in ("mu", "w0", "a0", "k_k", "k_a", "ln_w", "ln_b"):
            put(n, per_partition(f["rwkv_" + n][l]))
        put("r_k", per_partition(f["rwkv_r_k"][l].reshape(-1)))
        put("sinks", np.broadcast_to(f["attn_sinks"][l], (P, 8)))
        put("i_bias", f["mlstm_i_bias"][l][:, None])
        put("f_bias", f["mlstm_f_bias"][l][:, None])
    a["vecs"] = np.ascontiguousarray(vecs.transpose(1, 0, 2))
    attn_cols, rwkv_at = 768, 768 + 1032
    pick = np.r_[rwkv_at:rwkv_at + 1024, 0:attn_cols + 1024]

    def gate_tile(w):
        t = np.zeros((D, P), np.float32)
        t[:, 0:4], t[:, 32:36] = w[:, rwkv_at - 8:rwkv_at - 4], w[:, rwkv_at - 4:rwkv_at]
        return t

    a["w_in"] = each(lambda w: columns(np.concatenate([w[:, pick], gate_tile(w)], 1)), f["w_in"])
    a["w_out"] = each(columns, f["w_out"])
    a["loras"] = np.stack([np.stack([np.concatenate([f["rwkv_w_up"][l], f["rwkv_a_up"][l]]), f["rwkv_g_up"][l]])
                           for l in range(DEPTH)])
    a["positions"] = np.broadcast_to(f["positions"].astype(np.int32, copy=False), (P, S))
    d = np.arange(P) % DH
    inv = 500000.0 ** (-2.0 * (d % (ROPE_DIM // 2)) / ROPE_DIM)
    a["inv_freq"] = np.where(d < ROPE_DIM, inv, 0.0).astype(np.float32)[:, None]
    lag = np.arange(P)[:, None] + WIN - np.arange(2 * WIN)[None, :]
    band = (lag >= 0) & (lag < WIN)
    blocks = np.stack([band & ((n > 0) | (np.arange(2 * WIN) >= WIN)) for n in range(NT)], 1)
    by_key = np.tile(np.concatenate([band[:, WIN:].T, band[:, :WIN].T], 1), (1, 2))
    a["window_masks"] = np.where(np.concatenate([blocks.reshape(P, 2, S), by_key[:, None]], 1), 0.0, NEG).astype(np.float32)
    sel = np.zeros((4, 6, P), np.float32)
    for h in range(4):
        sel[h, h] = 1.0
        sel[h, 4 + h // 2, DH * (h % 2):DH * (h % 2) + DH] = 1.0
    a["selectors"] = sel
    m = a["mats"]
    a["chunk_masks"] = np.stack([np.tile(m[:, MATS.index(n)], 2) for n in ("strict_low", "strict_up", "incl_up")], 1)
    a["reset"] = np.broadcast_to((np.arange(S) % CHUNK != 0).astype(np.float32), (P, S))
    a["w_in_2"], a["w_out_2"] = columns(f["w_in_2"]), columns(f["w_out_2"])
    a["w_up_2"], a["w_down_2"] = gate_up(f["w_up_2"]), pieces(f["w_down_2"])
    v2 = np.zeros((P, NVEC2), np.float32)
    for name, n in (("norm1", "norm1_g_2"), ("outa", "outa_norm_g_2"), ("outb", "outb_norm_g_2"), ("norm2", "norm2_g_2")):
        cols = per_partition(f[n])
        v2[:, VEC2[name]:VEC2[name] + cols.shape[1]] = cols
    for name in ("qa", "ka", "qb", "kb"):
        v2[:, VEC2[name]] = np.concatenate([f[f"{name}_norm_g_2"]] * 2)
    taps = np.concatenate([f["conv_w_2"], f["conv_b_2"][None]])
    v2[:, VEC2["conv"]:] = taps.reshape(4, 2, KF, P).transpose(3, 2, 1, 0).reshape(P, -1)
    a["vecs_2"] = v2
    token, d = np.arange(S), np.arange(P) % DH
    place = np.where(d[:, None] < 32, token[None] // 64, token[None] % 64)
    angle = place * (10000.0 ** (-2.0 * (d % 16) / 32))[:, None]
    a["axial"] = np.stack([np.cos(angle), np.sin(angle)], 1).astype(np.float32)
    apart = np.abs(np.arange(P)[:, None] + (NT - 1) * P - np.arange(SPAN)[None, :])
    count = sum((apart % step == 0) & (apart <= window // 2) for window, step in ((128, 1), (512, 4), (2048, 16)))
    held = np.where(count > 0, np.log(np.maximum(count, 1)), NEG)
    a["biases"] = np.stack([(held - 2.0 ** -(h + 1) * apart) * DH ** 0.5 for h in range(8)]).astype(np.float32)
    return a


def kernel(**inputs):
    import concourse.bacc as bacc
    from concourse.bass_utils import run_bass_kernel_spmd

    nc = bacc.Bacc("TRN2", target_bir_lowering=False, num_devices=1)
    arrays = {f"in_{n}": np.ascontiguousarray(v) for n, v in layouts(inputs).items()}
    aps = {n[3:]: nc.dram_tensor(n, v.shape, mybir.dt.from_np(v.dtype), kind="ExternalInput").ap()
           for n, v in arrays.items()}
    out = nc.dram_tensor("out", (P, KD, S), F32, kind="ExternalOutput").ap()
    build(nc, aps, out)
    run = run_bass_kernel_spmd(nc, [arrays], core_ids=[0])
    y = run.results[0]["out"]
    return np.ascontiguousarray(np.asarray(y).transpose(1, 0, 2).reshape(D, S).T).reshape(1, S, D)
```
